# Optimizing a Trainium2 kernel written in Bass

```python
import jax, jax.numpy as jnp
from jax import lax
import numpy as np

D_MODEL = 1024
BATCH = 1
SEQ = 1024
DEPTH = 1
DEC_BATCH = 8
DEC_SEQ = 8
PAST_LEN = 1024
PAGE_SIZE = 128

HG_HEADS = 4
HG_DK = 128
HG_DV = 128
HG_KW = HG_HEADS * HG_DK
HG_WIDTH = HG_HEADS * HG_DV
HG_CHUNK = 32
FOX_HEADS = 8
FOX_DH = 64
FOX_WIDTH = FOX_HEADS * FOX_DH
Q_BLOCK = 128
D_FF = 4 * D_MODEL
N_BRANCH = 2
N_MOD = 6
RMS_EPS = 1e-6
SPLIT_SIZES = (HG_KW, HG_KW, HG_WIDTH, HG_WIDTH, FOX_WIDTH, FOX_WIDTH, FOX_WIDTH, FOX_HEADS, N_BRANCH * D_MODEL)
IN_COLS = sum(SPLIT_SIZES)
SPLIT_IDX = [int(i) for i in np.cumsum(SPLIT_SIZES)[:-1]]

kernel_name = "hybrid_hgrn2_fox_adaln_step"

def rmsnorm(x, w):
    x32 = x.astype(jnp.float32)
    r = x32 * lax.rsqrt(jnp.mean(x32 * x32, axis=-1, keepdims=True) + RMS_EPS)
    return (r * w.astype(jnp.float32)).astype(x.dtype)

def hgrn_chunked(q, k, v, logf, s0):
    B, L, H, DK = q.shape
    DV = v.shape[-1]
    C = HG_CHUNK if L % HG_CHUNK == 0 else L
    n = L // C

    def to_chunks(a):
        return jnp.moveaxis(a.astype(jnp.float32).reshape(B, n, C, H, a.shape[-1]), 1, 0)

    causal = jnp.tril(jnp.ones((C, C), dtype=bool))

    def step(S, inp):
        qc, kc, vc, gc = inp
        b = jnp.cumsum(gc, axis=1)
        qt = qc * jnp.exp(b)
        kt = kc * jnp.exp(-b)
        a = jnp.where(causal, jnp.einsum('bthk,bshk->bhts', qt, kt), 0.0)
        o = jnp.einsum('bchk,bhkv->bchv', qt, S) + jnp.einsum('bhts,bshv->bthv', a, vc)
        bl = b[:, -1:]
        S = jnp.exp(bl[:, 0])[..., None] * S + jnp.einsum('bshk,bshv->bhkv', kc * jnp.exp(bl - b), vc)
        return S, o

    S, o = lax.scan(step, s0.astype(jnp.float32), (to_chunks(q), to_chunks(k), to_chunks(v), to_chunks(logf)))
    o = jnp.moveaxis(o, 0, 1).reshape(B, L, H, DV)
    return o.astype(v.dtype), S.astype(s0.dtype)

def fox_attend(q, k, v, dq, dk, q_pos, k_pos):
    B, Lq, H, Dh = q.shape
    bq = Q_BLOCK if Lq % Q_BLOCK == 0 else Lq
    nb = Lq // bq
    scale = Dh ** -0.5
    qs = jnp.moveaxis(q.reshape(B, nb, bq, H, Dh), 1, 0)
    dqs = jnp.moveaxis(dq.reshape(B, nb, bq, H), 1, 0)
    qps = q_pos.reshape(nb, bq)
    dk_t = jnp.transpose(dk, (0, 2, 1))[:, :, None, :]

    def blk(args):
        qb, dqb, qpb = args
        s = jnp.einsum('bqhd,bkhd->bhqk', qb, k, preferred_element_type=jnp.float32) * scale
        s = s + jnp.transpose(dqb, (0, 2, 1))[..., None] - dk_t
        mask = k_pos[None, :] <= qpb[:, None]
        s = jnp.where(mask, s, -jnp.inf)
        p = jax.nn.softmax(s, axis=-1)
        return jnp.einsum('bhqk,bkhd->bqhd', p.astype(v.dtype), v)

    o = lax.map(blk, (qs, dqs, qps))
    return jnp.moveaxis(o, 0, 1).reshape(B, Lq, H, Dh)

def token_mixer(h, lw, lb, s0, past):
    B, L, _ = h.shape
    hq, hf, hi, hg, fq, fk, fv, ff, mg = jnp.split(h @ lw['w_in'], SPLIT_IDX, axis=-1)
    hf32 = hf.astype(jnp.float32)
    f = lb + (1.0 - lb) * jax.nn.sigmoid(hf32)
    g_log = jnp.log(f)
    k_in = (1.0 - lb) * jax.nn.sigmoid(-hf32)
    q_h = hq.reshape(B, L, HG_HEADS, HG_DK) * (HG_DK ** -0.5)
    o_h, s_new = hgrn_chunked(q_h, k_in.reshape(B, L, HG_HEADS, HG_DK),
                              hi.reshape(B, L, HG_HEADS, HG_DV),
                              g_log.reshape(B, L, HG_HEADS, HG_DK), s0)
    o_h = rmsnorm(o_h, lw['hg_onorm']) * jax.nn.silu(hg.reshape(B, L, HG_HEADS, HG_DV))
    br_h = o_h.reshape(B, L, HG_WIDTH) @ lw['w_br_h']
    q_f = fq.reshape(B, L, FOX_HEADS, FOX_DH)
    k_f = fk.reshape(B, L, FOX_HEADS, FOX_DH)
    v_f = fv.reshape(B, L, FOX_HEADS, FOX_DH)
    logf = jax.nn.log_sigmoid(ff.astype(jnp.float32) + lw['fox_b_f'].astype(jnp.float32))
    if past is None:
        kk, vv, lf_all = k_f, v_f, logf
    else:
        pk, pv, plf = past
        kk = jnp.concatenate([pk, k_f], axis=1)
        vv = jnp.concatenate([pv, v_f], axis=1)
        lf_all = jnp.concatenate([plf.astype(jnp.float32), logf], axis=1)
    Lk = kk.shape[1]
    D = jnp.cumsum(lf_all, axis=1)
    k_pos = jnp.arange(Lk, dtype=jnp.int32)
    q_pos = k_pos[Lk - L:]
    o_f = fox_attend(q_f, kk, vv, D[:, Lk - L:], D, q_pos, k_pos)
    br_f = o_f.reshape(B, L, FOX_WIDTH) @ lw['w_br_f']
    g_h, g_f = jnp.split(jax.nn.sigmoid(mg), N_BRANCH, axis=-1)
    y = (g_h * br_h + g_f * br_f) @ lw['w_out']
    return y, (k_f, v_f, logf.astype(h.dtype), s_new)

def layer(x, c, lw, lb, s0, past):
    mod = (jax.nn.silu(c) @ lw['ada_w'] + lw['ada_b'])[:, None, :]
    sh1, sc1, gt1, sh2, sc2, gt2 = jnp.split(mod, N_MOD, axis=-1)
    h = rmsnorm(x, lw['n1_pre']) * (1.0 + sc1) + sh1
    y, new_state = token_mixer(h, lw, lb, s0, past)
    x = x + gt1 * rmsnorm(y, lw['n1_post'])
    h = rmsnorm(x, lw['n2_pre']) * (1.0 + sc2) + sh2
    u = jnp.square(jax.nn.relu(h @ lw['w_up'])) @ lw['w_down']
    x = x + gt2 * rmsnorm(u, lw['n2_post'])
    return x, new_state

def setup_inputs(seed: int = 0) -> dict:
    key = jax.random.key(seed)
    ks = jax.random.split(key, 32)
    f32 = jnp.float32

    def nrm(k, shape, scale):
        return jax.random.normal(k, shape, f32) * scale

    n_pages = PAST_LEN // PAGE_SIZE
    n_used = DEC_BATCH * n_pages
    n_phys = n_used + max(1, n_used // 4)
    page_table = jax.random.permutation(ks[0], n_phys)[:n_used].reshape(DEC_BATCH, n_pages).astype(jnp.int32)
    return {
        'x_prompt': nrm(ks[1], (BATCH, SEQ, D_MODEL), 1.0),
        'x_sample': nrm(ks[2], (DEC_BATCH, DEC_SEQ, D_MODEL), 1.0),
        'c_prompt': nrm(ks[3], (BATCH, D_MODEL), 1.0),
        'c_sample': nrm(ks[4], (DEC_BATCH, D_MODEL), 1.0),
        'cache_k': nrm(ks[5], (DEPTH, n_phys, PAGE_SIZE, FOX_HEADS, FOX_DH), 1.0),
        'cache_v': nrm(ks[6], (DEPTH, n_phys, PAGE_SIZE, FOX_HEADS, FOX_DH), 1.0),
        'cache_logf': jax.nn.log_sigmoid(2.0 + nrm(ks[7], (DEPTH, n_phys, PAGE_SIZE, FOX_HEADS), 1.0)),
        'state_hgrn': nrm(ks[8], (DEPTH, DEC_BATCH, HG_HEADS, HG_DK, HG_DV), 0.5),
        'page_table': page_table,
        'ada_w': nrm(ks[9], (DEPTH, D_MODEL, N_MOD * D_MODEL), 0.5 * D_MODEL ** -0.5),
        'ada_b': nrm(ks[10], (DEPTH, N_MOD * D_MODEL), 0.02),
        'norm_mix_pre': 1.0 + nrm(ks[11], (DEPTH, D_MODEL), 0.02),
        'norm_mix_post': 1.0 + nrm(ks[12], (DEPTH, D_MODEL), 0.02),
        'norm_mlp_pre': 1.0 + nrm(ks[13], (DEPTH, D_MODEL), 0.02),
        'norm_mlp_post': 1.0 + nrm(ks[14], (DEPTH, D_MODEL), 0.02),
        'w_in': nrm(ks[15], (DEPTH, D_MODEL, IN_COLS), D_MODEL ** -0.5),
        'hgrn_lower_bounds': nrm(ks[16], (DEPTH + 1, HG_KW), 0.1),
        'hgrn_onorm': 1.0 + nrm(ks[17], (DEPTH, HG_DV), 0.02),
        'fox_b_f': 2.0 + nrm(ks[18], (DEPTH, FOX_HEADS), 0.1),
        'w_br_h': nrm(ks[19], (DEPTH, HG_WIDTH, D_MODEL), HG_WIDTH ** -0.5),
        'w_br_f': nrm(ks[20], (DEPTH, FOX_WIDTH, D_MODEL), FOX_WIDTH ** -0.5),
        'w_out': nrm(ks[21], (DEPTH, D_MODEL, D_MODEL), D_MODEL ** -0.5),
        'w_mlp_up': nrm(ks[22], (DEPTH, D_MODEL, D_FF), D_MODEL ** -0.5),
        'w_mlp_down': nrm(ks[23], (DEPTH, D_FF, D_MODEL), D_FF ** -0.5),
    }

def reference(x_prompt, x_sample, c_prompt, c_sample, cache_k, cache_v, cache_logf, state_hgrn, page_table,
              ada_w, ada_b, norm_mix_pre, norm_mix_post, norm_mlp_pre, norm_mlp_post, w_in,
              hgrn_lower_bounds, hgrn_onorm, fox_b_f, w_br_h, w_br_f, w_out, w_mlp_up, w_mlp_down):
    lb_all = jnp.cumsum(jax.nn.softmax(hgrn_lower_bounds.astype(jnp.float32), axis=0), axis=0)
    n_dec, n_pages = page_table.shape
    yp, ys = x_prompt, x_sample
    kp_l, vp_l, lfp_l, sp_l, ks_l, vs_l, lfs_l, ss_l = [], [], [], [], [], [], [], []
    for l in range(DEPTH):
        lw = {'ada_w': ada_w[l], 'ada_b': ada_b[l], 'n1_pre': norm_mix_pre[l], 'n1_post': norm_mix_post[l],
              'n2_pre': norm_mlp_pre[l], 'n2_post': norm_mlp_post[l], 'w_in': w_in[l],
              'hg_onorm': hgrn_onorm[l], 'fox_b_f': fox_b_f[l], 'w_br_h': w_br_h[l], 'w_br_f': w_br_f[l],
              'w_out': w_out[l], 'w_up': w_mlp_up[l], 'w_down': w_mlp_down[l]}
        lb = lb_all[l]
        s0 = jnp.zeros((x_prompt.shape[0], HG_HEADS, HG_DK, HG_DV), x_prompt.dtype)
        yp, (kp, vp, lfp, sp) = layer(yp, c_prompt, lw, lb, s0, None)
        past_k = cache_k[l][page_table].reshape(n_dec, n_pages * PAGE_SIZE, FOX_HEADS, FOX_DH)
        past_v = cache_v[l][page_table].reshape(n_dec, n_pages * PAGE_SIZE, FOX_HEADS, FOX_DH)
        past_lf = cache_logf[l][page_table].reshape(n_dec, n_pages * PAGE_SIZE, FOX_HEADS)
        ys, (kss, vss, lfs, ss) = layer(ys, c_sample, lw, lb, state_hgrn[l], (past_k, past_v, past_lf))
        kp_l.append(kp); vp_l.append(vp); lfp_l.append(lfp); sp_l.append(sp)
        ks_l.append(kss); vs_l.append(vss); lfs_l.append(lfs); ss_l.append(ss)
    k_prompt = jnp.stack(kp_l)
    v_prompt = jnp.stack(vp_l)
    logf_prompt = jnp.stack(lfp_l)
    s_prompt = jnp.stack(sp_l)
    k_sample = jnp.stack(ks_l)
    v_sample = jnp.stack(vs_l)
    logf_sample = jnp.stack(lfs_l)
    s_sample = jnp.stack(ss_l)
    return (yp, ys, k_prompt, v_prompt, logf_prompt, s_prompt, k_sample, v_sample, logf_sample, s_sample)


_drawn_inputs = setup_inputs


def setup_inputs(seed=0):
    import zlib

    import numpy as np

    out = dict(_drawn_inputs(seed))
    spreads = {}
    factors = {'norm_mix_pre': 2.936,
     'norm_mix_post': 62.491,
     'norm_mlp_pre': 80.337,
     'norm_mlp_post': 113.319,
     'hgrn_onorm': 23.368,
     'cache_v': 2.953,
     'cache_logf': 64.0,
     'cache_k': 3.017}
    for name, (base, spread) in spreads.items():
        noise = np.random.default_rng([zlib.crc32(name.encode()), seed]).standard_normal(out[name].shape)
        drawn = base * np.exp(spread * noise) if base else spread * noise
        out[name] = __import__('jax').numpy.asarray(drawn.astype(out[name].dtype))
    for name, factor in factors.items():
        out[name] = (out[name] * factor).astype(out[name].dtype)
    return out
```

```python
from contextlib import ExitStack

import concourse.bass as bass
from concourse import mybir

F32 = mybir.dt.float32
F32R = mybir.dt.float32r
BF16 = mybir.dt.bfloat16
I32 = mybir.dt.int32
ALU = mybir.AluOpType
ACT = mybir.ActivationFunctionType
AX = mybir.AxisListType.X

P = 128
NEG = -1e30
EPS = 1e-6
HG_CHUNK = 32


def build_layer(nc, x_prompt, x_sample, c_prompt, c_sample, cache_k, cache_v, cache_logf, state_hgrn, page_table,
                ada_w, ada_b, norm_mix_pre, norm_mix_post, norm_mlp_pre, norm_mlp_post, w_in, hgrn_lower_bounds,
                hgrn_onorm, fox_b_f, w_br_h, w_br_f, w_out, w_mlp_up, w_mlp_down,
                y_prompt, y_sample, k_prompt, v_prompt, logf_prompt, s_prompt, k_sample, v_sample, logf_sample,
                s_sample):
    _, L, D = x_prompt.shape
    NB, LS, _ = x_sample.shape
    TS = NB * LS
    T = L + TS
    KD = D // P
    NT = L // P
    _, NPHYS, PAGE, FH, DH = cache_k.shape
    NPG = page_table.shape[1]
    PAST = NPG * PAGE
    HH, DK, DV = state_hgrn.shape[2:]
    HW, FW = HH * DK, FH * DH
    FF = w_mlp_up.shape[2]
    NM = ada_w.shape[2] // P
    NC = 1 + NB
    G = FW // P
    CP = P // HG_CHUNK
    NCH = L // HG_CHUNK
    MB = 512
    NMB = FF // MB
    UT = MB // P
    assert (L, D, TS, PAGE, DK, DV, DH, KD, G, HH) == (1024, 1024, 64, P, P, P, 64, 8, 4, 4)
    O_HQ, O_HF, O_HI, O_HG = 0, HW, 2 * HW, 3 * HW
    O_FQ, O_FK, O_FV = 4 * HW, 4 * HW + FW, 4 * HW + 2 * FW
    O_FF = O_FV + FW
    O_MG = O_FF + FH
    V_AB, V_N1, V_P1, V_N2, V_P2 = 0, NM, NM + KD, NM + 2 * KD, NM + 3 * KD
    V_ON, V_L0 = NM + 4 * KD, NM + 4 * KD + 1
    V_L1 = V_L0 + HH
    NV = V_L1 + HH
    U_FF, U_FOX, U_HG = 0, 1, 1 + 3 * G
    U_MG = U_HG + 4 * HH
    U_OUT = U_MG + 2 * KD
    U_MLP = U_OUT + KD

    w_in_v = w_in[0].rearrange("(k p) n -> p k n", p=P)
    w_out_v = w_out[0].rearrange("(k p) n -> p k n", p=P)
    w_up_v = w_mlp_up[0].rearrange("(k p) n -> p k n", p=P)
    w_dn_v = w_mlp_down[0].rearrange("(k p) n -> p k n", p=P)
    w_bh_v = w_br_h[0].rearrange("(k p) n -> p k n", p=P)
    w_bf_v = w_br_f[0].rearrange("(k p) n -> p k n", p=P)
    ada_v = ada_w[0].rearrange("(k p) n -> p k n", p=P)
    kp_v = k_prompt[0, 0].rearrange("(t p) h d -> p t (h d)", p=P)
    vp_v = v_prompt[0, 0].rearrange("(t p) h d -> p t (h d)", p=P)
    yp_v = y_prompt[0].rearrange("(t p) n -> p t n", p=P)
    ys_v = y_sample.rearrange("b l n -> (b l) n")
    xp_v = x_prompt[0].rearrange("(t p) n -> p t n", p=P)
    xs_v = x_sample.rearrange("b l n -> (b l) n")
    ck_v = cache_k[0].rearrange("g p h d -> g p (h d)")
    cv_v = cache_v[0].rearrange("g p h d -> g p (h d)")
    cl_v = cache_logf[0]
    x1_dram = nc.dram_tensor("x1_scratch", [P, KD, T], F32, kind="Internal").ap()

    with ExitStack() as ctx:
        def sb(name, shape, dt=F32):
            return ctx.enter_context(nc.sbuf_tensor(name, shape, dt))

        def sem(name):
            return ctx.enter_context(nc.semaphore(name))

        h_hi, h_lo = sb("h_hi", [P, KD, T], F32R), sb("h_lo", [P, KD, T], F32R)
        w_raw = sb("w_raw", [P, 2, 1024])
        w_hi, w_lo = sb("w_hi", [P, 2, 1024], F32R), sb("w_lo", [P, 2, 1024], F32R)
        ident = sb("ident", [P, P])
        ident_b = sb("ident_b", [P, P], BF16)
        ones = sb("ones", [P, 1])
        causal_neg = sb("causal_neg", [P, P], BF16)
        chunk_mask = sb("chunk_mask", [P, P])
        chunk_mask_s = sb("chunk_mask_s", [TS, TS])
        batch_mask = sb("batch_mask", [TS, NB])
        new_neg_room = sb("new_neg", [TS, NB * (TS + LS)], BF16)
        new_neg = new_neg_room[:, 0:NB * TS].rearrange("p (b k) -> p b k", k=TS)
        new_neg_own = new_neg_room[:, :].rearrange("p (b k) -> p b k", k=TS + LS)[:, :, 0:LS]
        not_after = sb("not_after", [LS, FH, LS])
        neg_pick = sb("neg_pick", [P, FH, P], BF16)
        neg_pick_s = sb("neg_pick_s", [TS, NB, TS])
        reset = sb("reset", [P, T])
        d_past = reset[0:TS, 0:PAST + LS]
        vec = sb("vec", [P, NV])
        c_act = sb("c_act", [P, NC * KD])
        mod = sb("mod", [P, NM, NC])
        pre1, post1 = sb("pre1", [P, KD, NC]), sb("post1", [P, KD, NC])
        pre2, post2 = sb("pre2", [P, KD, NC]), sb("post2", [P, KD, NC])
        lb, omlb = sb("lb", [P, HH]), sb("omlb", [P, HH])
        lb_diff = sb("lb_diff", [P, HH])
        fox_b = sb("fox_b", [FH, 1])
        stat = sb("stat", [P, NT + 1])
        half = sb("half", [P, NT + 1])
        d_parts = sb("d_parts", [96, L], BF16)
        q_new, k_new = sb("q_new", [P, G, TS]), sb("k_new", [P, G, TS])
        new_tok = sb("new_tok", [2 * TS, FW])
        v_new, k_new_tok = new_tok[0:TS, :], new_tok[TS:2 * TS, :]
        nmax, sums, rinv = sb("nmax", [P, 2]), sb("sums", [P, 16]), sb("rinv", [P, 2])
        pages = sb("pages", [1, NB * NPG], I32)

        with nc.sbuf_tensor("mix", [P, G + HH, T], F32) as mix:
            pass
        u_hi, u_lo = sb("u_hi", [P, UT, T], F32R), sb("u_lo", [P, UT, T], F32R)
        WORK = 15360
        work = sb("work", [P, WORK])

        def cut(at, *shape, rows=P):
            n = 1
            for s in shape:
                n *= s
            assert at + n <= WORK
            v = work[0:rows, at:at + n]
            if len(shape) == 2:
                v = v.rearrange("p (a b) -> p a b", b=shape[1])
            if len(shape) == 3:
                v = v.rearrange("p (a b c) -> p a b c", b=shape[1], c=shape[2])
            return v

        psum = ctx.enter_context(nc.psum_tensor("psum", [P, 8 * 512], F32))

        def bank(i, a=0, b=512, rows=P):
            return psum[0:rows, 512 * i + a:512 * i + b]

        def acc(slot):
            return psum[:, 1536 * slot:1536 * slot + T]

        PIECES = [(0, 512), (512, 1024), (1024, T)]

        raw_landed = [sem("raw_landed0"), sem("raw_landed1")]
        w_hi_ready, w_lo_ready = sem("w_hi_ready"), sem("w_lo_ready")
        unit_done, acc_read = sem("unit_done"), sem("acc_read")
        done_of = {e: sem(f"phase_done_{e}") for e in ("pe", "act", "dve", "pool")}
        vecs_landed, pages_landed, past_logf_landed, x_landed, xs_landed = map(
            sem, ("vecs_landed", "pages_landed", "past_logf_landed", "x_landed", "xs_landed"))
        consts_ready, dve_consts_ready = sem("consts_ready"), sem("dve_consts_ready")
        ada_landed = [sem(f"ada_landed{i}") for i in range(3)]
        ada_used, vecs_tr, vecs_copied, c_ready, mod_ready, mod_done = map(
            sem, ("ada_used", "vecs_tr", "vecs_copied", "c_ready", "mod_ready", "mod_done"))
        x_sumsq, x_ms, x_rstd, x_scaled, h_tr, h_raw, h_split = map(
            sem, ("x_sumsq", "x_ms", "x_rstd", "x_scaled", "h_tr", "h_raw", "h_split"))
        lf_tr, lf_exp, lf_abs, lf_ln, lf_min, lf_ready, lf_out_tr, lf_out_copied, lf_new_moved, d_ready = map(
            sem, ("lf_tr", "lf_exp", "lf_abs", "lf_ln", "lf_min", "lf_ready", "lf_out_tr", "lf_out_copied",
                  "lf_new_moved", "d_ready"))
        tok_tr, tok_copied, new_stashed, kv_stored = map(sem, ("tok_tr", "tok_copied", "new_stashed", "kv_stored"))
        scores_ready, max_ready, probs_ready, probs_tr, pt_low, pt_high, pv_done, o_ready, o_tr, o_copied = map(
            sem, ("scores_ready", "max_ready", "probs_ready", "probs_tr", "pt_low", "pt_high", "pv_done", "o_ready",
                  "o_tr", "o_copied"))
        sk_landed, sv_landed, sq_ready, sk_tr, sk_copied_dve, sk_copied_act, ss_ready, smax_ready, sexp_ready = map(
            sem, ("sk_landed", "sv_landed", "sq_ready", "sk_tr", "sk_copied_dve", "sk_copied_act", "ss_ready",
                  "smax_ready", "sexp_ready"))
        sp_ready, sp_tr, spt_ready, spv_done, so_copied, s_scores_done = map(
            sem, ("sp_ready", "sp_tr", "spt_ready", "spv_done", "so_copied", "s_scores_done"))
        sig_ready, f_ready, g_ready, b_ready, eb_ready, hg_ops, hv_tr, hv_copied, hkd_tr, hkd_copied = map(
            sem, ("sig_ready", "f_ready", "g_ready", "b_ready", "eb_ready", "hg_ops", "hv_tr", "hv_copied", "hkd_tr",
                  "hkd_copied"))
        a_ready, a_masked, ds_ready, s_ready, ho_ready, ho_copied, hss_ready, hms_ready, hrstd, hn_ready = map(
            sem, ("a_ready", "a_masked", "ds_ready", "s_ready", "ho_ready", "ho_copied", "hss_ready", "hms_ready",
                  "hrstd", "hn_ready"))
        ho_tr, ho_mixed, s0_landed, state_stored, sds_ready, s_new_ready, masked_ready = map(
            sem, ("ho_tr", "ho_mixed", "s0_landed", "state_stored", "sds_ready", "s_new_ready", "masked_ready"))
        br_landed = [sem("br_landed0"), sem("br_landed1")]
        br_ready, br_read, br_added = map(sem, ("br_ready", "br_read", "br_added"))
        y_sq, ss_tr, ms_ready, rstd_ready, rb_ready, rb_copied, x1_ready, x1_stored, x1_summed, xT_ready = map(
            sem, ("y_sq", "ss_tr", "ms_ready", "rstd_ready", "rb_ready", "rb_copied", "x1_ready", "x1_stored",
                  "x1_summed", "xT_ready"))
        h2_scaled, h2_raw, h2_split, sq_zeroed, hg_zeroed, down_half, ones_set, v_spread = map(
            sem, ("h2_scaled", "h2_raw", "h2_split", "sq_zeroed", "hg_zeroed", "down_half", "ones_set", "v_spread"))
        relu_ready, u_hi_ready, u_lo_ready, down_copied, down_free = map(
            sem, ("relu_ready", "u_hi_ready", "u_lo_ready", "down_copied", "down_free"))
        x1_back, fin_ready, fin_tr, fin_copied, fin_stored, stored = map(
            sem, ("x1_back", "fin_ready", "fin_tr", "fin_copied", "fin_stored", "stored"))
        xtr_free = sem("xtr_free")

        order = ("pe", "act", "dve", "pool")
        passed = {e: sem(f"waits_passed_{e}") for e in order + ("sp",)}

        def past_waits(eng, me):
            eng.sem_inc(passed[me], 1)

        def phase_end(eng, me, k):
            eng.drain().then_inc(done_of[me], 1)
            for o in order:
                if o != me:
                    eng.wait_ge(done_of[o], k)

        def split_hi(act, n, slot, landed):
            act.wait_ge(raw_landed[slot], landed)
            if not (isinstance(n, int) and n < 2):
                act.wait_ge(unit_done, n - 1)
            nc.scalar.activation(w_hi[:, slot, :], w_raw[:, slot, :], ACT.Copy).then_inc(w_hi_ready, 1)

        def split_lo(dve, n, slot):
            dve.wait_ge(w_hi_ready, n + 1)
            nc.vector.tensor_sub(w_lo[:, slot, :], w_raw[:, slot, :], w_hi[:, slot, :].bitcast(F32))\
                .then_inc(w_lo_ready, 1)

        def number(base, per, it, j):
            return base + j + per * it, (base + j) % 2, 16 * ((base + j) // 2 + 1) + 16 * (per // 2) * it

        def project(pe, n, slot, acc_no=None, acc_slot=None, acc_free=False):
            acc_no, acc_slot = (n, slot) if acc_no is None else (acc_no, acc_slot)
            hi, lo = h_hi, h_lo
            pe.wait_ge(w_lo_ready, n + 1)
            pe.wait_ge(w_hi_ready, n + 1)
            if not (acc_free or (isinstance(n, int) and n < 2)):
                pe.wait_ge(acc_read, acc_no - 1)
            out = acc(acc_slot)
            for k in range(KD):
                wh, wl = (w[:, slot, P * k:P * k + P] for w in (w_hi, w_lo))
                for w, m in ((wh, hi), (wh, lo), (wl, hi)):
                    for a, b in PIECES:
                        last = nc.tensor.matmul(out[:, a:b], w, m[:, k, a:b], start=(k == 0 and w is wh and m is hi),
                                                stop=(k == KD - 1 and w is wl))
            last.then_inc(unit_done, 1)

        ada_ring = [cut(4096 * i, 4096) for i in range(3)]
        xs_tile = cut(12288, 1024, rows=TS)
        h_tmp = [cut(13312, 512), cut(13824, 512)]
        junk = cut(14336, 1024)
        mix_tail = mix[:, :, :].rearrange("p a b -> p (a b)")[:, NT * 1024:]
        vec_rows, c_rows = mix_tail[0:NV, 0:P], mix_tail[0:NC * KD, P:2 * P]
        xall = mix[:, :, :].rearrange("p a b -> p (a b)")[:, 0:NT * 1024].rearrange("p (t n) -> p t n", n=1024)
        past_lf = cut(0, NPG, NB, FH)
        lf_T = cut(512, T, rows=FH)
        lf_a, lf_m = cut(512 + T, T, rows=FH), cut(512 + 2 * T, T, rows=FH)
        lf_out = cut(512 + 3 * T, 128)
        lf_d = cut(640 + 3 * T, L, rows=FH)
        lf_b = cut(640 + 3 * T + L, L // 2, rows=FH).bitcast(BF16)
        fkT, fvT, fqT = cut(0, T), cut(T, T), cut(2 * T, T)
        fat = 3 * T
        f_vtok, f_ktok = cut(fat, NT, P), cut(fat + 1024, NT, P)
        probs = [cut(fat + 2048, 1024), cut(fat + 3072, 1024)]
        probsT = [cut(fat + 4096, NT, P), cut(fat + 5120, NT, P)]
        f_otok = cut(fat + 6144, NT, P)
        scan_ones = cut(640 + 3 * T + L + L // 2, L, rows=TS)
        sK, sKT, sV = cut(0, NPG, FW), cut(4096, G, PAST), cut(8192, NPG, FW)
        sP = cut(12288, PAST + TS, rows=TS)
        sPT = cut(13376, NPG + 1, TS)
        sQ_room = cut(13376 + 576, G * (TS + 2 * LS))
        sQ = sQ_room[:, 0:G * TS].rearrange("p (g c) -> p g c", c=TS)
        sQ_own = sQ_room.rearrange("p (g c) -> p g c", c=TS + 2 * LS)
        sPick = cut(13376 + 896, TS, rows=TS)
        sNeg = cut(13376 + 960, TS // 2, rows=TS).bitcast(BF16)
        hK, hF, hE, hN, hQ, hV, hS = (cut(T * i, T) for i in range(7))
        hg_at = 7 * T
        hB = cut(hg_at, T)
        v_by_chunk = hV[:, 0:2 * CP * P].rearrange("p (i c v) -> p i c v", c=CP, v=P)
        h_otok = cut(hg_at, NT + 1, P)
        h_vtok, h_kdtok = cut(hg_at + 1152, NT + 1, P), cut(hg_at + 2304, NT + 1, P)
        ring = hg_at + 3456
        states = [cut(ring + P * i, P) for i in range(8)]
        a_mask = [cut(ring + 1024, P), cut(ring + 1152, P)]
        a_mask_s = cut(ring + 1280, TS, rows=TS)
        s_states = cut(ring + 1344, NB, DV)
        kd_by_b = cut(ring + 2368, NB, DK, rows=TS)
        q_by_b_room = cut(ring + 3392, NB * (TS + LS))
        q_by_b = q_by_b_room[:, 0:NB * TS].rearrange("p (b t) -> p b t", t=TS)
        q_by_b_own = q_by_b_room.rearrange("p (b t) -> p b t", t=TS + LS)[:, :, 0:LS]
        h_ms = cut(ring + 3392 + 576, NT + 1)
        merged = cut(0, KD, T)
        br_raw = [cut(KD * T, 1024), cut(KD * T + 1024, 1024)]
        gate_h, gate_f, br_tmp = (cut(KD * T + 2048 + T * i, T) for i in range(3))
        yT = cut(0, KD, T)
        rb = cut(KD * T, T)
        sq = cut(KD * T + T, T)
        sq_sum = cut(KD * T + 2 * T, T)
        t1 = [cut(KD * T + 3 * T, T), cut(KD * T + 4 * T, T)]
        xs_again = cut(KD * T + 5 * T, 1024, rows=TS)
        relu = [cut(KD * T, T), cut(KD * T + T, T)]
        usq = cut(KD * T + 2 * T, T)
        down = [cut(KD * T + 3 * T, T), cut(KD * T + 4 * T, T)]
        x1b = [cut(KD * T + 3 * T, T), cut(KD * T + 4 * T, T)]
        out_tok = cut(KD * T + 5 * T, NT + 1, P)

        def by_batch(ap):
            return ap.rearrange("p (b l) -> p b l", l=LS)

        def per_batch(v, d):
            return v[:, d, 1:NC].unsqueeze(2).broadcast_to([P, NB, LS])

        block = ctx.enter_context(nc.Block())

        @block.sync
        def _(sp):
            def rows(at, n, src):
                sp.dma_start(vec_rows[at:at + n, :], src).then_inc(vecs_landed, 16)

            rows(V_AB, NM, ada_b[0].rearrange("(k p) -> k p", p=P))
            rows(V_N1, KD, norm_mix_pre[0].rearrange("(k p) -> k p", p=P))
            rows(V_P1, KD, norm_mix_post[0].rearrange("(k p) -> k p", p=P))
            rows(V_N2, KD, norm_mlp_pre[0].rearrange("(k p) -> k p", p=P))
            rows(V_P2, KD, norm_mlp_post[0].rearrange("(k p) -> k p", p=P))
            rows(V_ON, 1, hgrn_onorm)
            rows(V_L0, 2 * HH, hgrn_lower_bounds[0:2].rearrange("r (h p) -> (r h) p", p=P))
            sp.dma_start(c_rows[0:KD, :], c_prompt[0].rearrange("(k p) -> k p", p=P)).then_inc(vecs_landed, 16)
            sp.dma_start(c_rows[KD:NC * KD, :], c_sample.rearrange("b (k p) -> (b k) p", p=P))\
                .then_inc(vecs_landed, 16)
            sp.dma_start(fox_b[:, :], fox_b_f.rearrange("a h -> h a")).then_inc(vecs_landed, 16)
            for i in range(3):
                sp.dma_start(ada_ring[i].rearrange("p (k n) -> p k n", n=512), ada_v[:, :, 512 * i:512 * i + 512])\
                    .then_inc(ada_landed[i], 16)
            with sp.Fori(0, NM // 12 - 1) as it:
                for i in range(3):
                    sp.wait_ge(ada_used, 3 * it + i + 1)
                    sp.dma_start(ada_ring[i].rearrange("p (k n) -> p k n", n=512),
                                 ada_v[:, :, bass.ds((3 * it + (3 + i)) * 512, 512)]).then_inc(ada_landed[i], 16)

            def load(n, slot, src, width=P):
                if not (isinstance(n, int) and n < 2):
                    sp.wait_ge(w_lo_ready, n - 1)
                    if not isinstance(n, int):
                        past_waits(sp, "sp")
                sp.dma_start(w_raw[:, slot, :].rearrange("p (k n) -> p k n", n=width), src)\
                    .then_inc(raw_landed[slot], 16)

            load(U_FF, 0, w_in_v[:, :, O_FF:O_FF + P])
            for g in range(G):
                for j, off in enumerate((O_FK, O_FV, O_FQ)):
                    n, slot, _ = number(U_FOX, 0, 0, 3 * g + j)
                    load(n, slot, w_in_v[:, :, off + P * g:off + P * g + P])
            with sp.Fori(0, HH) as it:
                for j, off in enumerate((O_HF, O_HQ, O_HI, O_HG)):
                    n, slot, _ = number(U_HG, 4, it, j)
                    load(n, slot, w_in_v[:, :, bass.ds(it * P + off, P)])
            with sp.Fori(0, KD // 2) as it:
                for dd in range(2):
                    for j in range(2):
                        n, slot, _ = number(U_MG, 4, it, 2 * dd + j)
                        load(n, slot, w_in_v[:, :, bass.ds((2 * it + dd) * P + (O_MG + j * D), P)])
            with sp.Fori(0, KD // 2) as it:
                for j in range(2):
                    n, slot, _ = number(U_OUT, 2, it, j)
                    load(n, slot, w_out_v[:, :, bass.ds((2 * it + j) * P, P)])
            with sp.Fori(0, NMB) as it:
                for j in range(UT):
                    n, slot, _ = number(U_MLP, 2 * UT, it, j)
                    load(n, slot, w_up_v[:, :, bass.ds(it * MB + j * P, P)])
                for j in range(UT):
                    n, slot, _ = number(U_MLP, 2 * UT, it, UT + j)
                    load(n, slot, w_dn_v[:, bass.ds(it * UT, UT), 2 * P * j:2 * P * j + 2 * P], width=2 * P)

        @block.gpsimd
        def _(pool):
            pool.memset(ident[:, :], 0.0)
            pool.memset(causal_neg[:, :], 0.0)
            pool.memset(ones[:, :], 1.0)
            pool.memset(chunk_mask[:, :], 1.0)
            pool.memset(chunk_mask_s[:, :], 1.0)
            pool.memset(batch_mask[:, :], 1.0)
            pool.memset(new_neg_room[:, :], NEG)
            pool.memset(not_after[:, :, :], 1.0)
            pool.memset(neg_pick[:, :, :], 0.0)
            pool.memset(neg_pick_s[:, :, :], 0.0)
            pool.memset(half[:, :], -0.5)
            pool.memset(d_parts[:, :], 0.0)
            pool.drain()
            pool.affine_select(out=ident[:, :], in_=ident[:, :], compare_op=ALU.not_equal, fill=1.0, base=0,
                               pattern=[[-1, P]], channel_multiplier=1)
            pool.affine_select(out=causal_neg[:, :], in_=causal_neg[:, :], compare_op=ALU.is_ge, fill=NEG, base=0,
                               pattern=[[-1, P]], channel_multiplier=1)

            def keep(ap, base, pattern, mul, fill):
                pool.affine_select(out=ap, in_=ap, compare_op=ALU.is_ge, fill=fill, base=base, pattern=pattern,
                                   channel_multiplier=mul)

            def chunks_only(ap, n, c):
                v = ap.rearrange("p (a b) -> p a b", b=c)
                keep(ap, 0, [[1, n]], -1, 0.0)
                pool.drain()
                keep(v, 0, [[-c, n // c], [0, c]], 1, 0.0)
                pool.drain()

            chunks_only(chunk_mask[:, :], P, HG_CHUNK)
            chunks_only(chunk_mask_s[:, :], TS, LS)
            keep(batch_mask[:, :], 0, [[-LS, NB]], 1, 0.0)
            pool.drain()
            keep(batch_mask[:, :], LS - 1, [[LS, NB]], -1, 0.0)
            for part in range(3):
                pool.affine_select(out=neg_pick[:, :, :], in_=neg_pick[:, :, :], compare_op=ALU.not_equal, fill=-1.0,
                                   base=-32 * part, pattern=[[-1, FH], [0, P]], channel_multiplier=1)
                pool.drain()
            pool.affine_select(out=neg_pick_s[:, :, :].rearrange("p b (h q) -> p (b h) q", q=LS),
                               in_=neg_pick_s[:, :, :].rearrange("p b (h q) -> p (b h) q", q=LS),
                               compare_op=ALU.not_equal, fill=-1.0, base=0, pattern=[[-1, NB * FH], [0, LS]],
                               channel_multiplier=1)
            keep(not_after[:, :, :], 0, [[0, FH], [1, LS]], -1, 0.0)
            pool.tensor_copy(ident_b[:, :], ident[:, :])
            pool.drain().then_inc(consts_ready, 1)

            pool.dma_start(pages[:, :], page_table.rearrange("(a b) g -> a (b g)", a=1)).then_inc(pages_landed, 16)
            for t in range(NT):
                pool.dma_start(xall[:, t, :], xp_v[:, t, :]).then_inc(x_landed, 16)
            pool.dma_start(xs_tile, xs_v).then_inc(xs_landed, 16)
            pool.wait_ge(x_ms, 1)
            nc.gpsimd.tensor_tensor(stat[:, :], stat[:, :], half[:, :], ALU.pow).then_inc(x_rstd, 1)
            phase_end(pool, "pool", 1)
            phase_end(pool, "pool", 2)

            pool.memset(scan_ones, 1.0).then_inc(ones_set, 1)
            pool.wait_ge(pages_landed, 16)
            with pool.Fori(0, NB) as b:
                for g in range(NPG):
                    page = pool.value_load(pages[0:1, bass.ds(b * NPG + g, 1)], min_val=0, max_val=NPHYS - 1)
                    pool.dma_start(past_lf[:, g, bass.ds(b, 1), :].rearrange("p a h -> p (a h)"), cl_v[bass.ds(page, 1), :, :].rearrange("a p h -> p (a h)"))\
                        .then_inc(past_logf_landed, 16)
            pool.wait_ge(lf_ready, 1)
            for b in range(NB):
                pool.dma_start(d_past[FH * b:FH * b + FH, PAST:PAST + LS], lf_T[:, L + LS * b:L + LS * b + LS])\
                    .then_inc(lf_new_moved, 16)
            pool.wait_ge(lf_out_copied, 1)
            pool.dma_start(logf_prompt[0, 0].rearrange("(t p) h -> p t h", p=P),
                           lf_out[:, 0:NT * FH].rearrange("p (t h) -> p t h", h=FH)).then_inc(stored, 16)
            pool.dma_start(logf_sample[0].rearrange("b l h -> (b l) h"), lf_out[0:TS, NT * FH:NT * FH + FH])\
                .then_inc(stored, 16)
            pool.wait_ge(stored, 32)
            phase_end(pool, "pool", 3)

            with pool.Fori(0, G // 2) as it:
                for gg in range(2):
                    g = 2 * it + gg
                    pool.wait_ge(acc_read, 6 * it + (U_FOX + 3 * gg + 3))
                    pool.tensor_copy(q_new[:, bass.ds(g, 1), :].rearrange("p a b -> p (a b)"), fqT[:, L:T])
                    pool.tensor_copy(k_new[:, bass.ds(g, 1), :].rearrange("p a b -> p (a b)"), fkT[:, L:T])
                    pool.drain().then_inc(new_stashed, 1)
                    pool.wait_ge(tok_copied, 6 * g + 6)
                    pool.dma_start(kp_v[:, :, bass.ds(g * P, P)], f_ktok).then_inc(kv_stored, 16)
                    pool.dma_start(vp_v[:, :, bass.ds(g * P, P)], f_vtok).then_inc(kv_stored, 16)
            pool.dma_start(k_sample[0].rearrange("b l h d -> (b l) (h d)"), k_new_tok[:, :]).then_inc(stored, 16)
            pool.dma_start(v_sample[0].rearrange("b l h d -> (b l) (h d)"), v_new[:, :]).then_inc(stored, 16)
            pool.wait_ge(kv_stored, 32 * G)
            phase_end(pool, "pool", 4)

            pool.memset(sQ_room, 0.0).then_inc(sq_zeroed, 1)

            def load_pages(b, dst, src, landed):
                if not isinstance(b, int):
                    past_waits(pool, "pool")
                for g in range(NPG):
                    page = pool.value_load(pages[0:1, bass.ds(b * NPG + g, 1)], min_val=0, max_val=NPHYS - 1)
                    pool.dma_start(dst[:, g, :], src[bass.ds(page, 1), :, :].rearrange("a p n -> p (a n)"))\
                        .then_inc(landed, 16)

            load_pages(0, sK, ck_v, sk_landed)
            load_pages(0, sV, cv_v, sv_landed)
            with pool.Fori(1, NB) as b:
                pool.wait_ge(sk_tr, 8 * b)
                load_pages(b, sK, ck_v, sk_landed)
                pool.wait_ge(spv_done, b)
                load_pages(b, sV, cv_v, sv_landed)
            phase_end(pool, "pool", 5)

            pool.memset(q_by_b_room, 0.0)
            pool.memset(reset[:, :], 1.0)
            pool.drain()
            pool.memset(reset[:, 0:L:HG_CHUNK], 0.0)
            pool.memset(reset[:, L:T:LS], 0.0)
            pool.memset(h_ms, 1.0)
            pool.memset(a_mask[0], 0.0)
            pool.memset(a_mask[1], 0.0)
            pool.memset(a_mask_s, 0.0)
            pool.drain().then_inc(hg_zeroed, 1)
            with pool.Fori(0, HH) as h:
                pool.dma_start(s_states, state_hgrn[0, :, bass.ds(h, 1), :, :].rearrange("b a k v -> k b (a v)"))\
                    .then_inc(s0_landed, 16)
                pool.wait_ge(hv_tr, h + 1)
                past_waits(pool, "pool")
                pool.memset(hV[:, 0:2 * CP * P], 0.0)
                pool.drain()
                pool.wait_ge(hv_copied, h + 1)
                for t in range(NT):
                    if t >= 2:
                        pool.wait_ge(ds_ready, NT * h + t - 1)
                    past_waits(pool, "pool")
                    for i in range(CP):
                        last = nc.gpsimd.tensor_copy(v_by_chunk[32 * i:32 * i + 32, t % 2, i, :],
                                                     h_vtok[32 * i:32 * i + 32, t, :])
                    pool.drain().then_inc(v_spread, 1)
                pool.wait_ge(hms_ready, h + 1)
                nc.gpsimd.tensor_tensor(h_ms, h_ms, half[:, :], ALU.pow).then_inc(hrstd, 1)
                pool.wait_ge(s_ready, NCH * h + NCH)
                past_waits(pool, "pool")
                pool.dma_start(s_prompt[0, 0, bass.ds(h, 1), :, :].rearrange("a k v -> k (a v)"), states[NCH % 8])\
                    .then_inc(state_stored, 16)
                pool.wait_ge(s_new_ready, h + 1)
                past_waits(pool, "pool")
                pool.dma_start(s_sample[0, :, bass.ds(h, 1), :, :].rearrange("b a k v -> k b (a v)"), s_states)\
                    .then_inc(state_stored, 16)
                pool.wait_ge(state_stored, 32 * h + 32)
            phase_end(pool, "pool", 6)

            def load_br(d, slot):
                v = br_raw[slot].rearrange("p (k n) -> p k n", n=P)
                pool.dma_start(v[:, 0:HH, :], w_bh_v[:, :, bass.ds(d * P, P)]).then_inc(br_landed[slot], 16)
                pool.dma_start(v[:, HH:HH + G, :], w_bf_v[:, :, bass.ds(d * P, P)]).then_inc(br_landed[slot], 16)

            load_br(0, 0)
            load_br(1, 1)
            with pool.Fori(0, KD // 2 - 1) as it:
                for dd in range(2):
                    pool.wait_ge(br_ready, 12 * it + (6 * dd + 6))
                    load_br(2 * it + (2 + dd), dd)
            phase_end(pool, "pool", 7)

            for t in range(NT):
                pool.dma_start(xall[:, t, :], xp_v[:, t, :]).then_inc(x_landed, 16)
            pool.dma_start(xs_again, xs_v).then_inc(xs_landed, 16)

            def rstd(k):
                pool.wait_ge(ms_ready, k)
                nc.gpsimd.tensor_tensor(stat[:, :], stat[:, :], half[:, :], ALU.pow).then_inc(rstd_ready, 1)

            rstd(1)
            for d in range(KD):
                pool.wait_ge(x1_ready, d + 1)
                pool.dma_start(x1_dram[:, d, :], yT[:, d, :]).then_inc(x1_stored, 16)
            rstd(2)
            pool.wait_ge(x1_stored, 16 * KD)
            phase_end(pool, "pool", 8)

            pool.memset(yT, 0.0)
            for i in range(2):
                pool.memset(down[i], 0.0).then_inc(down_free, 1)
            pool.drain()
            with pool.Fori(0, NMB) as it:
                for j in range(KD):
                    pool.wait_ge(down_copied, KD * it + j + 1)
                    nc.gpsimd.tensor_add(yT[:, j, :], yT[:, j, :], down[j % 2]).then_inc(down_free, 1)
            pool.drain()
            phase_end(pool, "pool", 9)

            def store_out(d):
                pool.wait_ge(fin_copied, d + 1)
                pool.dma_start(yp_v[:, :, P * d:P * d + P], out_tok[:, 0:NT, :]).then_inc(fin_stored, 16)
                pool.dma_start(ys_v[:, P * d:P * d + P], out_tok[0:TS, NT, :]).then_inc(fin_stored, 16)

            rstd(3)
            for d in range(KD):
                if d >= 2:
                    pool.wait_ge(fin_ready, d - 1)
                pool.dma_start(x1b[d % 2], x1_dram[:, d, :]).then_inc(x1_back, 16)
                pool.wait_ge(x1_back, 16 * d + 16)
                if d >= 1:
                    store_out(d - 1)
            store_out(KD - 1)
            pool.wait_ge(fin_stored, 32 * KD)
            pool.wait_ge(stored, 64)

        @block.scalar
        def _(act):
            copy, ACTIVATE = nc.scalar.copy, nc.scalar.activation

            def hi(base, per, it, j):
                n, slot, landed = number(base, per, it, j)
                split_hi(act, n, slot, landed)

            act.wait_ge(vecs_tr, 1)
            ACTIVATE(vec[:, :], bank(6, 0, NV), ACT.Copy).then_inc(vecs_copied, 1)
            ACTIVATE(c_act[:, :], bank(7, 0, NC * KD), ACT.Silu).then_inc(c_ready, 1)
            act.wait_ge(x_landed, 16 * NT)
            act.wait_ge(xs_landed, 16)
            act.wait_ge(dve_consts_ready, 1)
            for t in range(NT):
                ACTIVATE(junk, xall[:, t, :], ACT.Square, accum_out=stat[:, t:t + 1])
                act.drain()
            ACTIVATE(junk[0:TS, :], xs_tile, ACT.Square, accum_out=stat[0:TS, NT:NT + 1])
            act.drain().then_inc(x_sumsq, 1)
            act.wait_ge(mod_done, 1)
            ACTIVATE(lb[:, :], lb_diff[:, :], ACT.Sigmoid)
            ACTIVATE(omlb[:, :], lb_diff[:, :], ACT.Sigmoid, scale=-1.0)
            phase_end(act, "act", 1)

            split_hi(act, 0, 0, 16)
            split_hi(act, 1, 1, 16)
            for i in range(2 * KD):
                d, half_no = i // 2, i % 2
                act.wait_ge(h_tr, i + 1)
                if i >= 2:
                    act.wait_ge(h_split, i - 1)
                ACTIVATE(h_tmp[i % 2], bank(i % 2), ACT.Identity, scale=pre1[:, d, 0:1], bias=mod[:, d, 0:1])
                act.drain()
                ACTIVATE(h_hi[:, d, 512 * half_no:512 * half_no + 512], h_tmp[i % 2], ACT.Copy).then_inc(h_raw, 1)
            phase_end(act, "act", 2)

            act.wait_ge(unit_done, 1)
            ACTIVATE(lf_T, acc(0)[0:FH, :], ACT.Identity, bias=fox_b[:, 0:1]).then_inc(acc_read, 1)
            act.drain()
            ACTIVATE(lf_a, lf_T, ACT.Abs)
            act.drain()
            ACTIVATE(lf_a, lf_a, ACT.Exp, scale=-1.0)
            act.drain()
            ACTIVATE(lf_a, lf_a, ACT.Ln, bias=1.0)
            act.drain().then_inc(lf_ln, 1)
            act.wait_ge(lf_out_tr, 1)
            ACTIVATE(lf_out[:, 0:NT * FH], bank(6, 0, NT * FH), ACT.Copy)
            ACTIVATE(lf_out[0:TS, NT * FH:NT * FH + FH], bank(6, NT * FH, NT * FH + FH, rows=TS), ACT.Copy)
            act.drain().then_inc(lf_out_copied, 1)
            phase_end(act, "act", 3)

            with act.Fori(0, G // 2) as it:
                for gg in range(2):
                    g = 2 * it + gg
                    for j, (dst, scale) in enumerate(((fkT, 1.0), (fvT, 1.0), (fqT, float(DH) ** -0.5))):
                        hi(U_FOX, 6, it, 3 * gg + j + 1)
                        n, slot, _ = number(U_FOX, 6, it, 3 * gg + j)
                        act.wait_ge(unit_done, n + 1)
                        ACTIVATE(dst, acc(slot), ACT.Copy, scale=scale).then_inc(acc_read, 1)
                    for a in range(17):
                        if a < 16:
                            n = P * (a % NT + 1)
                            act.wait_ge(max_ready, 16 * g + a + 1)
                            if a >= 2:
                                act.wait_ge(probs_tr, 16 * g + a - 1)
                            ACTIVATE(probs[a % 2][:, 0:n], bank(3 * (a % 2), 0, n), ACT.Exp,
                                     bias=nmax[:, a % 2:a % 2 + 1], accum_out=sums[:, a:a + 1])
                            act.drain().then_inc(probs_ready, 1)
                        e = a - 1
                        if e >= 0 and e % NT >= 4:
                            act.wait_ge(probs_tr, 16 * g + e + 1)
                            if e >= 2:
                                act.wait_ge(pv_done, 16 * g + e - 1)
                            ACTIVATE(probsT[e % 2][:, 4:e % NT + 1, :].rearrange("p a b -> p (a b)"),
                                     bank(5, 0, P * (e % NT - 3)), ACT.Copy).then_inc(pt_high, 1)
                    for i in range(2):
                        act.wait_ge(o_tr, 2 * g + i + 1)
                        ACTIVATE(mix[:, bass.ds(g, 1), 512 * i:512 * i + 512].rearrange("p a b -> p (a b)"),
                                 bank((2, 5)[i]), ACT.Copy).then_inc(o_copied, 1)
                    act.wait_ge(new_stashed, g + 1)
            phase_end(act, "act", 4)

            with act.Fori(0, NB) as b:
                for i in range(4):
                    act.wait_ge(sk_tr, 8 * b + 2 * i + 2)
                    ACTIVATE(sKT[:, i, 512:1024], bank(5), ACT.Copy).then_inc(sk_copied_act, 1)
                act.wait_ge(smax_ready, b + 1)
                ACTIVATE(sP, psum[0:TS, 0:PAST + TS], ACT.Exp, bias=nmax[0:TS, 0:1], accum_out=sums[0:TS, 0:1])
                act.drain().then_inc(sexp_ready, 1)
            phase_end(act, "act", 5)

            with act.Fori(0, HH) as h:
                hi(U_HG, 4, h, 1)
                act.wait_ge(unit_done, 4 * h + (U_HG + 1))
                a0 = acc(U_HG % 2)
                ACTIVATE(hK, a0, ACT.Sigmoid, scale=-1.0)
                ACTIVATE(hF, a0, ACT.Sigmoid)
                act.drain().then_inc(acc_read, 1)
                hi(U_HG, 4, h, 2)
                act.wait_ge(unit_done, 4 * h + (U_HG + 2))
                ACTIVATE(hQ, acc((U_HG + 1) % 2), ACT.Copy, scale=float(DK) ** -0.5).then_inc(acc_read, 1)
                act.wait_ge(f_ready, h + 1)
                ACTIVATE(hF, hF, ACT.Ln).then_inc(g_ready, 1)
                hi(U_HG, 4, h, 3)
                act.wait_ge(unit_done, 4 * h + (U_HG + 3))
                ACTIVATE(hV, acc(U_HG % 2), ACT.Copy).then_inc(acc_read, 1)
                act.wait_ge(b_ready, h + 1)
                ACTIVATE(hE, hB, ACT.Exp)
                ACTIVATE(hN, hB, ACT.Exp, scale=-1.0)
                act.drain().then_inc(eb_ready, 1)
                hi(U_HG, 4, h, 4)
                act.wait_ge(unit_done, 4 * h + (U_HG + 4))
                ACTIVATE(hS, acc((U_HG + 1) % 2), ACT.Silu).then_inc(acc_read, 1)
                for t in range(NT + 1):
                    r = P if t < NT else TS
                    act.wait_ge(ho_ready, (NT + 1) * h + t + 1)
                    ACTIVATE(h_otok[0:r, t, :], bank(4 + t % 2, 0, P, rows=r), ACT.Copy).then_inc(ho_copied, 1)
                    act.drain()
                    ACTIVATE(hF[0:r, P * (t % 2):P * (t % 2) + P], h_otok[0:r, t, :],
                             ACT.Square, accum_out=h_ms[0:r, t:t + 1])
                act.drain().then_inc(hss_ready, 1)
            phase_end(act, "act", 6)

            with act.Fori(0, KD // 2) as it:
                for dd in range(2):
                    for j, dst in enumerate((gate_h, gate_f)):
                        hi(U_MG, 4, it, 2 * dd + j + 1)
                        n, slot, _ = number(U_MG, 4, it, 2 * dd + j)
                        act.wait_ge(unit_done, n + 1)
                        ACTIVATE(dst, acc(slot), ACT.Sigmoid).then_inc(acc_read, 1)
                    act.wait_ge(br_added, 2 * it + dd + 1)
            for d in range(KD):
                ACTIVATE(h_hi[:, d, :], merged[:, d, :], ACT.Copy).then_inc(h_raw, 1)
            phase_end(act, "act", 7)

            with act.Fori(0, KD // 2) as it:
                for j in range(2):
                    hi(U_OUT, 2, it, j + 1)
                    n, slot, _ = number(U_OUT, 2, it, j)
                    act.wait_ge(unit_done, n + 1)
                    ACTIVATE(yT[:, bass.ds(2 * it + j, 1), :].rearrange("p a b -> p (a b)"), acc(slot), ACT.Copy)\
                        .then_inc(acc_read, 1)

            def norm_rows(k):
                act.wait_ge(rb_ready, k)
                ACTIVATE(rb, psum[:, 0:T], ACT.Copy).then_inc(rb_copied, 1)

            norm_rows(1)
            norm_rows(2)
            for d in range(KD):
                act.wait_ge(h2_scaled, d + 1)
                ACTIVATE(t1[d % 2][:, 0:L], t1[d % 2][:, 0:L], ACT.Identity, bias=mod[:, 3 * KD + d, 0:1])
                act.drain()
                ACTIVATE(h_hi[:, d, :], t1[d % 2], ACT.Copy).then_inc(h2_raw, 1)
            phase_end(act, "act", 8)

            def mlp_block(it, last=False):
                for j in range(UT):
                    hi(U_MLP, 2 * UT, it, j + 1)
                    n, slot, _ = number(U_MLP, 2 * UT, it, j)
                    act.wait_ge(unit_done, n + 1)
                    ACTIVATE(relu[j % 2], acc((U_MLP + j) % 2), ACT.Relu).then_inc(acc_read, 1)
                    act.drain().then_inc(relu_ready, 1)
                    ACTIVATE(u_hi[:, j, :], relu[j % 2], ACT.Square).then_inc(u_hi_ready, 1)
                for j in range(UT):
                    if not (last and j == UT - 1):
                        hi(U_MLP, 2 * UT, it, UT + j + 1)
                    n, slot, _ = number(U_MLP, 2 * UT, it, UT + j)
                    for i in range(2):
                        act.wait_ge(*((down_half, UT * it + j + 1), (unit_done, n + 1))[i])
                        act.wait_ge(down_free, KD * it + (2 * j + i + 1))
                        ACTIVATE(down[i], acc((U_MLP + i) % 2), ACT.Copy).then_inc(acc_read, 1)
                        act.drain().then_inc(down_copied, 1)

            with act.Fori(0, NMB - 1) as it:
                mlp_block(it)
            mlp_block(NMB - 1, last=True)
            phase_end(act, "act", 9)
            norm_rows(3)
            for d in range(KD):
                act.wait_ge(fin_tr, d + 1)
                if d >= 1:
                    act.wait_ge(fin_stored, 32 * d)
                ACTIVATE(out_tok[:, 0:NT, :].rearrange("p a b -> p (a b)"), psum[:, 2048 * (d % 2):2048 * (d % 2) + L],
                         ACT.Copy)
                ACTIVATE(out_tok[0:TS, NT, :], psum[0:TS, 2048 * (d % 2) + L:2048 * (d % 2) + L + P], ACT.Copy)
                act.drain().then_inc(fin_copied, 1)

        @block.vector
        def _(dve):
            v = nc.vector

            def lo(base, per, it, j):
                n, slot, _ = number(base, per, it, j)
                split_lo(dve, n, slot)

            v.memset(stat[:, :], 1.0)
            dve.drain().then_inc(dve_consts_ready, 1)
            dve.wait_ge(consts_ready, 1)
            dve.wait_ge(vecs_copied, 1)
            v.tensor_sub(lb_diff[:, :], vec[:, V_L0:V_L0 + HH], vec[:, V_L1:V_L1 + HH])
            dve.wait_ge(vecs_tr, 2)
            v.tensor_scalar(new_neg_own, bank(4, 0, LS, rows=TS).unsqueeze(1).broadcast_to([TS, NB, LS]), -NEG, NEG,
                            ALU.mult, ALU.add)
            dve.wait_ge(x_sumsq, 1)
            v.tensor_scalar(stat[:, :], stat[:, :], 1.0 / D, EPS, ALU.mult, ALU.add).then_inc(x_ms, 1)
            dve.wait_ge(x_rstd, 1)
            for t in range(NT):
                v.tensor_scalar(xall[:, t, :], xall[:, t, :], stat[:, t:t + 1], None, ALU.mult)
            v.tensor_scalar(xs_tile, xs_tile, stat[0:TS, NT:NT + 1], None, ALU.mult)
            dve.wait_ge(mod_ready, 1)
            v.tensor_tensor(mod[:, :, :], bank(5, 0, NM * NC).rearrange("p (m c) -> p m c", c=NC),
                            vec[:, V_AB:V_AB + NM].unsqueeze(2).broadcast_to([P, NM, NC]), ALU.add)
            dve.drain()

            def times_norm(dst, row, weight, plus_one):
                w = vec[:, weight:weight + KD].unsqueeze(2).broadcast_to([P, KD, NC])
                v.scalar_tensor_tensor(dst[:, :, :], mod[:, row * KD:row * KD + KD, :], 1.0 if plus_one else 0.0, w,
                                       ALU.add, ALU.mult)

            times_norm(pre1, 1, V_N1, True)
            times_norm(post1, 2, V_P1, False)
            times_norm(pre2, 4, V_N2, True)
            times_norm(post2, 5, V_P2, False)
            dve.drain().then_inc(mod_done, 1)
            phase_end(dve, "dve", 1)

            split_lo(dve, 0, 0)
            split_lo(dve, 1, 1)
            for i in range(2 * KD):
                d, c = i // 2, 512 * (i % 2)
                dve.wait_ge(h_raw, i + 1)
                v.tensor_sub(h_lo[:, d, c:c + 512], h_tmp[i % 2], h_hi[:, d, c:c + 512].bitcast(F32))\
                    .then_inc(h_split, 1)
            hs_tmp = junk[:, 0:KD * TS].rearrange("p (d b l) -> p d b l", b=NB, l=LS)
            dve.wait_ge(h_tr, 2 * KD + 1)
            v.tensor_tensor(hs_tmp, bank(2).rearrange("p (d b l) -> p d b l", b=NB, l=LS),
                            pre1[:, :, 1:NC].unsqueeze(3).broadcast_to([P, KD, NB, LS]), ALU.mult)
            dve.drain()
            v.tensor_tensor(hs_tmp, hs_tmp, mod[:, 0:KD, 1:NC].unsqueeze(3).broadcast_to([P, KD, NB, LS]), ALU.add)
            dve.drain()
            flat = junk[:, 0:KD * TS].rearrange("p (d t) -> p d t", t=TS)
            v.tensor_copy(h_hi[:, :, L:T], flat)
            dve.drain()
            v.tensor_sub(h_lo[:, :, L:T], flat, h_hi[:, :, L:T].bitcast(F32))
            phase_end(dve, "dve", 2)

            dve.wait_ge(lf_ln, 1)
            dve.wait_ge(ones_set, 1)
            v.tensor_scalar(lf_m, lf_T, 0.0, None, ALU.min)
            dve.drain()
            v.tensor_sub(lf_T, lf_m, lf_a)
            dve.drain().then_inc(lf_ready, 1)
            v.tensor_tensor_scan(lf_d, scan_ones[0:FH, :], lf_T[:, 0:L], 0.0, ALU.mult, ALU.add)
            dve.drain()
            for part in range(3):
                v.tensor_copy(lf_b, lf_d)
                dve.drain()
                v.tensor_sub(lf_d, lf_d, lf_b)
                v.tensor_copy(d_parts[32 * part:32 * part + FH, :], lf_b)
                dve.drain()
            dve.wait_ge(lf_tr, 1)
            v.tensor_tensor_scan(d_past[:, 0:PAST], scan_ones, psum[0:TS, 1536:1536 + PAST], 0.0, ALU.mult,
                                 ALU.add)
            dve.drain()
            dve.wait_ge(lf_new_moved, 16 * NB)
            v.tensor_tensor_scan(d_past[:, PAST:PAST + LS], scan_ones[:, 0:LS], d_past[:, PAST:PAST + LS],
                                 d_past[:, PAST - 1:PAST], ALU.mult, ALU.add)
            phase_end(dve, "dve", 3)

            with dve.Fori(0, G // 2) as it:
                for gg in range(2):
                    g = 2 * it + gg
                    for j in range(3):
                        lo(U_FOX, 6, it, 3 * gg + j + 1)
                    for i, (src, dst) in enumerate((
                            (bank(2), f_vtok[:, 0:4, :].rearrange("p a b -> p (a b)")),
                            (bank(5), f_vtok[:, 4:8, :].rearrange("p a b -> p (a b)")),
                            (bank(6, 0, P, rows=TS), v_new[:, bass.ds(g * P, P)]),
                            (bank(7), f_ktok[:, 0:4, :].rearrange("p a b -> p (a b)")),
                            (bank(6, P, 2 * P, rows=TS), k_new_tok[:, bass.ds(g * P, P)]),
                            (bank(2), f_ktok[:, 4:8, :].rearrange("p a b -> p (a b)")))):
                        dve.wait_ge(tok_tr, 6 * g + i + 1)
                        v.tensor_copy(dst, src).then_inc(tok_copied, 1)
                    for a in range(18):
                        if a < 16:
                            n = P * (a % NT + 1)
                            dve.wait_ge(scores_ready, 16 * g + a + 1)
                            v.tensor_reduce(nmax[:, a % 2:a % 2 + 1], bank(3 * (a % 2), 0, n), axis=AX, op=ALU.max,
                                            negate=True).then_inc(max_ready, 1)
                        e = a - 1
                        if 0 <= e < 16:
                            dve.wait_ge(probs_tr, 16 * g + e + 1)
                            if e >= 2:
                                dve.wait_ge(pv_done, 16 * g + e - 1)
                            m = min(e % NT + 1, 4)
                            v.tensor_copy(probsT[e % 2][:, 0:m, :].rearrange("p a b -> p (a b)"),
                                          bank(2, 0, P * m)).then_inc(pt_low, 1)
                        o = a - 2
                        if o >= 0:
                            dve.wait_ge(pv_done, 16 * g + o + 1)
                            v.reciprocal(rinv[:, o % 2:o % 2 + 1], sums[:, o:o + 1])
                            dve.drain()
                            c = DH * (o // NT)
                            v.tensor_scalar(f_otok[:, o % NT, c:c + DH], bank(6 + o % 2, 0, DH),
                                            rinv[:, o % 2:o % 2 + 1], None, ALU.mult).then_inc(o_ready, 1)
                    dve.wait_ge(kv_stored, 32 * g + 32)
            phase_end(dve, "dve", 4)

            dve.wait_ge(sq_zeroed, 1)
            with dve.Fori(0, NB) as b:
                for i in range(2):
                    v.tensor_copy(sQ_own[64 * i:64 * i + 64, :, LS * i:LS * i + LS],
                                  q_new[64 * i:64 * i + 64, :, bass.ds(b * LS, LS)])
                v.tensor_copy(sPick, neg_pick_s[:, bass.ds(b, 1), :].rearrange("p a c -> p (a c)"))
                v.tensor_copy(sNeg, new_neg[:, bass.ds(b, 1), :].rearrange("p a k -> p (a k)"))
                dve.drain().then_inc(sq_ready, 1)
                for i in range(4):
                    dve.wait_ge(sk_tr, 8 * b + 2 * i + 1)
                    v.tensor_copy(sKT[:, i, 0:512], bank(4)).then_inc(sk_copied_dve, 1)
                dve.wait_ge(ss_ready, b + 1)
                v.tensor_reduce(nmax[0:TS, 0:1], psum[0:TS, 0:PAST + TS], axis=AX, op=ALU.max, negate=True)\
                    .then_inc(smax_ready, 1)
                dve.wait_ge(sexp_ready, b + 1)
                v.reciprocal(rinv[0:TS, 0:1], sums[0:TS, 0:1])
                dve.drain()
                v.tensor_scalar(sP, sP, rinv[0:TS, 0:1], None, ALU.mult).then_inc(sp_ready, 1)
                dve.wait_ge(sp_tr, b + 1)
                v.tensor_copy(sPT[:, 0:NPG, :].rearrange("p a b -> p (a b)"), bank(3))
                v.tensor_copy(sPT[0:TS, NPG, :], bank(6, 0, TS, rows=TS)).then_inc(spt_ready, 1)
                dve.wait_ge(spv_done, b + 1)
                for i in range(2):
                    last = v.tensor_copy(
                        mix[64 * i:64 * i + 64, 0:G, bass.ds(b * LS + L, LS)],
                        bank(7, 0, 16 * G)[64 * i:64 * i + 64, :].rearrange("p (g c) -> p g c", c=16)
                        [:, :, LS * i:LS * i + LS])
                last.then_inc(so_copied, 1)
            phase_end(dve, "dve", 5)

            def chunk_ends(ap, c):
                e = ap.rearrange("p (n c) -> p n c", c=c)[:, :, c - 1:c]
                return e.broadcast_to([P, ap.shape[1] // c, c])

            dve.wait_ge(hg_zeroed, 1)
            with dve.Fori(0, HH) as h:
                lo(U_HG, 4, h, 1)
                dve.wait_ge(acc_read, 4 * h + (U_HG + 1))
                om, lbh = omlb[:, bass.ds(h, 1)], lb[:, bass.ds(h, 1)]
                v.tensor_tensor(hK, hK, om.broadcast_to([P, T]), ALU.mult)
                v.tensor_tensor(hF, hF, om.broadcast_to([P, T]), ALU.mult)
                dve.drain()
                v.tensor_tensor(hF, hF, lbh.broadcast_to([P, T]), ALU.add).then_inc(f_ready, 1)
                lo(U_HG, 4, h, 2)
                dve.wait_ge(g_ready, h + 1)
                v.tensor_tensor_scan(hB, reset[:, :], hF, 0.0, ALU.mult, ALU.add).then_inc(b_ready, 1)
                lo(U_HG, 4, h, 3)
                dve.wait_ge(eb_ready, h + 1)
                v.tensor_mul(hQ, hQ, hE)
                v.tensor_mul(hN, hK, hN)
                dve.drain().then_inc(hg_ops, 1)
                v.tensor_copy(q_by_b_own, by_batch(hQ[:, L:T]))
                v.tensor_tensor(hK[:, 0:L].rearrange("p (n c) -> p n c", c=HG_CHUNK),
                                hN[:, 0:L].rearrange("p (n c) -> p n c", c=HG_CHUNK),
                                chunk_ends(hE[:, 0:L], HG_CHUNK), ALU.mult)
                v.tensor_tensor(by_batch(hK[:, L:T]), by_batch(hN[:, L:T]), chunk_ends(hE[:, L:T], LS), ALU.mult)
                v.memset(states[0], 0.0)
                dve.drain().then_inc(hg_ops, 1)
                lo(U_HG, 4, h, 4)
                for i, (src, dst) in enumerate((
                        (psum[:, 0:L], h_vtok[:, 0:NT, :].rearrange("p a b -> p (a b)")),
                        (bank(2, 0, P, rows=TS), h_vtok[0:TS, NT, :]))):
                    dve.wait_ge(hv_tr, h + 1)
                    v.tensor_copy(dst, src)
                dve.drain().then_inc(hv_copied, 1)
                dve.wait_ge(hkd_tr, h + 1)
                v.tensor_copy(h_kdtok[:, 0:NT, :].rearrange("p a b -> p (a b)"), psum[:, 1536:1536 + L])
                v.tensor_copy(h_kdtok[0:TS, NT, :], bank(5, 0, P, rows=TS))
                dve.drain().then_inc(hkd_copied, 1)
                v.tensor_tensor(kd_by_b, h_kdtok[0:TS, NT, :].unsqueeze(1).broadcast_to([TS, NB, DK]),
                                batch_mask[:, :].unsqueeze(2).broadcast_to([TS, NB, DK]), ALU.mult)
                dve.drain().then_inc(masked_ready, 1)
                for t in range(NT):
                    dve.wait_ge(a_ready, (NT + 1) * h + t + 1)
                    if t >= 2:
                        dve.wait_ge(ho_ready, (NT + 1) * h + t - 1)
                    past_waits(dve, "dve")
                    v.copy_predicated(a_mask[t % 2], chunk_mask[:, :].bitcast(I32), bank(2 + t % 2, 0, P))\
                        .then_inc(a_masked, 1)
                    dve.wait_ge(ds_ready, NT * h + t + 1)
                    for i in range(CP):
                        c = CP * t + i
                        if c + 1 >= 8 and (c + 1) % CP == 0:
                            dve.wait_ge(ho_ready, (NT + 1) * h + (c - 7) // CP + 1)
                        end = HG_CHUNK * (c + 1) - 1
                        v.scalar_tensor_tensor(states[(c + 1) % 8], states[c % 8], hE[:, end:end + 1],
                                               bank(t % 2, P * i, P * i + P), ALU.mult, ALU.add)\
                            .then_inc(s_ready, 1)
                        dve.wait_ge(s_ready, NCH * h + c + 1)
                dve.wait_ge(a_ready, (NT + 1) * h + NT + 1)
                past_waits(dve, "dve")
                v.copy_predicated(a_mask_s, chunk_mask_s[:, :].bitcast(I32), bank(2, 0, TS, rows=TS))\
                    .then_inc(a_masked, 1)
                dve.wait_ge(sds_ready, h + 1)
                dve.wait_ge(ho_ready, (NT + 1) * h + NT + 1)
                for b in range(NB):
                    end = L + LS * (b + 1) - 1
                    v.scalar_tensor_tensor(s_states[:, b, :], s_states[:, b, :], hE[:, end:end + 1],
                                           psum[:, P * b:P * b + P], ALU.mult, ALU.add)
                dve.drain().then_inc(s_new_ready, 1)
                dve.wait_ge(hss_ready, h + 1)
                v.tensor_scalar(h_ms, h_ms, 1.0 / DV, EPS, ALU.mult, ALU.add).then_inc(hms_ready, 1)
                dve.wait_ge(hrstd, h + 1)
                v.tensor_tensor(h_otok[:, 0:NT, :], h_otok[:, 0:NT, :],
                                h_ms[:, 0:NT].unsqueeze(2).broadcast_to([P, NT, DV]), ALU.mult)
                v.tensor_scalar(h_otok[0:TS, NT, :], h_otok[0:TS, NT, :], h_ms[0:TS, NT:NT + 1], None, ALU.mult)
                dve.drain().then_inc(hn_ready, 1)
                dve.wait_ge(ho_tr, h + 1)
                v.scalar_tensor_tensor(mix[:, bass.ds(h + G, 1), :].rearrange("p a b -> p (a b)"), psum[:, 0:T],
                                       vec[:, V_ON:V_ON + 1], hS, ALU.mult, ALU.mult).then_inc(ho_mixed, 1)
                dve.wait_ge(state_stored, 32 * h + 32)
            phase_end(dve, "dve", 6)

            with dve.Fori(0, KD // 2) as it:
                for dd in range(2):
                    d = 2 * it + dd
                    for j in range(2):
                        lo(U_MG, 4, it, 2 * dd + j + 1)
                    dve.wait_ge(acc_read, 4 * it + (U_MG + 2 * dd + 2))
                    dst = merged[:, bass.ds(d, 1), :].rearrange("p a b -> p (a b)")
                    for i in range(6):
                        a, b = PIECES[i % 3]
                        dve.wait_ge(br_ready, 6 * d + i + 1)
                        v.tensor_mul(dst[:, a:b] if i < 3 else br_tmp[:, a:b], bank(6 + i % 2, 0, b - a),
                                     (gate_h if i < 3 else gate_f)[:, a:b]).then_inc(br_read, 1)
                    dve.drain()
                    v.tensor_add(dst, dst, br_tmp)
                    dve.drain().then_inc(br_added, 1)
            for d in range(KD):
                dve.wait_ge(h_raw, 2 * KD + d + 1)
                v.tensor_sub(h_lo[:, d, :], merged[:, d, :], h_hi[:, d, :].bitcast(F32))
            phase_end(dve, "dve", 7)

            v.memset(sq_sum, 0.0)
            dve.drain()

            def add_square(y):
                v.tensor_mul(sq, y, y)
                dve.drain()
                v.tensor_add(sq_sum, sq_sum, sq)
                dve.drain()

            def mean_square(k):
                dve.wait_ge(ss_tr, k)
                v.tensor_scalar(stat[:, 0:NT], bank(6, 0, NT), 1.0 / D, EPS, ALU.mult, ALU.add)
                v.tensor_scalar(stat[0:TS, NT:NT + 1], bank(6, NT, NT + 1, rows=TS), 1.0 / D, EPS, ALU.mult, ALU.add)
                dve.drain().then_inc(ms_ready, 1)

            def scaled(dst, y, m, d):
                v.scalar_tensor_tensor(dst[:, 0:L], y[:, 0:L], m[:, d, 0:1], rb[:, 0:L], ALU.mult, ALU.mult)
                v.tensor_mul(dst[:, L:T], y[:, L:T], rb[:, L:T])
                dve.drain()
                v.tensor_tensor(by_batch(dst[:, L:T]), by_batch(dst[:, L:T]), per_batch(m, d), ALU.mult)
                dve.drain()

            with dve.Fori(0, KD // 2) as it:
                for j in range(2):
                    lo(U_OUT, 2, it, j + 1)
                    dve.wait_ge(acc_read, 2 * it + (U_OUT + j + 1))
                    add_square(yT[:, bass.ds(2 * it + j, 1), :].rearrange("p a b -> p (a b)"))
            dve.drain().then_inc(y_sq, 1)
            mean_square(1)
            dve.wait_ge(rb_copied, 1)
            v.memset(sq_sum, 0.0)
            for d in range(KD):
                scaled(t1[0], yT[:, d, :], post1, d)
                dve.wait_ge(xT_ready, d + 1)
                v.tensor_add(yT[:, d, :], t1[0], acc(d % 2))
                dve.drain().then_inc(x1_ready, 1)
                add_square(yT[:, d, :])
            dve.drain().then_inc(y_sq, 1)
            mean_square(2)
            dve.wait_ge(rb_copied, 2)
            for d in range(KD + 1):
                if d < KD:
                    t = t1[d % 2]
                    scaled(t, yT[:, d, :], pre2, d)
                    v.tensor_tensor(by_batch(t[:, L:T]), by_batch(t[:, L:T]), per_batch(mod[:, 3 * KD:4 * KD, :], d),
                                    ALU.add)
                    dve.drain().then_inc(h2_scaled, 1)
                if d >= 1:
                    dve.wait_ge(h2_raw, d)
                    v.tensor_sub(h_lo[:, d - 1, :], t1[(d - 1) % 2], h_hi[:, d - 1, :].bitcast(F32))
                    dve.drain()
            phase_end(dve, "dve", 8)

            def mlp_block(it, last=False):
                for j in range(UT):
                    lo(U_MLP, 2 * UT, it, j + 1)
                    dve.wait_ge(relu_ready, UT * it + j + 1)
                    v.tensor_mul(usq, relu[j % 2], relu[j % 2])
                    dve.drain()
                    dve.wait_ge(u_hi_ready, UT * it + j + 1)
                    v.tensor_sub(u_lo[:, j, :], usq, u_hi[:, j, :].bitcast(F32))
                    dve.drain().then_inc(u_lo_ready, 1)
                for j in range(UT):
                    if not (last and j == UT - 1):
                        lo(U_MLP, 2 * UT, it, UT + j + 1)

            with dve.Fori(0, NMB - 1) as it:
                mlp_block(it)
            mlp_block(NMB - 1, last=True)
            phase_end(dve, "dve", 9)

            v.memset(sq_sum, 0.0)
            dve.drain()
            for d in range(KD):
                add_square(yT[:, d, :])
            dve.drain().then_inc(y_sq, 1)
            mean_square(3)
            dve.wait_ge(rb_copied, 3)
            for d in range(KD):
                scaled(yT[:, d, :], yT[:, d, :], post2, d)
                dve.wait_ge(x1_back, 16 * d + 16)
                v.tensor_add(yT[:, d, :], yT[:, d, :], x1b[d % 2])
                dve.drain().then_inc(fin_ready, 1)

        @block.tensor
        def _(pe):
            mm, tr = nc.tensor.matmul, nc.tensor.transpose

            pe.wait_ge(consts_ready, 1)
            pe.wait_ge(vecs_landed, 16 * 10)
            tr(bank(6, 0, NV), vec_rows[:, :], ident[0:NV, 0:NV])
            tr(bank(7, 0, NC * KD), c_rows[:, :], ident[0:NC * KD, 0:NC * KD]).then_inc(vecs_tr, 1)
            tr(bank(4, 0, LS, rows=TS), not_after[:, :, :].rearrange("p h q -> p (h q)"), ident[0:LS, 0:LS])\
                .then_inc(vecs_tr, 1)
            pe.wait_ge(c_ready, 1)
            c_cols = c_act[:, :].rearrange("p (c k) -> p k c", k=KD)
            with pe.Fori(0, NM // 12) as it:
                for i in range(3):
                    pe.wait_ge(ada_landed[i], 16 * it + 16)
                    w = ada_ring[i].rearrange("p (k n) -> p k n", n=512)
                    for m in range(4):
                        for k in range(KD):
                            last = mm(psum[:, bass.ds(it * (12 * NC) + (5 * 512 + (4 * i + m) * NC), NC)],
                                      w[:, k, P * m:P * m + P], c_cols[:, k, :], start=(k == 0), stop=(k == KD - 1))
                    last.then_inc(ada_used, 1)
            pe.drain().then_inc(mod_ready, 1)
            phase_end(pe, "pe", 1)

            for d in range(KD):
                last = tr(bank(2, TS * d, TS * d + TS), xs_tile[:, P * d:P * d + P], ident[0:TS, 0:TS])
            for i in range(2 * KD):
                if i >= 2:
                    pe.wait_ge(h_raw, i - 1)
                for t in range(4):
                    tile = 4 * (i % 2) + t
                    last = tr(bank(i % 2, P * t, P * t + P), xall[:, tile, P * (i // 2):P * (i // 2) + P], ident[:, :])
                last.then_inc(h_tr, 1)
            pe.drain().then_inc(h_tr, 1)
            phase_end(pe, "pe", 2)

            project(pe, U_FF, 0)
            pe.wait_ge(past_logf_landed, 16 * NB * NPG)
            for g in range(NPG):
                tr(psum[0:TS, 1536 + P * g:1536 + P * g + P],
                   past_lf[:, g, :, :].rearrange("p b h -> p (b h)"), ident[:, :])
            pe.drain().then_inc(lf_tr, 1)
            pe.wait_ge(lf_ready, 1)
            for t in range(NT + 1):
                r = P if t < NT else TS
                last = tr(bank(6, FH * t, FH * t + FH, rows=r), lf_T[:, P * t:P * t + r], ident[0:FH, 0:FH])
            last.then_inc(lf_out_tr, 1)
            phase_end(pe, "pe", 3)

            with pe.Fori(0, G // 2) as it:
                for gg in range(2):
                    g = 2 * it + gg
                    for j in range(3):
                        n, slot, _ = number(U_FOX, 6, it, 3 * gg + j)
                        project(pe, n, slot, acc_free=(j == 0))
                    pe.wait_ge(acc_read, 6 * it + (U_FOX + 3 * gg + 3))

                    def four(src, dst, first):
                        for t in range(4):
                            last = tr(bank(dst, P * t, P * t + P), src[:, P * (first + t):P * (first + t) + P],
                                      ident[:, :])
                        last.then_inc(tok_tr, 1)

                    four(fvT, 2, 0)
                    four(fvT, 5, 4)
                    tr(bank(6, 0, P, rows=TS), fvT[:, L:T], ident[:, :]).then_inc(tok_tr, 1)
                    four(fkT, 7, 0)
                    pe.wait_ge(tok_copied, 6 * g + 3)
                    past_waits(pe, "pe")
                    tr(bank(6, P, 2 * P, rows=TS), fkT[:, L:T], ident[:, :]).then_inc(tok_tr, 1)
                    four(fkT, 2, 4)
                    pe.wait_ge(tok_copied, 6 * g + 6)
                    for a in range(18):
                        if a < 16:
                            j, i = a // NT, a % NT
                            n = P * (i + 1)
                            rows = slice(64 * j, 64 * j + 64)
                            if a >= 2:
                                pe.wait_ge(probs_ready, 16 * g + a - 1)
                            base = 1536 * (a % 2)
                            for c in range(0, n, 512):
                                e = min(c + 512, n)
                                mm(psum[:, base + c:base + e], fqT[rows, P * i:P * i + P], fkT[rows, c:e], start=True,
                                   stop=False)
                                if e == n:
                                    mm(psum[:, base + n - P:base + n], ident_b[:, :], causal_neg[:, :], start=False,
                                       stop=False)
                                last = mm(psum[:, base + c:base + e],
                                          neg_pick[0:96, bass.ds(2 * g + j, 1), :].rearrange("p a b -> p (a b)"),
                                          d_parts[:, c:e], start=False, stop=True)
                            last.then_inc(scores_ready, 1)
                        e = a - 1
                        if 0 <= e < 16:
                            pe.wait_ge(probs_ready, 16 * g + e + 1)
                            if e >= 1:
                                pe.wait_ge(pt_low, 16 * g + e)
                            if e >= 5 and (e - 1) // NT >= 0:
                                done = (e // NT) * 4 + max(0, e % NT - 4)
                                if done:
                                    pe.wait_ge(pt_high, 8 * g + done)
                            for kb in range(e % NT + 1):
                                last = tr(bank(2 if kb < 4 else 5, P * (kb % 4), P * (kb % 4) + P),
                                          probs[e % 2][:, P * kb:P * kb + P], ident[:, :])
                            last.then_inc(probs_tr, 1)
                        o = a - 2
                        if o >= 0:
                            pe.wait_ge(pt_low, 16 * g + o + 1)
                            if o % NT >= 4:
                                pe.wait_ge(pt_high, 8 * g + (o // NT) * 4 + o % NT - 3)
                            if o >= 2:
                                pe.wait_ge(o_ready, 16 * g + o - 1)
                            for kb in range(o % NT + 1):
                                last = mm(bank(6 + o % 2, 0, DH), probsT[o % 2][:, kb, :],
                                          f_vtok[:, kb, DH * (o // NT):DH * (o // NT) + DH], start=(kb == 0),
                                          stop=(kb == o % NT))
                            last.then_inc(pv_done, 1)
                    pe.wait_ge(o_ready, 16 * g + 16)
                    for i in range(2):
                        for t in range(4):
                            last = tr(bank((2, 5)[i], P * t, P * t + P), f_otok[:, 4 * i + t, :], ident[:, :])
                        last.then_inc(o_tr, 1)
                    pe.wait_ge(o_copied, 2 * g + 2)
            phase_end(pe, "pe", 4)

            with pe.Fori(0, NB) as b:
                pe.wait_ge(sk_landed, 16 * NPG * b + 16 * NPG)
                for i in range(8):
                    if i >= 2:
                        pe.wait_ge(*((sk_copied_dve, 4 * b + i // 2), (sk_copied_act, 4 * b + i // 2))[i % 2])
                    for t in range(4):
                        last = tr(bank(4 + i % 2, P * t, P * t + P),
                                  sK[:, 4 * (i % 2) + t, P * (i // 2):P * (i // 2) + P], ident[:, :])
                    last.then_inc(sk_tr, 1)
                pe.wait_ge(sk_copied_dve, 4 * b + 4)
                pe.wait_ge(sk_copied_act, 4 * b + 4)
                pe.wait_ge(sq_ready, b + 1)
                new = psum[0:TS, PAST:PAST + TS]
                for c in range(2):
                    for g in range(G):
                        mm(bank(c, rows=TS), sQ[:, g, :], sKT[:, g, 512 * c:512 * c + 512], start=(g == 0), stop=False)
                    mm(bank(c, rows=TS), sPick, d_past[:, 512 * c:512 * c + 512], start=False, stop=True)
                for g in range(G):
                    mm(new, sQ[:, g, :], k_new[:, g, :], start=(g == 0), stop=False)
                mm(new, ident_b[0:TS, 0:TS], sNeg, start=False, stop=False)
                mm(new, sPick, d_past[:, PAST:PAST + LS].unsqueeze(1).broadcast_to([TS, NB, LS]), start=False,
                   stop=True).then_inc(ss_ready, 1)
                pe.wait_ge(sp_ready, b + 1)
                past_waits(pe, "pe")
                for t in range(NPG):
                    tr(bank(3, TS * t, TS * t + TS), sP[:, P * t:P * t + P], ident[0:TS, 0:TS])
                tr(bank(6, 0, TS, rows=TS), sP[:, PAST:PAST + TS], ident[0:TS, 0:TS]).then_inc(sp_tr, 1)
                pe.wait_ge(spt_ready, b + 1)
                pe.wait_ge(sv_landed, 16 * NPG * b + 16 * NPG)
                for g in range(G):
                    out = bank(7, 16 * g, 16 * g + 16)
                    for t in range(NPG):
                        mm(out, sV[:, t, P * g:P * g + P], sPT[:, t, 16 * g:16 * g + 16], start=(t == 0), stop=False)
                    last = mm(out, v_new[:, P * g:P * g + P], sPT[0:TS, NPG, 16 * g:16 * g + 16], start=False,
                              stop=True)
                last.then_inc(spv_done, 1)
                pe.wait_ge(so_copied, b + 1)
            phase_end(pe, "pe", 5)

            pe.wait_ge(hg_zeroed, 1)
            with pe.Fori(0, HH) as h:
                for j in range(4):
                    n, slot, _ = number(U_HG, 4, h, j)
                    project(pe, n, slot)
                pe.wait_ge(acc_read, 4 * h + (U_HG + 4))
                for t in range(NT):
                    tr(psum[:, P * t:P * t + P], hV[:, P * t:P * t + P], ident[:, :])
                tr(bank(2, 0, P, rows=TS), hV[:, L:T], ident[:, :]).then_inc(hv_tr, 1)
                pe.wait_ge(hg_ops, 2 * h + 2)
                for t in range(NT):
                    tr(psum[:, 1536 + P * t:1536 + P * t + P], hK[:, P * t:P * t + P], ident[:, :])
                tr(bank(5, 0, P, rows=TS), hK[:, L:T], ident[:, :]).then_inc(hkd_tr, 1)
                pe.wait_ge(hv_copied, h + 1)
                pe.wait_ge(hkd_copied, h + 1)
                for t in range(NT + 1):
                    if t < NT:
                        cols = slice(P * t, P * t + P)
                        if t >= 2:
                            pe.wait_ge(a_masked, (NT + 1) * h + t - 1)
                        mm(bank(2 + t % 2, 0, P), hN[:, cols], hQ[:, cols], start=True, stop=True).then_inc(a_ready, 1)
                        if t >= 2:
                            pe.wait_ge(s_ready, NCH * h + CP * (t - 1))
                        pe.wait_ge(v_spread, NT * h + t + 1)
                        mm(bank(t % 2), h_kdtok[:, t, :], v_by_chunk[:, t % 2, :, :].rearrange("p c v -> p (c v)"),
                           start=True, stop=True).then_inc(ds_ready, 1)
                    e = t - 1
                    if e >= 0:
                        pe.wait_ge(a_masked, (NT + 1) * h + e + 1)
                        if e >= 1:
                            pe.wait_ge(s_ready, NCH * h + CP * e + CP - 1)
                        else:
                            pe.wait_ge(s_ready, NCH * h + CP - 1)
                        if e >= 2:
                            pe.wait_ge(ho_copied, (NT + 1) * h + e - 1)
                        mm(bank(4 + e % 2, 0, P), a_mask[e % 2], h_vtok[:, e, :], start=True, stop=False)
                        for i in range(CP):
                            last = mm(bank(4 + e % 2, 0, P)[32 * i:32 * i + 32, :],
                                      hQ[:, P * e + 32 * i:P * e + 32 * i + 32], states[(CP * e + i) % 8], start=False,
                                      stop=True)
                        last.then_inc(ho_ready, 1)
                mm(bank(2, 0, TS, rows=TS), hN[:, L:T], hQ[:, L:T], start=True, stop=True).then_inc(a_ready, 1)
                pe.wait_ge(masked_ready, h + 1)
                pe.wait_ge(s_ready, NCH * h + NCH)
                for b in range(NB):
                    last = mm(psum[:, P * b:P * b + P], kd_by_b[:, b, :], h_vtok[0:TS, NT, :], start=True, stop=True)
                last.then_inc(sds_ready, 1)
                pe.wait_ge(a_masked, (NT + 1) * h + NT + 1)
                pe.wait_ge(s0_landed, 16 * h + 16)
                pe.wait_ge(ho_copied, (NT + 1) * h + NT - 1)
                past_waits(pe, "pe")
                mm(bank(4, 0, P, rows=TS), a_mask_s, h_vtok[0:TS, NT, :], start=True, stop=False)
                for b in range(NB):
                    last = mm(bank(4, 0, P, rows=TS), q_by_b[:, b, :], s_states[:, b, :], start=False,
                              stop=(b == NB - 1))
                last.then_inc(ho_ready, 1)
                pe.wait_ge(hn_ready, h + 1)
                for t in range(NT):
                    tr(psum[:, P * t:P * t + P], h_otok[:, t, :], ident[:, :])
                tr(bank(2, 0, TS), h_otok[0:TS, NT, :], ident[0:TS, 0:TS]).then_inc(ho_tr, 1)
                pe.wait_ge(ho_mixed, h + 1)
            phase_end(pe, "pe", 6)

            with pe.Fori(0, KD // 2) as it:
                for dd in range(2):
                    d = 2 * it + dd
                    for j in range(2):
                        n, slot, _ = number(U_MG, 4, it, 2 * dd + j)
                        project(pe, n, slot)
                    pe.wait_ge(br_landed[dd], 32 * it + 32)
                    w = br_raw[dd].rearrange("p (k n) -> p k n", n=P)
                    for i in range(6):
                        a, b = PIECES[i % 3]
                        if i >= 2:
                            pe.wait_ge(br_read, 6 * d + i - 1)
                        for k in range(4):
                            kw = k if i < 3 else HH + k
                            km = G + k if i < 3 else k
                            last = mm(bank(6 + i % 2, 0, b - a), w[:, kw, :], mix[:, km, a:b], start=(k == 0),
                                      stop=(k == 3))
                        last.then_inc(br_ready, 1)
                    pe.wait_ge(br_read, 6 * d + 6)
            phase_end(pe, "pe", 7)

            with pe.Fori(0, KD // 2) as it:
                for j in range(2):
                    n, slot, _ = number(U_OUT, 2, it, j)
                    project(pe, n, slot)

            def norm_rows(k):
                pe.wait_ge(y_sq, k)
                for t in range(NT + 1):
                    r = P if t < NT else TS
                    last = mm(bank(6, t, t + 1, rows=r), sq_sum[:, P * t:P * t + r], ones[:, 0:1], start=True,
                              stop=True)
                last.then_inc(ss_tr, 1)
                pe.wait_ge(rstd_ready, k)
                for t in range(NT + 1):
                    r = P if t < NT else TS
                    last = mm(psum[:, P * t:P * t + r], stat[0:r, t:t + 1].broadcast_to([r, P]), ident[0:r, 0:r],
                              start=True, stop=True)
                last.then_inc(rb_ready, 1)

            norm_rows(1)
            pe.wait_ge(rb_copied, 1)
            pe.wait_ge(x_landed, 32 * NT)
            pe.wait_ge(xs_landed, 32)
            for d in range(KD):
                if d >= 2:
                    pe.wait_ge(x1_ready, d - 1)
                for t in range(NT):
                    tr(acc(d % 2)[:, P * t:P * t + P], xall[:, t, P * d:P * d + P], ident[:, :])
                tr(acc(d % 2)[:, L:T], xs_again[:, P * d:P * d + P], ident[0:TS, 0:TS]).then_inc(xT_ready, 1)
            norm_rows(2)
            phase_end(pe, "pe", 8)

            def mlp_block(it):
                for j in range(UT):
                    n, slot, _ = number(U_MLP, 2 * UT, it, j)
                    project(pe, n, slot, acc_no=3 * UT * it + (U_MLP + j), acc_slot=(U_MLP + j) % 2)
                for j in range(UT):
                    n, slot, _ = number(U_MLP, 2 * UT, it, UT + j)
                    pe.wait_ge(w_hi_ready, n + 1)
                    pe.wait_ge(w_lo_ready, n + 1)
                    if j == 0:
                        pe.wait_ge(u_hi_ready, UT * it + UT)
                        pe.wait_ge(u_lo_ready, UT * it + UT)
                    for i in range(2):
                        pe.wait_ge(acc_read, 3 * UT * it + (U_MLP + UT + 2 * j + i - 1))
                        out = acc((U_MLP + i) % 2)
                        for k in range(UT):
                            at = 2 * P * k + P * i
                            wh, wl = (w[:, slot, at:at + P] for w in (w_hi, w_lo))
                            for w, m in ((wh, u_hi), (wh, u_lo), (wl, u_hi)):
                                for a, b in PIECES:
                                    last = mm(out[:, a:b], w, m[:, k, a:b],
                                              start=(k == 0 and w is wh and m is u_hi), stop=(k == UT - 1 and w is wl))
                        last.then_inc((down_half, unit_done)[i], 1)

            with pe.Fori(0, NMB) as it:
                mlp_block(it)
            phase_end(pe, "pe", 9)

            norm_rows(3)
            pe.wait_ge(rb_copied, 3)
            for d in range(KD):
                pe.wait_ge(fin_ready, d + 1)
                if d >= 2:
                    pe.wait_ge(fin_copied, d - 1)
                base = 2048 * (d % 2)
                for t in range(NT):
                    tr(psum[:, base + P * t:base + P * t + P], yT[:, d, P * t:P * t + P], ident[:, :])
                tr(psum[0:TS, base + L:base + L + P], yT[:, d, L:T], ident[:, :]).then_inc(fin_tr, 1)


_INS = ['x_prompt', 'x_sample', 'c_prompt', 'c_sample', 'cache_k', 'cache_v', 'cache_logf', 'state_hgrn', 'page_table',
        'ada_w', 'ada_b', 'norm_mix_pre', 'norm_mix_post', 'norm_mlp_pre', 'norm_mlp_post', 'w_in',
        'hgrn_lower_bounds', 'hgrn_onorm', 'fox_b_f', 'w_br_h', 'w_br_f', 'w_out', 'w_mlp_up', 'w_mlp_down']


def kernel(**inputs):
    import numpy as _np
    import concourse.bacc as _bacc
    from concourse import mybir as _mybir
    from concourse.bass_utils import run_bass_kernel_spmd as _run

    xp, xs, ck, st = (inputs[n].shape for n in ('x_prompt', 'x_sample', 'cache_k', 'state_hgrn'))
    heads = (ck[3], ck[4])
    outs = [xp, xs, (1, 1, xp[1]) + heads, (1, 1, xp[1]) + heads, (1, 1, xp[1], ck[3]), (1, 1) + tuple(st[2:]),
            (1, xs[0], xs[1]) + heads, (1, xs[0], xs[1]) + heads, (1, xs[0], xs[1], ck[3]), tuple(st)]
    nc = _bacc.Bacc("TRN2", target_bir_lowering=False, num_devices=1)
    arrays, args = {}, []
    for name in _INS:
        a = _np.ascontiguousarray(inputs[name])
        arrays[f"in_{name}"] = a
        args.append(nc.dram_tensor(f"in_{name}", a.shape, _mybir.dt.from_np(a.dtype), kind="ExternalInput").ap())
    for i, shape in enumerate(outs):
        args.append(nc.dram_tensor(f"out_{i}", tuple(shape), F32, kind="ExternalOutput").ap())
    build_layer(nc, *args)
    r = _run(nc, [arrays], core_ids=[0])
    return tuple(r.results[0][f"out_{i}"] for i in range(len(outs)))
```

```python
from contextlib import ExitStack

import concourse.bass as bass
from concourse import mybir

F32 = mybir.dt.float32
F32R = mybir.dt.float32r
BF16 = mybir.dt.bfloat16
I32 = mybir.dt.int32
ALU = mybir.AluOpType
ACT = mybir.ActivationFunctionType
AX = mybir.AxisListType.X

P = 128
NEG = -1e30
EPS = 1e-6
HG_CHUNK = 32


def build_layer(nc, x_prompt, x_sample, c_prompt, c_sample, cache_k, cache_v, cache_logf, state_hgrn, page_table,
                ada_w, ada_b, norm_mix_pre, norm_mix_post, norm_mlp_pre, norm_mlp_post, w_in, hgrn_lower_bounds,
                hgrn_onorm, fox_b_f, w_br_h, w_br_f, w_out, w_mlp_up, w_mlp_down,
                y_prompt, y_sample, k_prompt, v_prompt, logf_prompt, s_prompt, k_sample, v_sample, logf_sample,
                s_sample):
    _, L, D = x_prompt.shape
    NB, LS, _ = x_sample.shape
    TS = NB * LS
    T = L + TS
    KD = D // P
    NT = L // P
    _, NPHYS, PAGE, FH, DH = cache_k.shape
    NPG = page_table.shape[1]
    PAST = NPG * PAGE
    HH, DK, DV = state_hgrn.shape[2:]
    HW, FW = HH * DK, FH * DH
    FF = w_mlp_up.shape[2]
    NM = ada_w.shape[2] // P
    NC = 1 + NB
    G = FW // P
    CP = P // HG_CHUNK
    NCH = L // HG_CHUNK
    NM1 = 2 * KD
    MB = 512
    NMB = FF // MB
    UT = MB // P
    assert (L, D, TS, PAGE, DK, DV, DH, KD, G, HH) == (1024, 1024, 64, P, P, P, 64, 8, 4, 4)
    O_HQ, O_HF, O_HI, O_HG = 0, HW, 2 * HW, 3 * HW
    O_FQ, O_FK, O_FV = 4 * HW, 4 * HW + FW, 4 * HW + 2 * FW
    O_FF = O_FV + FW
    O_MG = O_FF + FH
    V_AB, V_N1, V_P1, V_N2, V_P2 = 0, NM, NM + KD, NM + 2 * KD, NM + 3 * KD
    V_ON, V_L0 = NM + 4 * KD, NM + 4 * KD + 1
    V_L1 = V_L0 + HH
    NV = V_L1 + HH
    U_FF, U_FOX, U_HG = 0, 1, 1 + 3 * G
    U_MG = U_HG + 4 * HH
    U_OUT = U_MG + 2 * KD
    U_MLP = U_OUT + KD

    w_in_v = w_in[0].rearrange("(k p) n -> p k n", p=P)
    w_out_v = w_out[0].rearrange("(k p) n -> p k n", p=P)
    w_up_v = w_mlp_up[0].rearrange("(k p) n -> p k n", p=P)
    w_dn_v = w_mlp_down[0].rearrange("(k p) n -> p k n", p=P)
    w_bh_v = w_br_h[0].rearrange("(k p) n -> p k n", p=P)
    w_bf_v = w_br_f[0].rearrange("(k p) n -> p k n", p=P)
    ada_v = ada_w[0].rearrange("(k p) n -> p k n", p=P)
    kp_v = k_prompt[0, 0].rearrange("(t p) h d -> p t (h d)", p=P)
    vp_v = v_prompt[0, 0].rearrange("(t p) h d -> p t (h d)", p=P)
    yp_v = y_prompt[0].rearrange("(t p) n -> p t n", p=P)
    ys_v = y_sample.rearrange("b l n -> (b l) n")
    xp_v = x_prompt[0].rearrange("(t p) n -> p t n", p=P)
    xs_v = x_sample.rearrange("b l n -> (b l) n")
    ck_v = cache_k[0].rearrange("g p h d -> g p (h d)")
    cv_v = cache_v[0].rearrange("g p h d -> g p (h d)")
    cl_v = cache_logf[0]
    x1_dram = nc.dram_tensor("x1_scratch", [P, KD, T], F32, kind="Internal").ap()

    with ExitStack() as ctx:
        def sb(name, shape, dt=F32):
            return ctx.enter_context(nc.sbuf_tensor(name, shape, dt))

        def sem(name):
            return ctx.enter_context(nc.semaphore(name))

        h_hi, h_lo = sb("h_hi", [P, KD, T], F32R), sb("h_lo", [P, KD, T], F32R)
        w_raw = sb("w_raw", [P, 2, 1024])
        w_hi, w_lo = sb("w_hi", [P, 2, 1024], F32R), sb("w_lo", [P, 2, 1024], F32R)
        ident = sb("ident", [P, P])
        ident_b = sb("ident_b", [P, P], BF16)
        ones = sb("ones", [P, 1])
        causal_neg = sb("causal_neg", [P, P], BF16)
        chunk_mask = sb("chunk_mask", [P, P])
        chunk_mask_s = sb("chunk_mask_s", [TS, TS])
        batch_mask = sb("batch_mask", [TS, NB])
        new_neg_room = sb("new_neg", [TS, NB * (TS + LS)], BF16)
        new_neg = new_neg_room[:, 0:NB * TS].rearrange("p (b k) -> p b k", k=TS)
        new_neg_own = new_neg_room[:, :].rearrange("p (b k) -> p b k", k=TS + LS)[:, :, 0:LS]
        not_after = sb("not_after", [LS, FH, LS])
        neg_pick = sb("neg_pick", [P, FH, P], BF16)
        neg_pick_s = sb("neg_pick_s", [TS, NB, TS])
        reset = sb("reset", [P, T])
        d_past = reset[0:TS, 0:PAST + LS]
        vec = sb("vec", [P, NV])
        c_act = sb("c_act", [P, NC * KD])
        mod = sb("mod", [P, NM, NC])
        pre1, post1 = sb("pre1", [P, KD, NC]), sb("post1", [P, KD, NC])
        pre2, post2 = sb("pre2", [P, KD, NC]), sb("post2", [P, KD, NC])
        lb, omlb = sb("lb", [P, HH]), sb("omlb", [P, HH])
        lb_diff = sb("lb_diff", [P, HH])
        fox_b = sb("fox_b", [FH, 1])
        stat = sb("stat", [P, NT + 1])
        zero = sb("zero", [P, NT + 1])
        half = sb("half", [P, NT + 1])
        d_parts = sb("d_parts", [96, L], BF16)
        q_new, k_new = sb("q_new", [P, G, TS]), sb("k_new", [P, G, TS])
        new_tok = sb("new_tok", [2 * TS, FW])
        v_new, k_new_tok = new_tok[0:TS, :], new_tok[TS:2 * TS, :]
        nmax, sums, rinv = sb("nmax", [P, 2]), sb("sums", [P, 16]), sb("rinv", [P, 2])
        pages = sb("pages", [1, NB * NPG], I32)

        with nc.sbuf_tensor("mix", [P, G + HH, T], F32) as mix:
            pass
        u_hi, u_lo = sb("u_hi", [P, UT, T], F32R), sb("u_lo", [P, UT, T], F32R)
        WORK = 15360
        work = sb("work", [P, WORK])

        def cut(at, *shape, rows=P):
            n = 1
            for s in shape:
                n *= s
            assert at + n <= WORK
            v = work[0:rows, at:at + n]
            if len(shape) == 2:
                v = v.rearrange("p (a b) -> p a b", b=shape[1])
            if len(shape) == 3:
                v = v.rearrange("p (a b c) -> p a b c", b=shape[1], c=shape[2])
            return v

        psum = ctx.enter_context(nc.psum_tensor("psum", [P, 8 * 512], F32))

        def bank(i, a=0, b=512, rows=P):
            return psum[0:rows, 512 * i + a:512 * i + b]

        SIDE = (T - 512) // 2
        PIECES = [(0, SIDE), (SIDE, SIDE + 512), (SIDE + 512, T)]

        def acc(slot):
            return psum[:, 1536 * slot + 512 - SIDE:1536 * slot + 512 - SIDE + T]

        raw_landed = [sem("raw_landed0"), sem("raw_landed1")]
        w_hi_ready, w_lo_ready = sem("w_hi_ready"), sem("w_lo_ready")
        unit_done, acc_read = sem("unit_done"), sem("acc_read")
        done_of = {e: sem(f"phase_done_{e}") for e in ("pe", "act", "dve", "pool")}
        vecs_landed, pages_landed, past_logf_landed, x_landed, xs_landed = map(
            sem, ("vecs_landed", "pages_landed", "past_logf_landed", "x_landed", "xs_landed"))
        consts_ready, dve_consts_ready = sem("consts_ready"), sem("dve_consts_ready")
        ada_landed = [sem(f"ada_landed{i}") for i in range(3)]
        ada_used, vecs_tr, vecs_copied, c_ready, mod_ready, mod_done = map(
            sem, ("ada_used", "vecs_tr", "vecs_copied", "c_ready", "mod_ready", "mod_done"))
        x_sumsq, x_ms, x_rstd, x_scaled, h_tr, h_raw, h_split = map(
            sem, ("x_sumsq", "x_ms", "x_rstd", "x_scaled", "h_tr", "h_raw", "h_split"))
        lf_tr, lf_exp, lf_abs, lf_ln, lf_min, lf_ready, lf_out_tr, lf_out_copied, lf_new_moved, d_ready = map(
            sem, ("lf_tr", "lf_exp", "lf_abs", "lf_ln", "lf_min", "lf_ready", "lf_out_tr", "lf_out_copied",
                  "lf_new_moved", "d_ready"))
        tok_tr, tok_copied, new_stashed, kv_stored = map(sem, ("tok_tr", "tok_copied", "new_stashed", "kv_stored"))
        scores_ready, max_ready, probs_ready, probs_tr, pt_low, pt_high, pv_done, o_ready, o_tr, o_copied = map(
            sem, ("scores_ready", "max_ready", "probs_ready", "probs_tr", "pt_low", "pt_high", "pv_done", "o_ready",
                  "o_tr", "o_copied"))
        sk_landed, sv_landed, sq_ready, sk_tr, sk_copied_dve, sk_copied_act, ss_ready, smax_ready, sexp_ready = map(
            sem, ("sk_landed", "sv_landed", "sq_ready", "sk_tr", "sk_copied_dve", "sk_copied_act", "ss_ready",
                  "smax_ready", "sexp_ready"))
        sp_ready, sp_tr, spt_ready, spv_done, so_copied, s_scores_done = map(
            sem, ("sp_ready", "sp_tr", "spt_ready", "spv_done", "so_copied", "s_scores_done"))
        sig_ready, f_ready, g_ready, b_ready, eb_ready, hg_ops, hv_tr, hv_copied, hkd_tr, hkd_copied = map(
            sem, ("sig_ready", "f_ready", "g_ready", "b_ready", "eb_ready", "hg_ops", "hv_tr", "hv_copied", "hkd_tr",
                  "hkd_copied"))
        a_ready, a_masked, ds_ready, s_ready, ho_ready, ho_copied, hss_ready, hms_ready, hrstd, hn_ready = map(
            sem, ("a_ready", "a_masked", "ds_ready", "s_ready", "ho_ready", "ho_copied", "hss_ready", "hms_ready",
                  "hrstd", "hn_ready"))
        ho_tr, ho_mixed, s0_landed, state_stored, sds_ready, s_new_ready, masked_ready = map(
            sem, ("ho_tr", "ho_mixed", "s0_landed", "state_stored", "sds_ready", "s_new_ready", "masked_ready"))
        br_landed = [sem("br_landed0"), sem("br_landed1")]
        br_ready, br_read, br_added, ada_rest_landed, ada_rest_ready, ada_rest_read = map(
            sem, ("br_ready", "br_read", "br_added", "ada_rest_landed", "ada_rest_ready", "ada_rest_read"))
        y_sq, ss_tr, ms_ready, rstd_ready, rb_ready, rb_copied, x1_ready, x1_stored, x1_summed, xT_ready = map(
            sem, ("y_sq", "ss_tr", "ms_ready", "rstd_ready", "rb_ready", "rb_copied", "x1_ready", "x1_stored",
                  "x1_summed", "xT_ready"))
        h2_scaled, h2_raw, h2_split, sq_zeroed, hg_zeroed, down_half, ones_set, v_spread = map(
            sem, ("h2_scaled", "h2_raw", "h2_split", "sq_zeroed", "hg_zeroed", "down_half", "ones_set", "v_spread"))
        relu_ready, u_hi_ready, u_lo_ready, down_copied, down_free = map(
            sem, ("relu_ready", "u_hi_ready", "u_lo_ready", "down_copied", "down_free"))
        fin_ready, fin_tr, fin_copied, stored = map(sem, ("fin_ready", "fin_tr", "fin_copied", "stored"))
        x1_back = [sem("x1_back0"), sem("x1_back1")]
        fin_stored = [sem("fin_stored0"), sem("fin_stored1")]
        x1_sq, fin_sq, fin_summed, merged_split, x_again_landed = map(
            sem, ("x1_sq", "fin_sq", "fin_summed", "merged_split", "x_again_landed"))

        order = ("pe", "act", "dve", "pool")
        passed = {e: sem(f"waits_passed_{e}") for e in order + ("sp",)}

        def past_waits(eng, me):
            eng.sem_inc(passed[me], 1)

        def phase_end(eng, me, k, wait=True):
            eng.drain().then_inc(done_of[me], 1)
            if not wait:
                return
            for o in order:
                if o != me:
                    eng.wait_ge(done_of[o], k)

        def split_hi(act, n, slot, landed):
            act.wait_ge(raw_landed[slot], landed)
            if not (isinstance(n, int) and n < 2):
                act.wait_ge(unit_done, n - 1)
            nc.scalar.activation(w_hi[:, slot, :], w_raw[:, slot, :], ACT.Copy).then_inc(w_hi_ready, 1)

        def split_lo(dve, n, slot):
            dve.wait_ge(w_hi_ready, n + 1)
            nc.vector.tensor_sub(w_lo[:, slot, :], w_raw[:, slot, :], w_hi[:, slot, :].bitcast(F32))\
                .then_inc(w_lo_ready, 1)

        def number(base, per, it, j):
            return base + j + per * it, (base + j) % 2, 16 * ((base + j) // 2 + 1) + 16 * (per // 2) * it

        def project(pe, n, slot, acc_no=None, acc_slot=None, acc_free=False, parts_ready=None):
            acc_no, acc_slot = (n, slot) if acc_no is None else (acc_no, acc_slot)
            hi, lo = h_hi, h_lo
            pe.wait_ge(w_lo_ready, n + 1)
            pe.wait_ge(w_hi_ready, n + 1)
            if not (acc_free or (isinstance(n, int) and n < 2)):
                pe.wait_ge(acc_read, acc_no - 1)
            out = acc(acc_slot)
            for k in range(KD):
                if parts_ready:
                    sem_of, before = parts_ready
                    pe.wait_ge(sem_of, before + k + 1)
                wh, wl = (w[:, slot, P * k:P * k + P] for w in (w_hi, w_lo))
                for w, m in ((wh, hi), (wh, lo), (wl, hi)):
                    for a, b in PIECES:
                        last = nc.tensor.matmul(out[:, a:b], w, m[:, k, a:b], start=(k == 0 and w is wh and m is hi),
                                                stop=(k == KD - 1 and w is wl))
            last.then_inc(unit_done, 1)

        ada_ring = [cut(4096 * i, 4096) for i in range(3)]
        xs_tile = cut(12288, 1024, rows=TS)
        h_tmp = [cut(13312, 512), cut(13824, 512)]
        junk = cut(14336, 1024)
        mix_tail = mix[:, :, :].rearrange("p a b -> p (a b)")[:, NT * 1024:]
        vec_rows, c_rows = cut(13312, P, rows=NV), cut(13312 + P, P, rows=NC * KD)
        xall = mix[:, :, :].rearrange("p a b -> p (a b)")[:, 0:NT * 1024].rearrange("p (t n) -> p t n", n=1024)
        past_lf = mix_tail.rearrange("p (g b h) -> p g b h", b=NB, h=FH)
        lf = 3 * T + 7168
        lf_T, lf_a, lf_m = (cut(lf + T * i, T, rows=FH) for i in range(3))
        lf_d = lf_m[:, 0:L]
        lf_b = cut(lf + 3 * T, L // 2, rows=FH).bitcast(BF16)
        lf_out = cut(lf + 3 * T + L // 2, 128)
        scan_ones = cut(lf + 3 * T + L // 2 + 128, L, rows=TS)
        fkT, fvT, fqT = cut(0, T), cut(T, T), cut(2 * T, T)
        fat = 3 * T
        f_vtok, f_ktok = cut(fat, NT, P), cut(fat + 1024, NT, P)
        probs = [cut(fat + 2048, 1024), cut(fat + 3072, 1024)]
        probsT = [cut(fat + 4096, NT, P), cut(fat + 5120, NT, P)]
        f_otok = cut(fat + 6144, NT, P)
        sK, sKT, sV = cut(0, NPG, FW), cut(4096, G, PAST), cut(8192, NPG, FW)
        sP = cut(12288, PAST + TS, rows=TS)
        sPT = cut(13376, NPG + 1, TS)
        sQ_room = cut(13376 + 576, G * (TS + 2 * LS))
        sQ = sQ_room[:, 0:G * TS].rearrange("p (g c) -> p g c", c=TS)
        sQ_own = sQ_room.rearrange("p (g c) -> p g c", c=TS + 2 * LS)
        sPick = cut(13376 + 896, TS, rows=TS)
        sNeg = cut(13376 + 960, TS // 2, rows=TS).bitcast(BF16)
        hK, hF, hE, hN, hQ, hV, hS = (cut(T * i, T) for i in range(7))
        hg_at = 7 * T
        hB = cut(hg_at, T)
        v_by_chunk = hV[:, 0:2 * CP * P].rearrange("p (i c v) -> p i c v", c=CP, v=P)
        h_otok = cut(hg_at, NT + 1, P)
        h_vtok, h_kdtok = cut(hg_at + 1152, NT + 1, P), cut(hg_at + 2304, NT + 1, P)
        ring = hg_at + 3456
        states = [cut(ring + P * i, P) for i in range(8)]
        a_mask = [cut(ring + 1024, P), cut(ring + 1152, P)]
        a_mask_s = cut(ring + 1280, TS, rows=TS)
        s_states = cut(ring + 1344, NB, DV)
        kd_by_b = cut(ring + 2368, NB, DK, rows=TS)
        q_by_b_room = cut(ring + 3392, NB * (TS + LS))
        q_by_b = q_by_b_room[:, 0:NB * TS].rearrange("p (b t) -> p b t", t=TS)
        q_by_b_own = q_by_b_room.rearrange("p (b t) -> p b t", t=TS + LS)[:, :, 0:LS]
        h_ms = cut(ring + 3392 + 576, NT + 1)
        merged = cut(0, KD, T)
        br_raw = [cut(KD * T, 1024), cut(KD * T + 1024, 1024)]
        ada_raw = cut(KD * T + 2048 + 3 * T, 1024)
        gate_h, gate_f, br_tmp = (cut(KD * T + 2048 + T * i, T) for i in range(3))
        yT = cut(0, KD, T)
        rb = cut(KD * T, T)
        sq = [cut(KD * T + T, T), cut(KD * T + 2 * T, T)]
        t1 = [cut(KD * T + 3 * T, T), cut(KD * T + 4 * T, T)]
        xs_again = cut(KD * T + 5 * T, 1024, rows=TS)
        relu = [cut(KD * T, T), cut(KD * T + T, T)]
        usq = cut(KD * T + 2 * T, T)
        down = [cut(KD * T + 3 * T, T), cut(KD * T + 4 * T, T)]
        x1b = [cut(KD * T + 3 * T, T), cut(KD * T + 4 * T, T)]
        out_tok = [cut(KD * T + 5 * T, NT + 1, P), cut(KD * T + T, NT + 1, P)]

        BR_BANK = (6, 7, 6, 6, 7, 6)
        SUM_BANK = {1: 6, 2: 7, 3: 6}

        def by_batch(ap):
            return ap.rearrange("p (b l) -> p b l", l=LS)

        def per_batch(v, d):
            return v[:, d, 1:NC].unsqueeze(2).broadcast_to([P, NB, LS])

        block = ctx.enter_context(nc.Block())

        @block.sync
        def _(sp):
            def rows(at, n, src):
                sp.dma_start(vec_rows[at:at + n, :], src).then_inc(vecs_landed, 16)

            rows(V_AB, NM, ada_b[0].rearrange("(k p) -> k p", p=P))
            rows(V_N1, KD, norm_mix_pre[0].rearrange("(k p) -> k p", p=P))
            rows(V_P1, KD, norm_mix_post[0].rearrange("(k p) -> k p", p=P))
            rows(V_N2, KD, norm_mlp_pre[0].rearrange("(k p) -> k p", p=P))
            rows(V_P2, KD, norm_mlp_post[0].rearrange("(k p) -> k p", p=P))
            rows(V_ON, 1, hgrn_onorm)
            rows(V_L0, 2 * HH, hgrn_lower_bounds[0:2].rearrange("r (h p) -> (r h) p", p=P))
            sp.dma_start(c_rows[0:KD, :], c_prompt[0].rearrange("(k p) -> k p", p=P)).then_inc(vecs_landed, 16)
            sp.dma_start(c_rows[KD:NC * KD, :], c_sample.rearrange("b (k p) -> (b k) p", p=P))\
                .then_inc(vecs_landed, 16)
            sp.dma_start(fox_b[:, :], fox_b_f.rearrange("a h -> h a")).then_inc(vecs_landed, 16)
            for i in range(3):
                sp.dma_start(ada_ring[i].rearrange("p (k n) -> p k n", n=512), ada_v[:, :, 512 * i:512 * i + 512])\
                    .then_inc(ada_landed[i], 16)
            sp.wait_ge(ada_used, 1)
            sp.dma_start(ada_ring[0].rearrange("p (k n) -> p k n", n=512), ada_v[:, :, 3 * 512:4 * 512])\
                .then_inc(ada_landed[0], 16)

            def load(n, slot, src, width=P):
                if not (isinstance(n, int) and n < 2):
                    sp.wait_ge(w_lo_ready, n - 1)
                    if not isinstance(n, int):
                        past_waits(sp, "sp")
                sp.dma_start(w_raw[:, slot, :].rearrange("p (k n) -> p k n", n=width), src)\
                    .then_inc(raw_landed[slot], 16)

            load(U_FF, 0, w_in_v[:, :, O_FF:O_FF + P])
            for g in range(G):
                for j, off in enumerate((O_FK, O_FV, O_FQ)):
                    n, slot, _ = number(U_FOX, 0, 0, 3 * g + j)
                    load(n, slot, w_in_v[:, :, off + P * g:off + P * g + P])
            def load_heads(first, last):
                for i in range(first, last):
                    h, off = i // 4, (O_HF, O_HQ, O_HI, O_HG)[i % 4]
                    load(U_HG + i, (U_HG + i) % 2, w_in_v[:, :, off + P * h:off + P * h + P])

            def load_pages(page, dst, src, landed):
                for g in range(NPG):
                    sp.dma_start(dst[:, g, :], src[bass.ds(page[g], 1), :, :].rearrange("a p n -> p (a n)"))\
                        .then_inc(landed, 16)

            def page_numbers(b):
                return [sp.value_load(pages[0:1, bass.ds(b * NPG + g, 1)], min_val=0, max_val=NPHYS - 1)
                        for g in range(NPG)]

            load_heads(0, 2)
            sp.wait_ge(pages_landed, 16)
            page = page_numbers(0)
            for e in order:
                sp.wait_ge(done_of[e], 3)
            load_pages(page, sK, ck_v, sk_landed)
            load_pages(page, sV, cv_v, sv_landed)
            with sp.Fori(1, NB) as b:
                page = page_numbers(b)
                sp.wait_ge(sk_tr, 8 * b)
                past_waits(sp, "sp")
                load_pages(page, sK, ck_v, sk_landed)
                sp.wait_ge(spv_done, b)
                past_waits(sp, "sp")
                load_pages(page, sV, cv_v, sv_landed)
            load_heads(2, 4 * HH)
            with sp.Fori(0, KD // 2) as it:
                for dd in range(2):
                    for j in range(2):
                        n, slot, _ = number(U_MG, 4, it, 2 * dd + j)
                        load(n, slot, w_in_v[:, :, bass.ds((2 * it + dd) * P + (O_MG + j * D), P)])
            with sp.Fori(0, KD // 2) as it:
                for j in range(2):
                    n, slot, _ = number(U_OUT, 2, it, j)
                    load(n, slot, w_out_v[:, :, bass.ds((2 * it + j) * P, P)])
            with sp.Fori(0, NMB) as it:
                for j in range(UT):
                    n, slot, _ = number(U_MLP, 2 * UT, it, j)
                    load(n, slot, w_up_v[:, :, bass.ds(it * MB + j * P, P)])
                for j in range(UT):
                    n, slot, _ = number(U_MLP, 2 * UT, it, UT + j)
                    load(n, slot, w_dn_v[:, bass.ds(it * UT, UT), 2 * P * j:2 * P * j + 2 * P], width=2 * P)

            for d in range(KD):
                sp.wait_ge(fin_copied, d + 1)
                sp.dma_start(yp_v[:, :, P * d:P * d + P], out_tok[d % 2][:, 0:NT, :]).then_inc(fin_stored[d % 2], 16)
                sp.dma_start(ys_v[:, P * d:P * d + P], out_tok[d % 2][0:TS, NT, :]).then_inc(fin_stored[d % 2], 16)
            for i in range(2):
                sp.wait_ge(fin_stored[i], 16 * KD)

        @block.gpsimd
        def _(pool):
            pool.memset(ident[:, :], 0.0)
            pool.memset(causal_neg[:, :], 0.0)
            pool.memset(ones[:, :], 1.0)
            pool.memset(chunk_mask[:, :], 1.0)
            pool.memset(chunk_mask_s[:, :], 1.0)
            pool.memset(batch_mask[:, :], 1.0)
            pool.memset(new_neg_room[:, :], NEG)
            pool.memset(not_after[:, :, :], 1.0)
            pool.memset(neg_pick[:, :, :], 0.0)
            pool.memset(neg_pick_s[:, :, :], 0.0)
            pool.memset(half[:, :], -0.5)
            pool.memset(zero[:, :], 0.0)
            pool.memset(d_parts[:, :], 0.0)
            pool.drain()
            pool.affine_select(out=ident[:, :], in_=ident[:, :], compare_op=ALU.not_equal, fill=1.0, base=0,
                               pattern=[[-1, P]], channel_multiplier=1)
            pool.affine_select(out=causal_neg[:, :], in_=causal_neg[:, :], compare_op=ALU.is_ge, fill=NEG, base=0,
                               pattern=[[-1, P]], channel_multiplier=1)

            def keep(ap, base, pattern, mul, fill):
                pool.affine_select(out=ap, in_=ap, compare_op=ALU.is_ge, fill=fill, base=base, pattern=pattern,
                                   channel_multiplier=mul)

            def chunks_only(ap, n, c):
                v = ap.rearrange("p (a b) -> p a b", b=c)
                keep(ap, 0, [[1, n]], -1, 0.0)
                pool.drain()
                keep(v, 0, [[-c, n // c], [0, c]], 1, 0.0)
                pool.drain()

            chunks_only(chunk_mask[:, :], P, HG_CHUNK)
            chunks_only(chunk_mask_s[:, :], TS, LS)
            keep(batch_mask[:, :], 0, [[-LS, NB]], 1, 0.0)
            pool.drain()
            keep(batch_mask[:, :], LS - 1, [[LS, NB]], -1, 0.0)
            for part in range(3):
                pool.affine_select(out=neg_pick[:, :, :], in_=neg_pick[:, :, :], compare_op=ALU.not_equal, fill=-1.0,
                                   base=-32 * part, pattern=[[-1, FH], [0, P]], channel_multiplier=1)
                pool.drain()
            pool.affine_select(out=neg_pick_s[:, :, :].rearrange("p b (h q) -> p (b h) q", q=LS),
                               in_=neg_pick_s[:, :, :].rearrange("p b (h q) -> p (b h) q", q=LS),
                               compare_op=ALU.not_equal, fill=-1.0, base=0, pattern=[[-1, NB * FH], [0, LS]],
                               channel_multiplier=1)
            keep(not_after[:, :, :], 0, [[0, FH], [1, LS]], -1, 0.0)
            pool.tensor_copy(ident_b[:, :], ident[:, :])
            pool.drain().then_inc(consts_ready, 1)

            pool.dma_start(pages[:, :], page_table.rearrange("(a b) g -> a (b g)", a=1)).then_inc(pages_landed, 16)
            pool.wait_ge(x_ms, 1)
            nc.gpsimd.tensor_tensor(stat[:, :], stat[:, :], half[:, :], ALU.pow).then_inc(x_rstd, 1)
            pool.wait_ge(pages_landed, 16)
            with pool.Fori(0, NB) as b:
                for g in range(NPG):
                    page = pool.value_load(pages[0:1, bass.ds(b * NPG + g, 1)], min_val=0, max_val=NPHYS - 1)
                    pool.dma_start(past_lf[:, g, bass.ds(b, 1), :].rearrange("p a h -> p (a h)"), cl_v[bass.ds(page, 1), :, :].rearrange("a p h -> p (a h)"))\
                        .then_inc(past_logf_landed, 16)
            phase_end(pool, "pool", 1)
            phase_end(pool, "pool", 2)

            pool.memset(scan_ones, 1.0).then_inc(ones_set, 1)
            pool.wait_ge(lf_ready, 1)
            for b in range(NB):
                pool.dma_start(d_past[FH * b:FH * b + FH, PAST:PAST + LS], lf_T[:, L + LS * b:L + LS * b + LS])\
                    .then_inc(lf_new_moved, 16)
            with pool.Fori(0, G // 2) as it:
                for gg in range(2):
                    g = 2 * it + gg
                    pool.wait_ge(acc_read, 6 * it + (U_FOX + 3 * gg + 3))
                    pool.tensor_copy(q_new[:, bass.ds(g, 1), :].rearrange("p a b -> p (a b)"), fqT[:, L:T])
                    pool.tensor_copy(k_new[:, bass.ds(g, 1), :].rearrange("p a b -> p (a b)"), fkT[:, L:T])
                    pool.drain().then_inc(new_stashed, 1)
                    pool.wait_ge(tok_copied, 6 * g + 6)
                    pool.dma_start(kp_v[:, :, bass.ds(g * P, P)], f_ktok).then_inc(kv_stored, 16)
                    pool.dma_start(vp_v[:, :, bass.ds(g * P, P)], f_vtok).then_inc(kv_stored, 16)
            pool.dma_start(k_sample[0].rearrange("b l h d -> (b l) (h d)"), k_new_tok[:, :]).then_inc(stored, 16)
            pool.dma_start(v_sample[0].rearrange("b l h d -> (b l) (h d)"), v_new[:, :]).then_inc(stored, 16)
            pool.wait_ge(kv_stored, 32 * G)
            pool.wait_ge(lf_out_copied, 1)
            pool.dma_start(logf_prompt[0, 0].rearrange("(t p) h -> p t h", p=P),
                           lf_out[:, 0:NT * FH].rearrange("p (t h) -> p t h", h=FH)).then_inc(stored, 16)
            pool.dma_start(logf_sample[0].rearrange("b l h -> (b l) h"), lf_out[0:TS, NT * FH:NT * FH + FH])\
                .then_inc(stored, 16)
            pool.wait_ge(stored, 64)
            phase_end(pool, "pool", 3)

            pool.memset(sQ_room, 0.0).then_inc(sq_zeroed, 1)

            phase_end(pool, "pool", 4)

            pool.memset(q_by_b_room, 0.0)
            pool.memset(reset[:, :], 1.0)
            pool.drain()
            pool.memset(reset[:, 0:L:HG_CHUNK], 0.0)
            pool.memset(reset[:, L:T:LS], 0.0)
            pool.memset(h_ms, 1.0)
            pool.memset(a_mask[0], 0.0)
            pool.memset(a_mask[1], 0.0)
            pool.memset(a_mask_s, 0.0)
            pool.drain().then_inc(hg_zeroed, 1)
            with pool.Fori(0, HH) as h:
                pool.dma_start(s_states, state_hgrn[0, :, bass.ds(h, 1), :, :].rearrange("b a k v -> k b (a v)"))\
                    .then_inc(s0_landed, 16)
                pool.wait_ge(hv_tr, h + 1)
                past_waits(pool, "pool")
                pool.memset(hV[:, 0:2 * CP * P], 0.0)
                pool.drain()
                pool.wait_ge(hv_copied, h + 1)
                for t in range(NT):
                    if t >= 2:
                        pool.wait_ge(ds_ready, NT * h + t - 1)
                    past_waits(pool, "pool")
                    for i in range(CP):
                        last = nc.gpsimd.tensor_copy(v_by_chunk[32 * i:32 * i + 32, t % 2, i, :],
                                                     h_vtok[32 * i:32 * i + 32, t, :])
                    pool.drain().then_inc(v_spread, 1)
                pool.wait_ge(hms_ready, h + 1)
                nc.gpsimd.tensor_tensor(h_ms, h_ms, half[:, :], ALU.pow).then_inc(hrstd, 1)
                pool.wait_ge(s_ready, NCH * h + NCH)
                past_waits(pool, "pool")
                pool.dma_start(s_prompt[0, 0, bass.ds(h, 1), :, :].rearrange("a k v -> k (a v)"), states[NCH % 8])\
                    .then_inc(state_stored, 16)
                pool.wait_ge(s_new_ready, h + 1)
                past_waits(pool, "pool")
                pool.dma_start(s_sample[0, :, bass.ds(h, 1), :, :].rearrange("b a k v -> k b (a v)"), s_states)\
                    .then_inc(state_stored, 16)
                pool.wait_ge(state_stored, 32 * h + 32)
            phase_end(pool, "pool", 5)

            def load_br(d, slot):
                v = br_raw[slot].rearrange("p (k n) -> p k n", n=P)
                pool.dma_start(v[:, 0:HH, :], w_bh_v[:, :, bass.ds(d * P, P)]).then_inc(br_landed[slot], 16)
                pool.dma_start(v[:, HH:HH + G, :], w_bf_v[:, :, bass.ds(d * P, P)]).then_inc(br_landed[slot], 16)

            load_br(0, 0)
            load_br(1, 1)
            for m in range(NM - NM1):
                if m:
                    pool.wait_ge(ada_used, NM1 // 4 + m)
                pool.dma_start(ada_raw.rearrange("p (k n) -> p k n", n=P),
                               ada_v[:, :, P * (NM1 + m):P * (NM1 + m) + P]).then_inc(ada_rest_landed, 16)
                if m % 4 == 3 and m // 4 < KD - 2:
                    pool.wait_ge(br_ready, 6 * (m // 4) + 6)
                    load_br(m // 4 + 2, m // 4 % 2)
            phase_end(pool, "pool", 6)

            for t in range(NT):
                pool.dma_start(xall[:, t, :], xp_v[:, t, :]).then_inc(x_again_landed, 16)
            pool.dma_start(xs_again, xs_v).then_inc(x_again_landed, 16)

            def rstd(k):
                pool.wait_ge(ms_ready, k)
                nc.gpsimd.tensor_tensor(stat[:, :], stat[:, :], half[:, :], ALU.pow).then_inc(rstd_ready, 1)

            rstd(1)
            for d in range(KD):
                pool.wait_ge(x1_ready, d + 1)
                pool.dma_start(x1_dram[:, d, :], yT[:, d, :]).then_inc(x1_stored, 16)
            rstd(2)
            pool.wait_ge(x1_stored, 16 * KD)
            phase_end(pool, "pool", 7)

            pool.memset(yT, 0.0)
            for i in range(2):
                pool.memset(down[i], 0.0).then_inc(down_free, 1)
            pool.drain()
            with pool.Fori(0, NMB) as it:
                for j in range(KD):
                    pool.wait_ge(down_copied, KD * it + j + 1)
                    nc.gpsimd.tensor_add(yT[:, j, :], yT[:, j, :], down[j % 2]).then_inc(down_free, 1)
            pool.drain()
            rstd(3)
            phase_end(pool, "pool", 8)

            def load_x1(d):
                pool.dma_start(x1b[d % 2], x1_dram[:, d, :]).then_inc(x1_back[d % 2], 16)

            load_x1(0)
            load_x1(1)
            for d in range(2, KD):
                pool.wait_ge(fin_ready, d - 1)
                load_x1(d)

        @block.scalar
        def _(act):
            copy, ACTIVATE = nc.scalar.copy, nc.scalar.activation

            def hi(base, per, it, j):
                n, slot, landed = number(base, per, it, j)
                split_hi(act, n, slot, landed)

            for t in range(NT):
                act.dma_start(xall[:, t, :], xp_v[:, t, :]).then_inc(x_landed, 16)
            act.dma_start(xs_tile, xs_v).then_inc(xs_landed, 16)
            act.wait_ge(vecs_tr, 1)
            ACTIVATE(vec[:, :], bank(6, 0, NV), ACT.Copy).then_inc(vecs_copied, 1)
            ACTIVATE(c_act[:, :], bank(7, 0, NC * KD), ACT.Silu).then_inc(c_ready, 1)
            act.wait_ge(x_landed, 16 * NT)
            act.wait_ge(xs_landed, 16)
            act.wait_ge(dve_consts_ready, 1)
            for t in range(NT):
                ACTIVATE(junk, xall[:, t, :], ACT.Square, accum_out=stat[:, t:t + 1])
                act.drain()
            ACTIVATE(junk[0:TS, :], xs_tile, ACT.Square, accum_out=stat[0:TS, NT:NT + 1])
            act.drain().then_inc(x_sumsq, 1)
            act.wait_ge(mod_done, 1)
            ACTIVATE(lb[:, :], lb_diff[:, :], ACT.Sigmoid)
            ACTIVATE(omlb[:, :], lb_diff[:, :], ACT.Sigmoid, scale=-1.0)
            phase_end(act, "act", 1)

            split_hi(act, 0, 0, 16)
            split_hi(act, 1, 1, 16)
            for i in range(2 * KD):
                d, half_no = i // 2, i % 2
                act.wait_ge(h_tr, i + 1)
                if i >= 2:
                    act.wait_ge(h_split, i - 1)
                ACTIVATE(h_tmp[i % 2], bank(i % 2), ACT.Identity, scale=pre1[:, d, 0:1], bias=mod[:, d, 0:1])
                act.drain()
                ACTIVATE(h_hi[:, d, 512 * half_no:512 * half_no + 512], h_tmp[i % 2], ACT.Copy).then_inc(h_raw, 1)
            phase_end(act, "act", 2)

            act.wait_ge(unit_done, 1)
            ACTIVATE(lf_T, acc(0)[0:FH, :], ACT.Identity, bias=fox_b[:, 0:1]).then_inc(acc_read, 1)
            act.drain()
            ACTIVATE(lf_a, lf_T, ACT.Abs)
            act.drain()
            ACTIVATE(lf_a, lf_a, ACT.Exp, scale=-1.0)
            act.drain()
            ACTIVATE(lf_a, lf_a, ACT.Ln, bias=1.0)
            act.drain().then_inc(lf_ln, 1)
            with act.Fori(0, G // 2) as it:
                for gg in range(2):
                    g = 2 * it + gg
                    for j, (dst, scale) in enumerate(((fkT, 1.0), (fvT, 1.0), (fqT, float(DH) ** -0.5))):
                        hi(U_FOX, 6, it, 3 * gg + j + 1)
                        n, slot, _ = number(U_FOX, 6, it, 3 * gg + j)
                        act.wait_ge(unit_done, n + 1)
                        ACTIVATE(dst, acc(slot), ACT.Copy, scale=scale).then_inc(acc_read, 1)
                    for a in range(17):
                        if a < 16:
                            n = P * (a % NT + 1)
                            act.wait_ge(max_ready, 16 * g + a + 1)
                            if a >= 2:
                                act.wait_ge(probs_tr, 16 * g + a - 1)
                            ACTIVATE(probs[a % 2][:, 0:n], bank(3 * (a % 2), 0, n), ACT.Exp,
                                     bias=nmax[:, a % 2:a % 2 + 1], accum_out=sums[:, a:a + 1])
                            act.drain().then_inc(probs_ready, 1)
                        e = a - 1
                        if e >= 0 and e % NT >= 4:
                            act.wait_ge(probs_tr, 16 * g + e + 1)
                            if e >= 2:
                                act.wait_ge(pv_done, 16 * g + e - 1)
                            ACTIVATE(probsT[e % 2][:, 4:e % NT + 1, :].rearrange("p a b -> p (a b)"),
                                     bank(5, 0, P * (e % NT - 3)), ACT.Copy).then_inc(pt_high, 1)
                    for i in range(2):
                        act.wait_ge(o_tr, 2 * g + i + 1)
                        ACTIVATE(mix[:, bass.ds(g, 1), 512 * i:512 * i + 512].rearrange("p a b -> p (a b)"),
                                 bank((2, 5)[i]), ACT.Copy).then_inc(o_copied, 1)
                    act.wait_ge(new_stashed, g + 1)
            act.wait_ge(lf_out_tr, 1)
            ACTIVATE(lf_out[:, 0:NT * FH], bank(6, 0, NT * FH), ACT.Copy)
            ACTIVATE(lf_out[0:TS, NT * FH:NT * FH + FH], bank(6, NT * FH, NT * FH + FH, rows=TS), ACT.Copy)
            act.drain().then_inc(lf_out_copied, 1)
            phase_end(act, "act", 3)

            def odd_keys(b):
                for i in range(4):
                    act.wait_ge(sk_tr, 8 * b + (2 * i + 2))
                    ACTIVATE(sKT[:, i, 512:1024], bank(5), ACT.Copy).then_inc(sk_copied_act, 1)

            def sample(b, last=False):
                act.wait_ge(smax_ready, b + 1)
                ACTIVATE(sP, psum[0:TS, 0:PAST + TS], ACT.Exp, bias=nmax[0:TS, 0:1], accum_out=sums[0:TS, 0:1])
                act.drain().then_inc(sexp_ready, 1)
                if not last:
                    odd_keys(b + 1)

            odd_keys(0)
            with act.Fori(0, NB - 1) as b:
                sample(b)
            sample(NB - 1, last=True)
            phase_end(act, "act", 4)

            with act.Fori(0, HH) as h:
                hi(U_HG, 4, h, 1)
                act.wait_ge(unit_done, 4 * h + (U_HG + 1))
                a0 = acc(U_HG % 2)
                ACTIVATE(hK, a0, ACT.Sigmoid, scale=-1.0)
                ACTIVATE(hF, a0, ACT.Sigmoid)
                act.drain().then_inc(acc_read, 1)
                hi(U_HG, 4, h, 2)
                act.wait_ge(unit_done, 4 * h + (U_HG + 2))
                ACTIVATE(hQ, acc((U_HG + 1) % 2), ACT.Copy, scale=float(DK) ** -0.5).then_inc(acc_read, 1)
                act.wait_ge(f_ready, h + 1)
                ACTIVATE(hF, hF, ACT.Ln).then_inc(g_ready, 1)
                hi(U_HG, 4, h, 3)
                act.wait_ge(unit_done, 4 * h + (U_HG + 3))
                ACTIVATE(hV, acc(U_HG % 2), ACT.Copy).then_inc(acc_read, 1)
                act.wait_ge(b_ready, h + 1)
                ACTIVATE(hE, hB, ACT.Exp)
                ACTIVATE(hN, hB, ACT.Exp, scale=-1.0)
                act.drain().then_inc(eb_ready, 1)
                hi(U_HG, 4, h, 4)
                act.wait_ge(unit_done, 4 * h + (U_HG + 4))
                ACTIVATE(hS, acc((U_HG + 1) % 2), ACT.Silu).then_inc(acc_read, 1)
                for t in range(NT + 1):
                    r = P if t < NT else TS
                    act.wait_ge(ho_ready, (NT + 1) * h + t + 1)
                    ACTIVATE(h_otok[0:r, t, :], bank(4 + t % 2, 0, P, rows=r), ACT.Copy).then_inc(ho_copied, 1)
                    act.drain()
                    ACTIVATE(hF[0:r, P * (t % 2):P * (t % 2) + P], h_otok[0:r, t, :],
                             ACT.Square, accum_out=h_ms[0:r, t:t + 1])
                act.drain().then_inc(hss_ready, 1)
            phase_end(act, "act", 5)

            with act.Fori(0, KD // 2) as it:
                for dd in range(2):
                    for j, dst in enumerate((gate_h, gate_f)):
                        hi(U_MG, 4, it, 2 * dd + j + 1)
                        n, slot, _ = number(U_MG, 4, it, 2 * dd + j)
                        act.wait_ge(unit_done, n + 1)
                        ACTIVATE(dst, acc(slot), ACT.Sigmoid).then_inc(acc_read, 1)
                    act.wait_ge(br_added, 2 * it + dd + 1)
            for d in range(KD):
                ACTIVATE(h_hi[:, d, :], merged[:, d, :], ACT.Copy).then_inc(h_raw, 1)
            phase_end(act, "act", 6)

            with act.Fori(0, KD // 2) as it:
                for j in range(2):
                    hi(U_OUT, 2, it, j + 1)
                    n, slot, _ = number(U_OUT, 2, it, j)
                    act.wait_ge(unit_done, n + 1)
                    ACTIVATE(yT[:, bass.ds(2 * it + j, 1), :].rearrange("p a b -> p (a b)"), acc(slot), ACT.Copy)
                    ACTIVATE(sq[j], acc(slot), ACT.Square)
                    act.drain().then_inc(acc_read, 1)

            def norm_rows(k):
                act.wait_ge(rb_ready, k)
                ACTIVATE(rb, psum[:, 0:T], ACT.Copy).then_inc(rb_copied, 1)

            norm_rows(1)
            for d in range(KD):
                act.wait_ge(x1_ready, d + 1)
                if d >= 2:
                    act.wait_ge(x1_summed, d - 1)
                ACTIVATE(sq[d % 2], yT[:, d, :], ACT.Square).then_inc(x1_sq, 1)
            norm_rows(2)
            for d in range(KD):
                act.wait_ge(h2_scaled, d + 1)
                ACTIVATE(h_hi[:, d, 0:L], t1[d % 2][:, 0:L], ACT.Identity, bias=mod[:, 3 * KD + d, 0:1])
                ACTIVATE(h_hi[:, d, L:T], t1[d % 2][:, L:T], ACT.Copy)
                act.drain().then_inc(h2_raw, 1)
            phase_end(act, "act", 7)

            def squares(d):
                act.wait_ge(down_free, KD * (NMB - 1) + d + 3)
                if d >= 2:
                    act.wait_ge(fin_summed, d - 1)
                ACTIVATE(relu[d % 2], yT[:, d, :], ACT.Square).then_inc(fin_sq, 1)

            def mlp_block(it, last=False):
                for j in range(UT):
                    hi(U_MLP, 2 * UT, it, j + 1)
                    n, slot, _ = number(U_MLP, 2 * UT, it, j)
                    act.wait_ge(unit_done, n + 1)
                    ACTIVATE(relu[j % 2], acc((U_MLP + j) % 2), ACT.Relu).then_inc(acc_read, 1)
                    act.drain().then_inc(relu_ready, 1)
                    ACTIVATE(u_hi[:, j, :], relu[j % 2], ACT.Square).then_inc(u_hi_ready, 1)
                for j in range(UT):
                    if not (last and j == UT - 1):
                        hi(U_MLP, 2 * UT, it, UT + j + 1)
                    n, slot, _ = number(U_MLP, 2 * UT, it, UT + j)
                    for i in range(2):
                        act.wait_ge(*((down_half, UT * it + j + 1), (unit_done, n + 1))[i])
                        act.wait_ge(down_free, KD * it + (2 * j + i + 1))
                        ACTIVATE(down[i], acc((U_MLP + i) % 2), ACT.Copy).then_inc(acc_read, 1)
                        act.drain().then_inc(down_copied, 1)
                    if last and j >= 1:
                        squares(2 * j - 2)
                        squares(2 * j - 1)
                if last:
                    squares(KD - 2)
                    squares(KD - 1)

            with act.Fori(0, NMB - 1) as it:
                mlp_block(it)
            mlp_block(NMB - 1, last=True)
            norm_rows(3)
            phase_end(act, "act", 8)
            for d in range(KD):
                act.wait_ge(fin_tr, d + 1)
                if d >= 2:
                    act.wait_ge(fin_stored[d % 2], 32 * (d // 2))
                ACTIVATE(out_tok[d % 2][:, 0:NT, :].rearrange("p a b -> p (a b)"), psum[:, 2048 * (d % 2):2048 * (d % 2) + L],
                         ACT.Copy)
                ACTIVATE(out_tok[d % 2][0:TS, NT, :], psum[0:TS, 2048 * (d % 2) + L:2048 * (d % 2) + L + P], ACT.Copy)
                act.drain().then_inc(fin_copied, 1)

        @block.vector
        def _(dve):
            v = nc.vector

            def lo(base, per, it, j):
                n, slot, _ = number(base, per, it, j)
                split_lo(dve, n, slot)

            v.memset(stat[:, :], 1.0)
            dve.drain().then_inc(dve_consts_ready, 1)
            dve.wait_ge(consts_ready, 1)
            dve.wait_ge(vecs_copied, 1)
            v.tensor_sub(lb_diff[:, :], vec[:, V_L0:V_L0 + HH], vec[:, V_L1:V_L1 + HH])
            dve.wait_ge(vecs_tr, 2)
            v.tensor_scalar(new_neg_own, bank(4, 0, LS, rows=TS).unsqueeze(1).broadcast_to([TS, NB, LS]), -NEG, NEG,
                            ALU.mult, ALU.add)
            dve.wait_ge(x_sumsq, 1)
            v.tensor_scalar(stat[:, :], stat[:, :], 1.0 / D, EPS, ALU.mult, ALU.add).then_inc(x_ms, 1)
            dve.wait_ge(x_rstd, 1)
            for t in range(NT):
                v.tensor_scalar(xall[:, t, :], xall[:, t, :], stat[:, t:t + 1], None, ALU.mult)
            v.tensor_scalar(xs_tile, xs_tile, stat[0:TS, NT:NT + 1], None, ALU.mult)
            dve.wait_ge(mod_ready, 1)
            v.tensor_tensor(mod[:, 0:NM1, :], bank(5, 0, NM1 * NC).rearrange("p (m c) -> p m c", c=NC),
                            vec[:, V_AB:V_AB + NM1].unsqueeze(2).broadcast_to([P, NM1, NC]), ALU.add)
            dve.drain()

            def times_norm(dst, row, weight, plus_one):
                w = vec[:, weight:weight + KD].unsqueeze(2).broadcast_to([P, KD, NC])
                v.scalar_tensor_tensor(dst[:, :, :], mod[:, row * KD:row * KD + KD, :], 1.0 if plus_one else 0.0, w,
                                       ALU.add, ALU.mult)

            times_norm(pre1, 1, V_N1, True)
            dve.drain().then_inc(mod_done, 1)
            phase_end(dve, "dve", 1)

            split_lo(dve, 0, 0)
            split_lo(dve, 1, 1)
            for i in range(2 * KD):
                d, c = i // 2, 512 * (i % 2)
                dve.wait_ge(h_raw, i + 1)
                v.tensor_sub(h_lo[:, d, c:c + 512], h_tmp[i % 2], h_hi[:, d, c:c + 512].bitcast(F32))\
                    .then_inc(h_split, 1)
            hs_tmp = junk[:, 0:KD * TS].rearrange("p (d b l) -> p d b l", b=NB, l=LS)
            dve.wait_ge(h_tr, 2 * KD + 1)
            v.tensor_tensor(hs_tmp, bank(2).rearrange("p (d b l) -> p d b l", b=NB, l=LS),
                            pre1[:, :, 1:NC].unsqueeze(3).broadcast_to([P, KD, NB, LS]), ALU.mult)
            dve.drain()
            v.tensor_tensor(hs_tmp, hs_tmp, mod[:, 0:KD, 1:NC].unsqueeze(3).broadcast_to([P, KD, NB, LS]), ALU.add)
            dve.drain()
            flat = junk[:, 0:KD * TS].rearrange("p (d t) -> p d t", t=TS)
            v.tensor_copy(h_hi[:, :, L:T], flat)
            dve.drain()
            v.tensor_sub(h_lo[:, :, L:T], flat, h_hi[:, :, L:T].bitcast(F32))
            phase_end(dve, "dve", 2)

            dve.wait_ge(lf_ln, 1)
            dve.wait_ge(ones_set, 1)
            v.tensor_scalar(lf_m, lf_T, 0.0, None, ALU.min)
            dve.drain()
            v.tensor_sub(lf_T, lf_m, lf_a)
            dve.drain().then_inc(lf_ready, 1)
            v.tensor_tensor_scan(lf_d, scan_ones[0:FH, :], lf_T[:, 0:L], 0.0, ALU.mult, ALU.add)
            dve.drain()
            for part in range(3):
                v.tensor_copy(lf_b, lf_d)
                dve.drain()
                v.tensor_sub(lf_d, lf_d, lf_b)
                v.tensor_copy(d_parts[32 * part:32 * part + FH, :], lf_b)
                dve.drain()
            dve.drain().then_inc(d_ready, 1)

            with dve.Fori(0, G // 2) as it:
                for gg in range(2):
                    g = 2 * it + gg
                    for j in range(3):
                        lo(U_FOX, 6, it, 3 * gg + j + 1)
                    for i, (src, dst) in enumerate((
                            (bank(2), f_vtok[:, 0:4, :].rearrange("p a b -> p (a b)")),
                            (bank(5), f_vtok[:, 4:8, :].rearrange("p a b -> p (a b)")),
                            (bank(6, 0, P, rows=TS), v_new[:, bass.ds(g * P, P)]),
                            (bank(7), f_ktok[:, 0:4, :].rearrange("p a b -> p (a b)")),
                            (bank(6, P, 2 * P, rows=TS), k_new_tok[:, bass.ds(g * P, P)]),
                            (bank(2), f_ktok[:, 4:8, :].rearrange("p a b -> p (a b)")))):
                        dve.wait_ge(tok_tr, 6 * g + i + 1)
                        v.tensor_copy(dst, src).then_inc(tok_copied, 1)
                    for a in range(18):
                        if a < 16:
                            n = P * (a % NT + 1)
                            dve.wait_ge(scores_ready, 16 * g + a + 1)
                            v.tensor_reduce(nmax[:, a % 2:a % 2 + 1], bank(3 * (a % 2), 0, n), axis=AX, op=ALU.max,
                                            negate=True).then_inc(max_ready, 1)
                        e = a - 1
                        if 0 <= e < 16:
                            dve.wait_ge(probs_tr, 16 * g + e + 1)
                            if e >= 2:
                                dve.wait_ge(pv_done, 16 * g + e - 1)
                            m = min(e % NT + 1, 4)
                            v.tensor_copy(probsT[e % 2][:, 0:m, :].rearrange("p a b -> p (a b)"),
                                          bank(2, 0, P * m)).then_inc(pt_low, 1)
                        o = a - 2
                        if o >= 0:
                            dve.wait_ge(pv_done, 16 * g + o + 1)
                            v.reciprocal(rinv[:, o % 2:o % 2 + 1], sums[:, o:o + 1])
                            dve.drain()
                            c = DH * (o // NT)
                            v.tensor_scalar(f_otok[:, o % NT, c:c + DH], bank(6 + o % 2, 0, DH),
                                            rinv[:, o % 2:o % 2 + 1], None, ALU.mult).then_inc(o_ready, 1)
                    dve.wait_ge(kv_stored, 32 * g + 32)
            dve.wait_ge(lf_tr, 1)
            v.tensor_tensor_scan(d_past[:, 0:PAST], scan_ones, psum[0:TS, 1536:1536 + PAST], 0.0, ALU.mult,
                                 ALU.add)
            dve.drain()
            dve.wait_ge(lf_new_moved, 16 * NB)
            v.tensor_tensor_scan(d_past[:, PAST:PAST + LS], scan_ones[:, 0:LS], d_past[:, PAST:PAST + LS],
                                 d_past[:, PAST - 1:PAST], ALU.mult, ALU.add)
            phase_end(dve, "dve", 3)

            dve.wait_ge(sq_zeroed, 1)
            def queries(b):
                for i in range(2):
                    v.tensor_copy(sQ_own[64 * i:64 * i + 64, :, LS * i:LS * i + LS],
                                  q_new[64 * i:64 * i + 64, :, bass.ds(b * LS, LS)])
                v.tensor_copy(sPick, neg_pick_s[:, bass.ds(b, 1), :].rearrange("p a c -> p (a c)"))
                v.tensor_copy(sNeg, new_neg[:, bass.ds(b, 1), :].rearrange("p a k -> p (a k)"))
                dve.drain().then_inc(sq_ready, 1)

            def even_keys(b):
                for i in range(4):
                    dve.wait_ge(sk_tr, 8 * b + (2 * i + 1))
                    v.tensor_copy(sKT[:, i, 0:512], bank(4)).then_inc(sk_copied_dve, 1)

            def sample(b, last=False):
                dve.wait_ge(ss_ready, b + 1)
                v.tensor_reduce(nmax[0:TS, 0:1], psum[0:TS, 0:PAST + TS], axis=AX, op=ALU.max, negate=True)\
                    .then_inc(smax_ready, 1)
                if not last:
                    queries(b + 1)
                    even_keys(b + 1)
                dve.wait_ge(sexp_ready, b + 1)
                v.reciprocal(rinv[0:TS, 0:1], sums[0:TS, 0:1])
                dve.drain()
                v.tensor_scalar(sP, sP, rinv[0:TS, 0:1], None, ALU.mult).then_inc(sp_ready, 1)
                dve.wait_ge(sp_tr, b + 1)
                v.tensor_copy(sPT[:, 0:NPG, :].rearrange("p a b -> p (a b)"), bank(3))
                v.tensor_copy(sPT[0:TS, NPG, :], bank(6, 0, TS, rows=TS)).then_inc(spt_ready, 1)
                dve.wait_ge(spv_done, b + 1)
                for i in range(2):
                    copied = v.tensor_copy(
                        mix[64 * i:64 * i + 64, 0:G, bass.ds(b * LS + L, LS)],
                        bank(7, 0, 16 * G)[64 * i:64 * i + 64, :].rearrange("p (g c) -> p g c", c=16)
                        [:, :, LS * i:LS * i + LS])
                copied.then_inc(so_copied, 1)

            queries(0)
            even_keys(0)
            with dve.Fori(0, NB - 1) as b:
                sample(b)
            sample(NB - 1, last=True)
            phase_end(dve, "dve", 4)

            def chunk_ends(ap, c):
                e = ap.rearrange("p (n c) -> p n c", c=c)[:, :, c - 1:c]
                return e.broadcast_to([P, ap.shape[1] // c, c])

            dve.wait_ge(hg_zeroed, 1)
            with dve.Fori(0, HH) as h:
                lo(U_HG, 4, h, 1)
                dve.wait_ge(acc_read, 4 * h + (U_HG + 1))
                om, lbh = omlb[:, bass.ds(h, 1)], lb[:, bass.ds(h, 1)]
                v.tensor_tensor(hK, hK, om.broadcast_to([P, T]), ALU.mult)
                v.tensor_tensor(hF, hF, om.broadcast_to([P, T]), ALU.mult)
                dve.drain()
                v.tensor_tensor(hF, hF, lbh.broadcast_to([P, T]), ALU.add).then_inc(f_ready, 1)
                lo(U_HG, 4, h, 2)
                dve.wait_ge(g_ready, h + 1)
                v.tensor_tensor_scan(hB, reset[:, :], hF, 0.0, ALU.mult, ALU.add).then_inc(b_ready, 1)
                lo(U_HG, 4, h, 3)
                dve.wait_ge(eb_ready, h + 1)
                v.tensor_mul(hQ, hQ, hE)
                v.tensor_mul(hN, hK, hN)
                dve.drain().then_inc(hg_ops, 1)
                v.tensor_copy(q_by_b_own, by_batch(hQ[:, L:T]))
                v.tensor_tensor(hK[:, 0:L].rearrange("p (n c) -> p n c", c=HG_CHUNK),
                                hN[:, 0:L].rearrange("p (n c) -> p n c", c=HG_CHUNK),
                                chunk_ends(hE[:, 0:L], HG_CHUNK), ALU.mult)
                v.tensor_tensor(by_batch(hK[:, L:T]), by_batch(hN[:, L:T]), chunk_ends(hE[:, L:T], LS), ALU.mult)
                v.memset(states[0], 0.0)
                dve.drain().then_inc(hg_ops, 1)
                lo(U_HG, 4, h, 4)
                for i, (src, dst) in enumerate((
                        (psum[:, 0:L], h_vtok[:, 0:NT, :].rearrange("p a b -> p (a b)")),
                        (bank(2, 0, P, rows=TS), h_vtok[0:TS, NT, :]))):
                    dve.wait_ge(hv_tr, h + 1)
                    v.tensor_copy(dst, src)
                dve.drain().then_inc(hv_copied, 1)
                dve.wait_ge(hkd_tr, h + 1)
                v.tensor_copy(h_kdtok[:, 0:NT, :].rearrange("p a b -> p (a b)"), psum[:, 1536:1536 + L])
                v.tensor_copy(h_kdtok[0:TS, NT, :], bank(5, 0, P, rows=TS))
                dve.drain().then_inc(hkd_copied, 1)
                v.tensor_tensor(kd_by_b, h_kdtok[0:TS, NT, :].unsqueeze(1).broadcast_to([TS, NB, DK]),
                                batch_mask[:, :].unsqueeze(2).broadcast_to([TS, NB, DK]), ALU.mult)
                dve.drain().then_inc(masked_ready, 1)
                for t in range(NT):
                    dve.wait_ge(a_ready, (NT + 1) * h + t + 1)
                    if t >= 2:
                        dve.wait_ge(ho_ready, (NT + 1) * h + t - 1)
                    past_waits(dve, "dve")
                    v.copy_predicated(a_mask[t % 2], chunk_mask[:, :].bitcast(I32), bank(2 + t % 2, 0, P))\
                        .then_inc(a_masked, 1)
                    dve.wait_ge(ds_ready, NT * h + t + 1)
                    for i in range(CP):
                        c = CP * t + i
                        if c + 1 >= 8 and (c + 1) % CP == 0:
                            dve.wait_ge(ho_ready, (NT + 1) * h + (c - 7) // CP + 1)
                        end = HG_CHUNK * (c + 1) - 1
                        v.scalar_tensor_tensor(states[(c + 1) % 8], states[c % 8], hE[:, end:end + 1],
                                               bank(t % 2, P * i, P * i + P), ALU.mult, ALU.add)\
                            .then_inc(s_ready, 1)
                        dve.wait_ge(s_ready, NCH * h + c + 1)
                dve.wait_ge(a_ready, (NT + 1) * h + NT + 1)
                past_waits(dve, "dve")
                v.copy_predicated(a_mask_s, chunk_mask_s[:, :].bitcast(I32), bank(2, 0, TS, rows=TS))\
                    .then_inc(a_masked, 1)
                dve.wait_ge(sds_ready, h + 1)
                dve.wait_ge(ho_ready, (NT + 1) * h + NT + 1)
                for b in range(NB):
                    end = L + LS * (b + 1) - 1
                    v.scalar_tensor_tensor(s_states[:, b, :], s_states[:, b, :], hE[:, end:end + 1],
                                           psum[:, P * b:P * b + P], ALU.mult, ALU.add)
                dve.drain().then_inc(s_new_ready, 1)
                dve.wait_ge(hss_ready, h + 1)
                v.tensor_scalar(h_ms, h_ms, 1.0 / DV, EPS, ALU.mult, ALU.add).then_inc(hms_ready, 1)
                dve.wait_ge(hrstd, h + 1)
                v.tensor_tensor(h_otok[:, 0:NT, :], h_otok[:, 0:NT, :],
                                h_ms[:, 0:NT].unsqueeze(2).broadcast_to([P, NT, DV]), ALU.mult)
                v.tensor_scalar(h_otok[0:TS, NT, :], h_otok[0:TS, NT, :], h_ms[0:TS, NT:NT + 1], None, ALU.mult)
                dve.drain().then_inc(hn_ready, 1)
                dve.wait_ge(ho_tr, h + 1)
                v.scalar_tensor_tensor(mix[:, bass.ds(h + G, 1), :].rearrange("p a b -> p (a b)"), psum[:, 0:T],
                                       vec[:, V_ON:V_ON + 1], hS, ALU.mult, ALU.mult).then_inc(ho_mixed, 1)
                dve.wait_ge(state_stored, 32 * h + 32)
            phase_end(dve, "dve", 5)

            with dve.Fori(0, KD // 2) as it:
                for dd in range(2):
                    d = 2 * it + dd
                    def ada_tile(m):
                        dve.wait_ge(ada_used, 8 * it + (NM1 // 4 + 4 * dd + m + 1))
                        at = 8 * it + (NM1 + 4 * dd + m)
                        v.tensor_tensor(mod[:, bass.ds(at, 1), :].rearrange("p a c -> p (a c)"),
                                        bank((6, 7, 7, 7)[m], 0, NC), vec[:, bass.ds(at, 1)].broadcast_to([P, NC]),
                                        ALU.add).then_inc(ada_rest_read, 1)

                    def branch(first):
                        for i in range(first, first + 3):
                            a, b = PIECES[i % 3]
                            dve.wait_ge(br_ready, 6 * d + i + 1)
                            v.tensor_mul(dst[:, a:b] if i < 3 else br_tmp[:, a:b], bank(BR_BANK[i], 0, b - a),
                                         (gate_h if i < 3 else gate_f)[:, a:b]).then_inc(br_read, 1)

                    lo(U_MG, 4, it, 2 * dd + 1)
                    ada_tile(0)
                    lo(U_MG, 4, it, 2 * dd + 2)
                    ada_tile(1)
                    dve.wait_ge(acc_read, 4 * it + (U_MG + 2 * dd + 2))
                    dst = merged[:, bass.ds(d, 1), :].rearrange("p a b -> p (a b)")
                    branch(0)
                    ada_tile(2)
                    branch(3)
                    ada_tile(3)
                    dve.drain()
                    v.tensor_add(dst, dst, br_tmp)
                    dve.drain().then_inc(br_added, 1)
            for d in range(KD):
                dve.wait_ge(h_raw, 2 * KD + d + 1)
                v.tensor_sub(h_lo[:, d, :], merged[:, d, :], h_hi[:, d, :].bitcast(F32)).then_inc(merged_split, 1)
            phase_end(dve, "dve", 6)

            times_norm(post1, 2, V_P1, False)
            times_norm(pre2, 4, V_N2, True)
            times_norm(post2, 5, V_P2, False)
            dve.drain()

            def mean_square(k):
                b = SUM_BANK[k]
                dve.wait_ge(ss_tr, k)
                v.tensor_scalar(stat[:, 0:NT], bank(b, 0, NT), 1.0 / D, EPS, ALU.mult, ALU.add)
                v.tensor_scalar(stat[0:TS, NT:NT + 1], bank(b, NT, NT + 1, rows=TS), 1.0 / D, EPS, ALU.mult, ALU.add)
                dve.drain().then_inc(ms_ready, 1)

            def scaled(dst, y, m, d):
                v.scalar_tensor_tensor(dst[:, 0:L], y[:, 0:L], m[:, d, 0:1], rb[:, 0:L], ALU.mult, ALU.mult)
                v.tensor_mul(dst[:, L:T], y[:, L:T], rb[:, L:T])
                dve.drain()
                v.tensor_tensor(by_batch(dst[:, L:T]), by_batch(dst[:, L:T]), per_batch(m, d), ALU.mult)
                dve.drain()

            with dve.Fori(0, KD // 2) as it:
                for j in range(2):
                    lo(U_OUT, 2, it, j + 1)
            mean_square(1)
            dve.wait_ge(rb_copied, 1)
            for d in range(KD):
                scaled(t1[0], yT[:, d, :], post1, d)
                dve.wait_ge(xT_ready, d + 1)
                v.tensor_add(yT[:, d, :], t1[0], psum[:, 1536 * (d % 2):1536 * (d % 2) + T])
                dve.drain().then_inc(x1_ready, 1)
            mean_square(2)
            dve.wait_ge(rb_copied, 2)
            for d in range(KD + 1):
                if d < KD:
                    t = t1[d % 2]
                    scaled(t, yT[:, d, :], pre2, d)
                    v.tensor_tensor(by_batch(t[:, L:T]), by_batch(t[:, L:T]), per_batch(mod[:, 3 * KD:4 * KD, :], d),
                                    ALU.add)
                    dve.drain().then_inc(h2_scaled, 1)
                if d >= 1:
                    e, t = d - 1, t1[(d - 1) % 2]
                    dve.wait_ge(h2_raw, d)
                    v.scalar_tensor_tensor(h_lo[:, e, 0:L], t[:, 0:L], mod[:, 3 * KD + e, 0:1],
                                           h_hi[:, e, 0:L].bitcast(F32), ALU.add, ALU.subtract)
                    v.tensor_sub(h_lo[:, e, L:T], t[:, L:T], h_hi[:, e, L:T].bitcast(F32))
                    dve.drain().then_inc(h2_split, 1)
            phase_end(dve, "dve", 7)

            def mlp_block(it, last=False):
                for j in range(UT):
                    lo(U_MLP, 2 * UT, it, j + 1)
                    dve.wait_ge(relu_ready, UT * it + j + 1)
                    v.tensor_mul(usq, relu[j % 2], relu[j % 2])
                    dve.drain()
                    dve.wait_ge(u_hi_ready, UT * it + j + 1)
                    v.tensor_sub(u_lo[:, j, :], usq, u_hi[:, j, :].bitcast(F32))
                    dve.drain().then_inc(u_lo_ready, 1)
                for j in range(UT):
                    if not (last and j == UT - 1):
                        lo(U_MLP, 2 * UT, it, UT + j + 1)

            with dve.Fori(0, NMB - 1) as it:
                mlp_block(it)
            mlp_block(NMB - 1, last=True)
            mean_square(3)
            phase_end(dve, "dve", 8)
            dve.wait_ge(rb_copied, 3)
            for d in range(KD):
                scaled(yT[:, d, :], yT[:, d, :], post2, d)
                dve.wait_ge(x1_back[d % 2], 16 * (d // 2) + 16)
                v.tensor_add(yT[:, d, :], yT[:, d, :], x1b[d % 2])
                dve.drain().then_inc(fin_ready, 1)

        @block.tensor
        def _(pe):
            mm, tr = nc.tensor.matmul, nc.tensor.transpose

            pe.wait_ge(consts_ready, 1)
            pe.wait_ge(vecs_landed, 16 * 10)
            tr(bank(6, 0, NV), vec_rows[:, :], ident[0:NV, 0:NV])
            tr(bank(7, 0, NC * KD), c_rows[:, :], ident[0:NC * KD, 0:NC * KD]).then_inc(vecs_tr, 1)
            tr(bank(4, 0, LS, rows=TS), not_after[:, :, :].rearrange("p h q -> p (h q)"), ident[0:LS, 0:LS])\
                .then_inc(vecs_tr, 1)
            pe.wait_ge(c_ready, 1)
            c_cols = c_act[:, :].rearrange("p (c k) -> p k c", k=KD)
            for i in range(NM1 // 4):
                pe.wait_ge(ada_landed[i % 3], 16 * (i // 3) + 16)
                w = ada_ring[i % 3].rearrange("p (k n) -> p k n", n=512)
                for m in range(4):
                    for k in range(KD):
                        last = mm(bank(5, (4 * i + m) * NC, (4 * i + m) * NC + NC), w[:, k, P * m:P * m + P],
                                  c_cols[:, k, :], start=(k == 0), stop=(k == KD - 1))
                last.then_inc(ada_used, 1)
            pe.drain().then_inc(mod_ready, 1)
            phase_end(pe, "pe", 1)

            for d in range(KD):
                last = tr(bank(2, TS * d, TS * d + TS), xs_tile[:, P * d:P * d + P], ident[0:TS, 0:TS])
            for i in range(2 * KD):
                if i >= 2:
                    pe.wait_ge(h_raw, i - 1)
                for t in range(4):
                    tile = 4 * (i % 2) + t
                    last = tr(bank(i % 2, P * t, P * t + P), xall[:, tile, P * (i // 2):P * (i // 2) + P], ident[:, :])
                last.then_inc(h_tr, 1)
            pe.drain().then_inc(h_tr, 1)
            phase_end(pe, "pe", 2)

            project(pe, U_FF, 0)
            with pe.Fori(0, G // 2) as it:
                for gg in range(2):
                    g = 2 * it + gg
                    for j in range(3):
                        n, slot, _ = number(U_FOX, 6, it, 3 * gg + j)
                        project(pe, n, slot, acc_free=(j == 0))
                    pe.wait_ge(acc_read, 6 * it + (U_FOX + 3 * gg + 3))

                    def four(src, dst, first):
                        for t in range(4):
                            last = tr(bank(dst, P * t, P * t + P), src[:, P * (first + t):P * (first + t) + P],
                                      ident[:, :])
                        last.then_inc(tok_tr, 1)

                    four(fvT, 2, 0)
                    four(fvT, 5, 4)
                    tr(bank(6, 0, P, rows=TS), fvT[:, L:T], ident[:, :]).then_inc(tok_tr, 1)
                    four(fkT, 7, 0)
                    pe.wait_ge(tok_copied, 6 * g + 3)
                    past_waits(pe, "pe")
                    tr(bank(6, P, 2 * P, rows=TS), fkT[:, L:T], ident[:, :]).then_inc(tok_tr, 1)
                    four(fkT, 2, 4)
                    pe.wait_ge(tok_copied, 6 * g + 6)
                    pe.wait_ge(d_ready, 1)
                    for a in range(18):
                        if a < 16:
                            j, i = a // NT, a % NT
                            n = P * (i + 1)
                            rows = slice(64 * j, 64 * j + 64)
                            if a >= 2:
                                pe.wait_ge(probs_ready, 16 * g + a - 1)
                            base = 1536 * (a % 2)
                            for c in range(0, n, 512):
                                e = min(c + 512, n)
                                mm(psum[:, base + c:base + e], fqT[rows, P * i:P * i + P], fkT[rows, c:e], start=True,
                                   stop=False)
                                if e == n:
                                    mm(psum[:, base + n - P:base + n], ident_b[:, :], causal_neg[:, :], start=False,
                                       stop=False)
                                last = mm(psum[:, base + c:base + e],
                                          neg_pick[0:96, bass.ds(2 * g + j, 1), :].rearrange("p a b -> p (a b)"),
                                          d_parts[:, c:e], start=False, stop=True)
                            last.then_inc(scores_ready, 1)
                        e = a - 1
                        if 0 <= e < 16:
                            pe.wait_ge(probs_ready, 16 * g + e + 1)
                            if e >= 1:
                                pe.wait_ge(pt_low, 16 * g + e)
                            if e >= 5 and (e - 1) // NT >= 0:
                                done = (e // NT) * 4 + max(0, e % NT - 4)
                                if done:
                                    pe.wait_ge(pt_high, 8 * g + done)
                            for kb in range(e % NT + 1):
                                last = tr(bank(2 if kb < 4 else 5, P * (kb % 4), P * (kb % 4) + P),
                                          probs[e % 2][:, P * kb:P * kb + P], ident[:, :])
                            last.then_inc(probs_tr, 1)
                        o = a - 2
                        if o >= 0:
                            pe.wait_ge(pt_low, 16 * g + o + 1)
                            if o % NT >= 4:
                                pe.wait_ge(pt_high, 8 * g + (o // NT) * 4 + o % NT - 3)
                            if o >= 2:
                                pe.wait_ge(o_ready, 16 * g + o - 1)
                            for kb in range(o % NT + 1):
                                last = mm(bank(6 + o % 2, 0, DH), probsT[o % 2][:, kb, :],
                                          f_vtok[:, kb, DH * (o // NT):DH * (o // NT) + DH], start=(kb == 0),
                                          stop=(kb == o % NT))
                            last.then_inc(pv_done, 1)
                    pe.wait_ge(o_ready, 16 * g + 16)
                    for i in range(2):
                        for t in range(4):
                            last = tr(bank((2, 5)[i], P * t, P * t + P), f_otok[:, 4 * i + t, :], ident[:, :])
                        last.then_inc(o_tr, 1)
                    pe.wait_ge(o_copied, 2 * g + 2)
            pe.wait_ge(past_logf_landed, 16 * NB * NPG)
            for g in range(NPG):
                tr(psum[0:TS, 1536 + P * g:1536 + P * g + P],
                   past_lf[:, g, :, :].rearrange("p b h -> p (b h)"), ident[:, :])
            pe.drain().then_inc(lf_tr, 1)
            pe.wait_ge(lf_ready, 1)
            for t in range(NT + 1):
                r = P if t < NT else TS
                last = tr(bank(6, FH * t, FH * t + FH, rows=r), lf_T[:, P * t:P * t + r], ident[0:FH, 0:FH])
            last.then_inc(lf_out_tr, 1)
            phase_end(pe, "pe", 3)

            def keys(b):
                pe.wait_ge(sk_landed, 16 * NPG * b + 16 * NPG)
                for i in range(8):
                    if i >= 2:
                        pe.wait_ge(*((sk_copied_dve, 4 * b + i // 2), (sk_copied_act, 4 * b + i // 2))[i % 2])
                    for t in range(4):
                        last = tr(bank(4 + i % 2, P * t, P * t + P),
                                  sK[:, 4 * (i % 2) + t, P * (i // 2):P * (i // 2) + P], ident[:, :])
                    last.then_inc(sk_tr, 1)

            def sample(b, last_one=False):
                pe.wait_ge(sk_copied_dve, 4 * b + 4)
                pe.wait_ge(sk_copied_act, 4 * b + 4)
                pe.wait_ge(sq_ready, b + 1)
                new = psum[0:TS, PAST:PAST + TS]
                for c in range(2):
                    for g in range(G):
                        mm(bank(c, rows=TS), sQ[:, g, :], sKT[:, g, 512 * c:512 * c + 512], start=(g == 0), stop=False)
                    mm(bank(c, rows=TS), sPick, d_past[:, 512 * c:512 * c + 512], start=False, stop=True)
                for g in range(G):
                    mm(new, sQ[:, g, :], k_new[:, g, :], start=(g == 0), stop=False)
                mm(new, ident_b[0:TS, 0:TS], sNeg, start=False, stop=False)
                mm(new, sPick, d_past[:, PAST:PAST + LS].unsqueeze(1).broadcast_to([TS, NB, LS]), start=False,
                   stop=True).then_inc(ss_ready, 1)
                if not last_one:
                    keys(b + 1)
                pe.wait_ge(sp_ready, b + 1)
                past_waits(pe, "pe")
                for t in range(NPG):
                    tr(bank(3, TS * t, TS * t + TS), sP[:, P * t:P * t + P], ident[0:TS, 0:TS])
                tr(bank(6, 0, TS, rows=TS), sP[:, PAST:PAST + TS], ident[0:TS, 0:TS]).then_inc(sp_tr, 1)
                pe.wait_ge(spt_ready, b + 1)
                pe.wait_ge(sv_landed, 16 * NPG * b + 16 * NPG)
                for g in range(G):
                    out = bank(7, 16 * g, 16 * g + 16)
                    for t in range(NPG):
                        mm(out, sV[:, t, P * g:P * g + P], sPT[:, t, 16 * g:16 * g + 16], start=(t == 0), stop=False)
                    last = mm(out, v_new[:, P * g:P * g + P], sPT[0:TS, NPG, 16 * g:16 * g + 16], start=False,
                              stop=True)
                last.then_inc(spv_done, 1)
                pe.wait_ge(so_copied, b + 1)

            keys(0)
            with pe.Fori(0, NB - 1) as b:
                sample(b)
            sample(NB - 1, last_one=True)
            phase_end(pe, "pe", 4)

            pe.wait_ge(hg_zeroed, 1)
            with pe.Fori(0, HH) as h:
                for j in range(4):
                    n, slot, _ = number(U_HG, 4, h, j)
                    project(pe, n, slot)
                pe.wait_ge(acc_read, 4 * h + (U_HG + 4))
                for t in range(NT):
                    tr(psum[:, P * t:P * t + P], hV[:, P * t:P * t + P], ident[:, :])
                tr(bank(2, 0, P, rows=TS), hV[:, L:T], ident[:, :]).then_inc(hv_tr, 1)
                pe.wait_ge(hg_ops, 2 * h + 2)
                for t in range(NT):
                    tr(psum[:, 1536 + P * t:1536 + P * t + P], hK[:, P * t:P * t + P], ident[:, :])
                tr(bank(5, 0, P, rows=TS), hK[:, L:T], ident[:, :]).then_inc(hkd_tr, 1)
                pe.wait_ge(hv_copied, h + 1)
                pe.wait_ge(hkd_copied, h + 1)
                for t in range(NT + 1):
                    if t < NT:
                        cols = slice(P * t, P * t + P)
                        if t >= 2:
                            pe.wait_ge(a_masked, (NT + 1) * h + t - 1)
                        mm(bank(2 + t % 2, 0, P), hN[:, cols], hQ[:, cols], start=True, stop=True).then_inc(a_ready, 1)
                        if t >= 2:
                            pe.wait_ge(s_ready, NCH * h + CP * (t - 1))
                        pe.wait_ge(v_spread, NT * h + t + 1)
                        mm(bank(t % 2), h_kdtok[:, t, :], v_by_chunk[:, t % 2, :, :].rearrange("p c v -> p (c v)"),
                           start=True, stop=True).then_inc(ds_ready, 1)
                    e = t - 1
                    if e >= 0:
                        pe.wait_ge(a_masked, (NT + 1) * h + e + 1)
                        if e >= 1:
                            pe.wait_ge(s_ready, NCH * h + CP * e + CP - 1)
                        else:
                            pe.wait_ge(s_ready, NCH * h + CP - 1)
                        if e >= 2:
                            pe.wait_ge(ho_copied, (NT + 1) * h + e - 1)
                        mm(bank(4 + e % 2, 0, P), a_mask[e % 2], h_vtok[:, e, :], start=True, stop=False)
                        for i in range(CP):
                            last = mm(bank(4 + e % 2, 0, P)[32 * i:32 * i + 32, :],
                                      hQ[:, P * e + 32 * i:P * e + 32 * i + 32], states[(CP * e + i) % 8], start=False,
                                      stop=True)
                        last.then_inc(ho_ready, 1)
                mm(bank(2, 0, TS, rows=TS), hN[:, L:T], hQ[:, L:T], start=True, stop=True).then_inc(a_ready, 1)
                pe.wait_ge(masked_ready, h + 1)
                pe.wait_ge(s_ready, NCH * h + NCH)
                for b in range(NB):
                    last = mm(psum[:, P * b:P * b + P], kd_by_b[:, b, :], h_vtok[0:TS, NT, :], start=True, stop=True)
                last.then_inc(sds_ready, 1)
                pe.wait_ge(a_masked, (NT + 1) * h + NT + 1)
                pe.wait_ge(s0_landed, 16 * h + 16)
                pe.wait_ge(ho_copied, (NT + 1) * h + NT - 1)
                past_waits(pe, "pe")
                mm(bank(4, 0, P, rows=TS), a_mask_s, h_vtok[0:TS, NT, :], start=True, stop=False)
                for b in range(NB):
                    last = mm(bank(4, 0, P, rows=TS), q_by_b[:, b, :], s_states[:, b, :], start=False,
                              stop=(b == NB - 1))
                last.then_inc(ho_ready, 1)
                pe.wait_ge(hn_ready, h + 1)
                for t in range(NT):
                    tr(psum[:, P * t:P * t + P], h_otok[:, t, :], ident[:, :])
                tr(bank(2, 0, TS), h_otok[0:TS, NT, :], ident[0:TS, 0:TS]).then_inc(ho_tr, 1)
                pe.wait_ge(ho_mixed, h + 1)
            phase_end(pe, "pe", 5)

            with pe.Fori(0, KD // 2) as it:
                for dd in range(2):
                    d = 2 * it + dd
                    def ada_tile(m, gate_after):
                        pe.wait_ge(ada_rest_landed, 64 * d + (16 * m + 16))
                        pe.wait_ge(*gate_after)
                        w = ada_raw.rearrange("p (k n) -> p k n", n=P)
                        for k in range(KD):
                            last = mm(bank((6, 7, 7, 7)[m], 0, NC), w[:, k, :], c_cols[:, k, :], start=(k == 0),
                                      stop=(k == KD - 1))
                        last.then_inc(ada_used, 1)

                    def branch(first):
                        for i in range(first, first + 3):
                            a, b = PIECES[i % 3]
                            if i in (0, 1):
                                pe.wait_ge(ada_rest_read, 4 * d + i + 1)
                            elif i == 4:
                                pe.wait_ge(ada_rest_read, 4 * d + 3)
                            else:
                                pe.wait_ge(br_read, 6 * d + {2: 1, 3: 3, 5: 4}[i])
                            for k in range(4):
                                kw = k if i < 3 else HH + k
                                km = G + k if i < 3 else k
                                last = mm(bank(BR_BANK[i], 0, b - a), w_br[:, kw, :], mix[:, km, a:b], start=(k == 0),
                                          stop=(k == 3))
                            last.then_inc(br_ready, 1)

                    w_br = br_raw[dd].rearrange("p (k n) -> p k n", n=P)
                    n, slot, _ = number(U_MG, 4, it, 2 * dd)
                    project(pe, n, slot)
                    ada_tile(0, (consts_ready, 1))
                    n, slot, _ = number(U_MG, 4, it, 2 * dd + 1)
                    project(pe, n, slot)
                    ada_tile(1, (consts_ready, 1))
                    pe.wait_ge(br_landed[dd], 32 * it + 32)
                    branch(0)
                    ada_tile(2, (br_read, 6 * d + 2))
                    branch(3)
                    ada_tile(3, (br_read, 6 * d + 5))
                    pe.wait_ge(ada_rest_read, 4 * d + 4)
                    pe.wait_ge(br_read, 6 * d + 6)
            phase_end(pe, "pe", 6, wait=False)

            def clear_sums(k):
                mm(bank(SUM_BANK[k], 0, NT + 1), ident[:, :], zero[:, :], start=True, stop=False,
                   skip_group_check=True)

            def add_sums(k, squares, ready, count, done=None):
                pe.wait_ge(ready, count)
                for t in range(NT + 1):
                    r = P if t < NT else TS
                    last = mm(bank(SUM_BANK[k], t, t + 1, rows=r), squares[:, P * t:P * t + r], ones[:, 0:1],
                              start=False, stop=True, skip_group_check=True)
                if done is not None:
                    last.then_inc(done, 1)
                return last

            def norm_rows(k, last_sum):
                last_sum.then_inc(ss_tr, 1)
                pe.wait_ge(rstd_ready, k)
                for t in range(NT + 1):
                    r = P if t < NT else TS
                    last = mm(psum[:, P * t:P * t + r], stat[0:r, t:t + 1].broadcast_to([r, P]), ident[0:r, 0:r],
                              start=True, stop=True)
                last.then_inc(rb_ready, 1)

            clear_sums(1)
            n, slot, _ = number(U_OUT, 0, 0, 0)
            project(pe, n, slot, parts_ready=(merged_split, 0))
            with pe.Fori(0, KD // 2 - 1) as it:
                for j in range(2):
                    n, slot, _ = number(U_OUT, 2, it, j + 1)
                    project(pe, n, slot)
                    add_sums(1, sq[j], acc_read, n)
            n, slot, _ = number(U_OUT, 0, 0, KD - 1)
            project(pe, n, slot)
            add_sums(1, sq[(KD - 2) % 2], acc_read, n)
            for e in ("act", "dve", "pool"):
                pe.wait_ge(done_of[e], 6)
            norm_rows(1, add_sums(1, sq[(KD - 1) % 2], acc_read, n + 1))
            pe.wait_ge(rb_copied, 1)
            pe.wait_ge(x_again_landed, 16 * (NT + 1))
            for d in range(KD):
                if d >= 2:
                    pe.wait_ge(x1_ready, d - 1)
                base = 1536 * (d % 2)
                for t in range(NT):
                    tr(psum[:, base + P * t:base + P * t + P], xall[:, t, P * d:P * d + P], ident[:, :])
                tr(psum[:, base + L:base + T], xs_again[:, P * d:P * d + P], ident[0:TS, 0:TS]).then_inc(xT_ready, 1)
                if d == 0:
                    clear_sums(2)
                else:
                    add_sums(2, sq[(d - 1) % 2], x1_sq, d, x1_summed)
            pe.wait_ge(x1_ready, KD)
            norm_rows(2, add_sums(2, sq[(KD - 1) % 2], x1_sq, KD))
            pe.wait_ge(rb_copied, 2)
            phase_end(pe, "pe", 7, wait=False)

            def mlp_block(it, last=False):
                for j in range(UT):
                    n, slot, _ = number(U_MLP, 2 * UT, it, j)
                    project(pe, n, slot, acc_no=3 * UT * it + (U_MLP + j), acc_slot=(U_MLP + j) % 2,
                            parts_ready=(h2_split, 0) if j == 0 else None)
                if last:
                    clear_sums(3)
                for j in range(UT):
                    n, slot, _ = number(U_MLP, 2 * UT, it, UT + j)
                    pe.wait_ge(w_hi_ready, n + 1)
                    pe.wait_ge(w_lo_ready, n + 1)
                    for i in range(2):
                        pe.wait_ge(acc_read, 3 * UT * it + (U_MLP + UT + 2 * j + i - 1))
                        out = acc((U_MLP + i) % 2)
                        for k in range(UT):
                            if j == 0 and i == 0:
                                pe.wait_ge(u_hi_ready, UT * it + k + 1)
                                pe.wait_ge(u_lo_ready, UT * it + k + 1)
                            at = 2 * P * k + P * i
                            wh, wl = (w[:, slot, at:at + P] for w in (w_hi, w_lo))
                            for w, m in ((wh, u_hi), (wh, u_lo), (wl, u_hi)):
                                for a, b in PIECES:
                                    product = mm(out[:, a:b], w, m[:, k, a:b],
                                                 start=(k == 0 and w is wh and m is u_hi),
                                                 stop=(k == UT - 1 and w is wl))
                        product.then_inc((down_half, unit_done)[i], 1)
                    if last and j >= 2:
                        for d in (2 * j - 4, 2 * j - 3):
                            add_sums(3, relu[d % 2], fin_sq, d + 1, fin_summed)

            with pe.Fori(0, NMB - 1) as it:
                mlp_block(it)
            mlp_block(NMB - 1, last=True)
            for d in range(KD - 4, KD - 1):
                add_sums(3, relu[d % 2], fin_sq, d + 1, fin_summed)
            norm_rows(3, add_sums(3, relu[(KD - 1) % 2], fin_sq, KD))
            phase_end(pe, "pe", 8)
            pe.wait_ge(rb_copied, 3)
            for d in range(KD):
                pe.wait_ge(fin_ready, d + 1)
                if d >= 2:
                    pe.wait_ge(fin_copied, d - 1)
                base = 2048 * (d % 2)
                for t in range(NT):
                    tr(psum[:, base + P * t:base + P * t + P], yT[:, d, P * t:P * t + P], ident[:, :])
                tr(psum[0:TS, base + L:base + L + P], yT[:, d, L:T], ident[:, :]).then_inc(fin_tr, 1)


_INS = ['x_prompt', 'x_sample', 'c_prompt', 'c_sample', 'cache_k', 'cache_v', 'cache_logf', 'state_hgrn', 'page_table',
        'ada_w', 'ada_b', 'norm_mix_pre', 'norm_mix_post', 'norm_mlp_pre', 'norm_mlp_post', 'w_in',
        'hgrn_lower_bounds', 'hgrn_onorm', 'fox_b_f', 'w_br_h', 'w_br_f', 'w_out', 'w_mlp_up', 'w_mlp_down']


def kernel(**inputs):
    import numpy as _np
    import concourse.bacc as _bacc
    from concourse import mybir as _mybir
    from concourse.bass_utils import run_bass_kernel_spmd as _run

    xp, xs, ck, st = (inputs[n].shape for n in ('x_prompt', 'x_sample', 'cache_k', 'state_hgrn'))
    heads = (ck[3], ck[4])
    outs = [xp, xs, (1, 1, xp[1]) + heads, (1, 1, xp[1]) + heads, (1, 1, xp[1], ck[3]), (1, 1) + tuple(st[2:]),
            (1, xs[0], xs[1]) + heads, (1, xs[0], xs[1]) + heads, (1, xs[0], xs[1], ck[3]), tuple(st)]
    nc = _bacc.Bacc("TRN2", target_bir_lowering=False, num_devices=1)
    arrays, args = {}, []
    for name in _INS:
        a = _np.ascontiguousarray(inputs[name])
        arrays[f"in_{name}"] = a
        args.append(nc.dram_tensor(f"in_{name}", a.shape, _mybir.dt.from_np(a.dtype), kind="ExternalInput").ap())
    for i, shape in enumerate(outs):
        args.append(nc.dram_tensor(f"out_{i}", tuple(shape), F32, kind="ExternalOutput").ap())
    build_layer(nc, *args)
    r = _run(nc, [arrays], core_ids=[0])
    return tuple(r.results[0][f"out_{i}"] for i in range(len(outs)))
```

```python
from contextlib import ExitStack

import concourse.bass as bass
from concourse import mybir

F32 = mybir.dt.float32
F32R = mybir.dt.float32r
BF16 = mybir.dt.bfloat16
I32 = mybir.dt.int32
ALU = mybir.AluOpType
ACT = mybir.ActivationFunctionType
AX = mybir.AxisListType.X

P = 128
NEG = -1e30
EPS = 1e-6
HG_CHUNK = 32


def build_layer(nc, x_prompt, x_sample, c_prompt, c_sample, cache_k, cache_v, cache_logf, state_hgrn, page_table,
                ada_w, ada_b, norm_mix_pre, norm_mix_post, norm_mlp_pre, norm_mlp_post, w_in, hgrn_lower_bounds,
                hgrn_onorm, fox_b_f, w_br_h, w_br_f, w_out, w_mlp_up, w_mlp_down,
                y_prompt, y_sample, k_prompt, v_prompt, logf_prompt, s_prompt, k_sample, v_sample, logf_sample,
                s_sample):
    _, L, D = x_prompt.shape
    NB, LS, _ = x_sample.shape
    TS = NB * LS
    T = L + TS
    KD = D // P
    NT = L // P
    _, NPHYS, PAGE, FH, DH = cache_k.shape
    NPG = page_table.shape[1]
    PAST = NPG * PAGE
    HH, DK, DV = state_hgrn.shape[2:]
    HW, FW = HH * DK, FH * DH
    FF = w_mlp_up.shape[2]
    NM = ada_w.shape[2] // P
    NC = 1 + NB
    G = FW // P
    CP = P // HG_CHUNK
    NCH = L // HG_CHUNK
    NM1 = 2 * KD
    MB = 512
    NMB = FF // MB
    UT = MB // P
    assert (L, D, TS, PAGE, DK, DV, DH, KD, G, HH) == (1024, 1024, 64, P, P, P, 64, 8, 4, 4)
    O_HQ, O_HF, O_HI, O_HG = 0, HW, 2 * HW, 3 * HW
    O_FQ, O_FK, O_FV = 4 * HW, 4 * HW + FW, 4 * HW + 2 * FW
    O_FF = O_FV + FW
    O_MG = O_FF + FH
    V_AB, V_N1, V_P1, V_N2, V_P2 = 0, NM, NM + KD, NM + 2 * KD, NM + 3 * KD
    V_ON, V_L0 = NM + 4 * KD, NM + 4 * KD + 1
    V_L1 = V_L0 + HH
    NV = V_L1 + HH
    U_FF, U_FOX, U_HG = 0, 1, 1 + 3 * G
    U_MG = U_HG + 4 * HH
    U_OUT = U_MG + 2 * KD
    U_MLP = U_OUT + KD

    w_in_v = w_in[0].rearrange("(k p) n -> p k n", p=P)
    w_out_v = w_out[0].rearrange("(k p) n -> p k n", p=P)
    w_up_v = w_mlp_up[0].rearrange("(k p) n -> p k n", p=P)
    w_dn_v = w_mlp_down[0].rearrange("(k p) n -> p k n", p=P)
    w_bh_v = w_br_h[0].rearrange("(k p) n -> p k n", p=P)
    w_bf_v = w_br_f[0].rearrange("(k p) n -> p k n", p=P)
    ada_v = ada_w[0].rearrange("(k p) n -> p k n", p=P)
    kp_v = k_prompt[0, 0].rearrange("(t p) h d -> p t (h d)", p=P)
    vp_v = v_prompt[0, 0].rearrange("(t p) h d -> p t (h d)", p=P)
    yp_v = y_prompt[0].rearrange("(t p) n -> p t n", p=P)
    ys_v = y_sample.rearrange("b l n -> (b l) n")
    xp_v = x_prompt[0].rearrange("(t p) n -> p t n", p=P)
    xs_v = x_sample.rearrange("b l n -> (b l) n")
    ck_v = cache_k[0].rearrange("g p h d -> g p (h d)")
    cv_v = cache_v[0].rearrange("g p h d -> g p (h d)")
    cl_v = cache_logf[0]
    x1_dram = nc.dram_tensor("x1_scratch", [P, KD, T], F32, kind="Internal").ap()

    with ExitStack() as ctx:
        def sb(name, shape, dt=F32):
            return ctx.enter_context(nc.sbuf_tensor(name, shape, dt))

        def sem(name):
            return ctx.enter_context(nc.semaphore(name))

        h_hi, h_lo = sb("h_hi", [P, KD, T], F32R), sb("h_lo", [P, KD, T], F32R)
        w_raw = sb("w_raw", [P, 2, 1024])
        w_hi, w_lo = sb("w_hi", [P, 2, 1024], F32R), sb("w_lo", [P, 2, 1024], F32R)
        ident = sb("ident", [P, P])
        ident_b = sb("ident_b", [P, P], BF16)
        ones = sb("ones", [P, 1])
        causal_neg = sb("causal_neg", [P, P], BF16)
        chunk_mask = sb("chunk_mask", [P, P])
        chunk_mask_s = sb("chunk_mask_s", [TS, TS])
        chunk_pick = sb("chunk_pick", [P, CP])
        batch_mask = sb("batch_mask", [TS, NB])
        new_neg_room = sb("new_neg", [TS, NB * (TS + LS)], BF16)
        new_neg = new_neg_room[:, 0:NB * TS].rearrange("p (b k) -> p b k", k=TS)
        new_neg_own = new_neg_room[:, :].rearrange("p (b k) -> p b k", k=TS + LS)[:, :, 0:LS]
        not_after = sb("not_after", [LS, FH, LS])
        neg_pick = sb("neg_pick", [P, FH, P], BF16)
        neg_pick_s = sb("neg_pick_s", [TS, NB, TS])
        reset = sb("reset", [P, T])
        d_past = reset[0:TS, 0:PAST + LS]
        vec = sb("vec", [P, NV])
        c_act = sb("c_act", [P, NC * KD])
        mod = sb("mod", [P, NM, NC])
        pre1, post1 = sb("pre1", [P, KD, NC]), sb("post1", [P, KD, NC])
        pre2, post2 = sb("pre2", [P, KD, NC]), sb("post2", [P, KD, NC])
        lb, omlb = sb("lb", [P, HH]), sb("omlb", [P, HH])
        lb_diff = sb("lb_diff", [P, HH])
        fox_b = sb("fox_b", [FH, 1])
        stat = sb("stat", [P, NT + 1])
        half = sb("half", [P, NT + 1])
        d_parts = sb("d_parts", [96, L], BF16)
        q_new, k_new = sb("q_new", [P, G, TS]), sb("k_new", [P, G, TS])
        new_tok = sb("new_tok", [2 * TS, FW])
        v_new, k_new_tok = new_tok[0:TS, :], new_tok[TS:2 * TS, :]
        nmax, sums, rinv = sb("nmax", [P, 2]), sb("sums", [P, 16]), sb("rinv", [P, 2])
        pages = sb("pages", [1, NB * NPG], I32)

        with nc.sbuf_tensor("mix", [P, G + HH, T], F32) as mix:
            pass
        u_hi, u_lo = sb("u_hi", [P, UT, T], F32R), sb("u_lo", [P, UT, T], F32R)
        WORK = 15360
        work = sb("work", [P, WORK])

        def cut(at, *shape, rows=P):
            n = 1
            for s in shape:
                n *= s
            assert at + n <= WORK
            v = work[0:rows, at:at + n]
            if len(shape) == 2:
                v = v.rearrange("p (a b) -> p a b", b=shape[1])
            if len(shape) == 3:
                v = v.rearrange("p (a b c) -> p a b c", b=shape[1], c=shape[2])
            return v

        psum = ctx.enter_context(nc.psum_tensor("psum", [P, 8 * 512], F32))

        def bank(i, a=0, b=512, rows=P):
            return psum[0:rows, 512 * i + a:512 * i + b]

        SIDE = (T - 512) // 2
        PIECES = [(0, SIDE), (SIDE, SIDE + 512), (SIDE + 512, T)]

        def acc(slot):
            return psum[:, 1536 * slot + 512 - SIDE:1536 * slot + 512 - SIDE + T]

        raw_landed = [sem("raw_landed0"), sem("raw_landed1")]
        w_hi_ready, w_lo_ready = sem("w_hi_ready"), sem("w_lo_ready")
        unit_done, acc_read = sem("unit_done"), sem("acc_read")
        done_of = {e: sem(f"phase_done_{e}") for e in ("pe", "act", "dve", "pool")}
        vecs_landed, pages_landed, past_logf_landed, x_landed, xs_landed = map(
            sem, ("vecs_landed", "pages_landed", "past_logf_landed", "x_landed", "xs_landed"))
        consts_ready, dve_consts_ready = sem("consts_ready"), sem("dve_consts_ready")
        ada_landed = [sem(f"ada_landed{i}") for i in range(3)]
        mod_rows_copied, sq_free, states_free, qk_split, hs_tr = map(
            sem, ("mod_rows_copied", "sq_free", "states_free", "qk_split", "hs_tr"))
        ada_used, vecs_tr, vecs_copied, c_ready, mod_ready, mod_done = map(
            sem, ("ada_used", "vecs_tr", "vecs_copied", "c_ready", "mod_ready", "mod_done"))
        x_sumsq, x_ms, x_rstd, x_scaled, h_tr, h_raw, h_split = map(
            sem, ("x_sumsq", "x_ms", "x_rstd", "x_scaled", "h_tr", "h_raw", "h_split"))
        lf_tr, lf_exp, lf_abs, lf_ln, lf_min, lf_ready, lf_out_tr, lf_out_copied, lf_new_moved, d_ready = map(
            sem, ("lf_tr", "lf_exp", "lf_abs", "lf_ln", "lf_min", "lf_ready", "lf_out_tr", "lf_out_copied",
                  "lf_new_moved", "d_ready"))
        tok_tr, tok_copied, new_stashed, kv_stored = map(sem, ("tok_tr", "tok_copied", "new_stashed", "kv_stored"))
        scores_ready, max_ready, probs_ready, probs_tr, pt_low, pt_high, pv_done, o_ready, o_tr, o_copied = map(
            sem, ("scores_ready", "max_ready", "probs_ready", "probs_tr", "pt_low", "pt_high", "pv_done", "o_ready",
                  "o_tr", "o_copied"))
        sk_landed, sv_landed, sq_ready, sk_tr, sk_copied_dve, sk_copied_act, ss_ready, smax_ready, sexp_ready = map(
            sem, ("sk_landed", "sv_landed", "sq_ready", "sk_tr", "sk_copied_dve", "sk_copied_act", "ss_ready",
                  "smax_ready", "sexp_ready"))
        sp_tr, spt_ready, spv_done, so_copied, so_tr = map(
            sem, ("sp_tr", "spt_ready", "spv_done", "so_copied", "so_tr"))
        sig_ready, f_ready, g_ready, b_ready, eb_ready, hg_ops, hv_tr, hv_copied, hkd_tr, hkd_copied = map(
            sem, ("sig_ready", "f_ready", "g_ready", "b_ready", "eb_ready", "hg_ops", "hv_tr", "hv_copied", "hkd_tr",
                  "hkd_copied"))
        a_ready, a_masked, ds_ready, s_ready, ho_ready, ho_copied, hss_ready, hms_ready, hrstd, hn_ready = map(
            sem, ("a_ready", "a_masked", "ds_ready", "s_ready", "ho_ready", "ho_copied", "hss_ready", "hms_ready",
                  "hrstd", "hn_ready"))
        ho_tr, ho_mixed, s0_landed, state_stored, sds_ready, s_new_ready, masked_ready = map(
            sem, ("ho_tr", "ho_mixed", "s0_landed", "state_stored", "sds_ready", "s_new_ready", "masked_ready"))
        br_landed = [sem("br_landed0"), sem("br_landed1")]
        br_ready, br_read, br_added, ada_rest_landed, ada_rest_ready, ada_rest_read = map(
            sem, ("br_ready", "br_read", "br_added", "ada_rest_landed", "ada_rest_ready", "ada_rest_read"))
        y_sq, ss_tr, ms_ready, rstd_ready, rb_ready, rb_copied, x1_ready, x1_stored, xT_ready = map(
            sem, ("y_sq", "ss_tr", "ms_ready", "rstd_ready", "rb_ready", "rb_copied", "x1_ready", "x1_stored",
                  "xT_ready"))
        h2_scaled, h2_raw, h2_split, sq_zeroed, hg_zeroed, down_half, ones_set, v_spread = map(
            sem, ("h2_scaled", "h2_raw", "h2_split", "sq_zeroed", "hg_zeroed", "down_half", "ones_set", "v_spread"))
        relu_ready, u_hi_ready, u_lo_ready, down_copied, down_free = map(
            sem, ("relu_ready", "u_hi_ready", "u_lo_ready", "down_copied", "down_free"))
        fin_ready, fin_tr, fin_copied, stored = map(sem, ("fin_ready", "fin_tr", "fin_copied", "stored"))
        x1_back = sem("x1_back")
        fin_stored = [sem("fin_stored0"), sem("fin_stored1")]
        x1_sq, fin_sq, merged_split, x_again_landed = map(
            sem, ("x1_sq", "fin_sq", "merged_split", "x_again_landed"))

        order = ("pe", "act", "dve", "pool")
        passed = {e: sem(f"waits_passed_{e}") for e in order + ("sp",)}

        def past_waits(eng, me):
            eng.sem_inc(passed[me], 1)

        def phase_end(eng, me, k, wait=True):
            eng.drain().then_inc(done_of[me], 1)
            if not wait:
                return
            for o in order:
                if o != me:
                    eng.wait_ge(done_of[o], k)

        def split_hi(act, n, slot, landed):
            act.wait_ge(raw_landed[slot], landed)
            if not (isinstance(n, int) and n < 2):
                act.wait_ge(unit_done, n - 1)
            nc.scalar.activation(w_hi[:, slot, :], w_raw[:, slot, :], ACT.Copy).then_inc(w_hi_ready, 1)

        def split_lo(dve, n, slot):
            dve.wait_ge(w_hi_ready, n + 1)
            nc.vector.tensor_sub(w_lo[:, slot, :], w_raw[:, slot, :], w_hi[:, slot, :].bitcast(F32))\
                .then_inc(w_lo_ready, 1)

        def number(base, per, it, j):
            return base + j + per * it, (base + j) % 2, 16 * ((base + j) // 2 + 1) + 16 * (per // 2) * it

        def channel_tile(slot, acc_slot, k):
            out = acc(acc_slot)
            wh, wl = (w[:, slot, P * k:P * k + P] for w in (w_hi, w_lo))
            for w, m in ((wh, h_hi), (wh, h_lo), (wl, h_hi)):
                for a, b in PIECES:
                    last = nc.tensor.matmul(out[:, a:b], w, m[:, k, a:b], start=(k == 0 and w is wh and m is h_hi),
                                            stop=(k == KD - 1 and w is wl))
            return last

        def project(pe, n, slot, acc_no=None, acc_slot=None, acc_free=False, parts_ready=None):
            acc_no, acc_slot = (n, slot) if acc_no is None else (acc_no, acc_slot)
            pe.wait_ge(w_lo_ready, n + 1)
            pe.wait_ge(w_hi_ready, n + 1)
            if not (acc_free or (isinstance(n, int) and n < 2)):
                pe.wait_ge(acc_read, acc_no - 1)
            for k in range(KD):
                if parts_ready:
                    sem_of, before = parts_ready
                    pe.wait_ge(sem_of, before + k + 1)
                last = channel_tile(slot, acc_slot, k)
            last.then_inc(unit_done, 1)

        ada_ring = [cut(4096 * i, 4096) for i in range(3)]
        xs_tile = cut(12288, 1024, rows=TS)
        h_tmp = [cut(13312, 512), cut(13824, 512)]
        junk = cut(14336, 1024)
        mod_rows = [reset[0:NC, 512 * i:512 * i + 512] for i in range(2)]
        vec_rows, c_rows = cut(13312, P, rows=NV), cut(13312 + P, P, rows=NC * KD)
        xall = mix[:, :, :].rearrange("p a b -> p (a b)")[:, 0:NT * 1024].rearrange("p (t n) -> p t n", n=1024)
        past_lf = reset[:, 0:NPG * NB * FH].rearrange("p (g b h) -> p g b h", b=NB, h=FH)
        lf = 3 * T + 7168
        lf_T, lf_a, lf_m = (cut(lf + T * i, T, rows=FH) for i in range(3))
        lf_d = lf_m[:, 0:L]
        lf_b = cut(lf + 3 * T, L // 2, rows=FH).bitcast(BF16)
        lf_out = cut(lf + 3 * T + L // 2, 128)
        scan_ones = cut(lf + 3 * T + L // 2 + 128, L, rows=TS)
        fkT, fvT, fqT = cut(0, T), cut(T, T), cut(2 * T, T)
        k_parts, q_hi, q_lo = [u_lo[:, 0, :], u_lo[:, 1, :]], [u_lo[:, 2, :], u_lo[:, 3, :]], u_hi[:, G - 1, :]
        fat = 3 * T
        f_vtok, f_ktok = cut(fat, NT, P), cut(fat + 1024, NT, P)
        probs = [cut(fat + 2048, 1024), cut(fat + 3072, 1024)]
        probsT = [cut(fat + 4096, NT, P), cut(fat + 5120, NT, P)]
        f_otok = cut(fat + 6144, NT, P)
        d_two, pick = u_lo[:, 0, 0:PAST + LS], u_lo[:, 1, 0:TS]
        sK, sKT, sV = cut(0, NPG, FW), cut(4096, G, PAST), cut(8192, NPG, FW)
        sP = cut(12288, PAST + TS, rows=TS)
        sPT = cut(13376, NPG + 1, TS)
        sQ_room = cut(13376 + 576, G * (TS + 2 * LS))
        sQ = sQ_room[:, 0:G * TS].rearrange("p (g c) -> p g c", c=TS)
        sQ_own = sQ_room.rearrange("p (g c) -> p g c", c=TS + 2 * LS)
        sNeg = cut(13376 + 960, TS // 2, rows=TS).bitcast(BF16)
        sO = cut(13376 + 992, FW, rows=TS)
        hK, hF, hE, hN, hQ, hV, hS = (cut(T * i, T) for i in range(7))
        hg_at = 7 * T
        hB = cut(hg_at, T)
        v_by_chunk = hV[:, 0:2 * CP * P].rearrange("p (i c v) -> p i c v", c=CP, v=P)
        h_otok = cut(hg_at, NT + 1, P)
        h_vtok, h_kdtok = cut(hg_at + 1152, NT + 1, P), cut(hg_at + 2304, NT + 1, P)
        ring = hg_at + 3456
        states = [cut(ring + P * i, P) for i in range(8)]
        a_mask = [cut(ring + 1024, P), cut(ring + 1152, P)]
        a_mask_s = cut(ring + 1280, TS, rows=TS)
        s_states = cut(ring + 1344, NB, DV)
        kd_by_b = cut(ring + 2368, NB, DK, rows=TS)
        q_by_b_room = cut(ring + 3392, NB * (TS + LS))
        q_by_b = q_by_b_room[:, 0:NB * TS].rearrange("p (b t) -> p b t", t=TS)
        q_by_b_own = q_by_b_room.rearrange("p (b t) -> p b t", t=TS + LS)[:, :, 0:LS]
        h_ms = cut(ring + 3392 + 576, NT + 1)
        merged = cut(0, KD, T)
        br_raw = [cut(KD * T, 1024), cut(KD * T + 1024, 1024)]
        ada_raw = cut(KD * T + 2048 + 3 * T, 1024)
        gate_h, gate_f, br_tmp = (cut(KD * T + 2048 + T * i, T) for i in range(3))
        yT = cut(0, KD, T)
        rb = cut(KD * T, T)
        sq = [cut(KD * T + T, T), cut(KD * T + 2 * T, T)]
        t1 = [cut(KD * T + 3 * T, T), cut(KD * T + 4 * T, T)]
        xs_again = cut(KD * T + 5 * T, 1024, rows=TS)
        relu = [cut(KD * T, T), cut(KD * T + T, T)]
        usq = cut(KD * T + 2 * T, T)
        down = [cut(KD * T + 3 * T, T), cut(KD * T + 4 * T, T)]
        x1_all = h_hi[:, :, :].bitcast(F32)
        out_tok = [cut(KD * T + 5 * T, NT + 1, P), cut(KD * T + T, NT + 1, P)]

        BR_BANK = (6, 7, 6, 6, 7, 6)
        ssq = {1: t1[1], 2: t1[1], 3: cut(KD * T + 5 * T, T)}

        def by_batch(ap):
            return ap.rearrange("p (b l) -> p b l", l=LS)

        def per_batch(v, d):
            return v[:, d, 1:NC].unsqueeze(2).broadcast_to([P, NB, LS])

        block = ctx.enter_context(nc.Block())

        @block.sync
        def _(sp):
            def rows(at, n, src):
                sp.dma_start(vec_rows[at:at + n, :], src).then_inc(vecs_landed, 16)

            rows(V_AB, NM, ada_b[0].rearrange("(k p) -> k p", p=P))
            rows(V_N1, KD, norm_mix_pre[0].rearrange("(k p) -> k p", p=P))
            rows(V_P1, KD, norm_mix_post[0].rearrange("(k p) -> k p", p=P))
            rows(V_N2, KD, norm_mlp_pre[0].rearrange("(k p) -> k p", p=P))
            rows(V_P2, KD, norm_mlp_post[0].rearrange("(k p) -> k p", p=P))
            rows(V_ON, 1, hgrn_onorm)
            rows(V_L0, 2 * HH, hgrn_lower_bounds[0:2].rearrange("r (h p) -> (r h) p", p=P))
            sp.dma_start(c_rows[0:KD, :], c_prompt[0].rearrange("(k p) -> k p", p=P)).then_inc(vecs_landed, 16)
            sp.dma_start(c_rows[KD:NC * KD, :], c_sample.rearrange("b (k p) -> (b k) p", p=P))\
                .then_inc(vecs_landed, 16)
            sp.dma_start(fox_b[:, :], fox_b_f.rearrange("a h -> h a")).then_inc(vecs_landed, 16)
            for i in range(3):
                sp.dma_start(ada_ring[i].rearrange("p (k n) -> p k n", n=512), ada_v[:, :, 512 * i:512 * i + 512])\
                    .then_inc(ada_landed[i], 16)
            sp.wait_ge(ada_used, 1)
            sp.dma_start(ada_ring[0].rearrange("p (k n) -> p k n", n=512), ada_v[:, :, 3 * 512:4 * 512])\
                .then_inc(ada_landed[0], 16)

            def load(n, slot, src, width=P):
                if not (isinstance(n, int) and n < 2):
                    sp.wait_ge(w_lo_ready, n - 1)
                    if not isinstance(n, int):
                        past_waits(sp, "sp")
                sp.dma_start(w_raw[:, slot, :].rearrange("p (k n) -> p k n", n=width), src)\
                    .then_inc(raw_landed[slot], 16)

            load(U_FF, 0, w_in_v[:, :, O_FF:O_FF + P])
            for g in range(G):
                for j, off in enumerate((O_FK, O_FQ, O_FV)):
                    n, slot, _ = number(U_FOX, 0, 0, 3 * g + j)
                    load(n, slot, w_in_v[:, :, off + P * g:off + P * g + P])
            def load_heads(first, last):
                for i in range(first, last):
                    h, off = i // 4, (O_HF, O_HQ, O_HI, O_HG)[i % 4]
                    load(U_HG + i, (U_HG + i) % 2, w_in_v[:, :, off + P * h:off + P * h + P])

            def load_pages(page, dst, src, landed):
                for g in range(NPG):
                    sp.dma_start(dst[:, g, :], src[bass.ds(page[g], 1), :, :].rearrange("a p n -> p (a n)"))\
                        .then_inc(landed, 16)

            def page_numbers(b):
                return [sp.value_load(pages[0:1, bass.ds(b * NPG + g, 1)], min_val=0, max_val=NPHYS - 1)
                        for g in range(NPG)]

            load_heads(0, 2)
            sp.wait_ge(pages_landed, 16)
            page = page_numbers(0)
            sp.wait_ge(pv_done, 16 * G)
            sp.wait_ge(kv_stored, 32 * G)
            sp.wait_ge(new_stashed, G)
            load_pages(page, sK, ck_v, sk_landed)
            for e in order:
                sp.wait_ge(done_of[e], 3)
            load_pages(page, sV, cv_v, sv_landed)
            page = page_numbers(1)
            sp.wait_ge(sk_tr, 8)
            load_pages(page, sK, ck_v, sk_landed)
            with sp.Fori(1, NB - 1) as b:
                page = page_numbers(b + 1)
                sp.wait_ge(sk_tr, 8 * b + 8)
                past_waits(sp, "sp")
                load_pages(page, sK, ck_v, sk_landed)
                page = page_numbers(b)
                sp.wait_ge(spv_done, b)
                past_waits(sp, "sp")
                load_pages(page, sV, cv_v, sv_landed)
            page = page_numbers(NB - 1)
            sp.wait_ge(spv_done, NB - 1)
            load_pages(page, sV, cv_v, sv_landed)
            load_heads(2, 4 * HH)
            with sp.Fori(0, KD // 2) as it:
                for dd in range(2):
                    for j in range(2):
                        n, slot, _ = number(U_MG, 4, it, 2 * dd + j)
                        load(n, slot, w_in_v[:, :, bass.ds((2 * it + dd) * P + (O_MG + j * D), P)])
            with sp.Fori(0, KD // 2) as it:
                for j in range(2):
                    n, slot, _ = number(U_OUT, 2, it, j)
                    load(n, slot, w_out_v[:, :, bass.ds((2 * it + j) * P, P)])
            with sp.Fori(0, NMB) as it:
                for j in range(UT):
                    n, slot, _ = number(U_MLP, 2 * UT, it, j)
                    load(n, slot, w_up_v[:, :, bass.ds(it * MB + j * P, P)])
                for j in range(UT):
                    n, slot, _ = number(U_MLP, 2 * UT, it, UT + j)
                    load(n, slot, w_dn_v[:, bass.ds(it * UT, UT), 2 * P * j:2 * P * j + 2 * P], width=2 * P)

            for d in range(KD):
                sp.wait_ge(fin_copied, d + 1)
                sp.dma_start(yp_v[:, :, P * d:P * d + P], out_tok[d % 2][:, 0:NT, :]).then_inc(fin_stored[d % 2], 16)
                sp.dma_start(ys_v[:, P * d:P * d + P], out_tok[d % 2][0:TS, NT, :]).then_inc(fin_stored[d % 2], 16)
            for i in range(2):
                sp.wait_ge(fin_stored[i], 16 * KD)

        @block.gpsimd
        def _(pool):
            pool.memset(ident[:, :], 0.0)
            pool.memset(causal_neg[:, :], 0.0)
            pool.memset(ones[:, :], 1.0)
            pool.memset(chunk_mask[:, :], 1.0)
            pool.memset(chunk_mask_s[:, :], 1.0)
            pool.memset(batch_mask[:, :], 1.0)
            pool.memset(chunk_pick[:, :], 1.0)
            pool.memset(new_neg_room[:, :], NEG)
            pool.memset(not_after[:, :, :], 1.0)
            pool.memset(neg_pick[:, :, :], 0.0)
            pool.memset(neg_pick_s[:, :, :], 0.0)
            pool.memset(half[:, :], -0.5)
            pool.memset(d_parts[:, :], 0.0)
            pool.drain()
            pool.affine_select(out=ident[:, :], in_=ident[:, :], compare_op=ALU.not_equal, fill=1.0, base=0,
                               pattern=[[-1, P]], channel_multiplier=1)
            pool.affine_select(out=causal_neg[:, :], in_=causal_neg[:, :], compare_op=ALU.is_ge, fill=NEG, base=0,
                               pattern=[[-1, P]], channel_multiplier=1)

            def keep(ap, base, pattern, mul, fill):
                pool.affine_select(out=ap, in_=ap, compare_op=ALU.is_ge, fill=fill, base=base, pattern=pattern,
                                   channel_multiplier=mul)

            def chunks_only(ap, n, c):
                v = ap.rearrange("p (a b) -> p a b", b=c)
                keep(ap, 0, [[1, n]], -1, 0.0)
                pool.drain()
                keep(v, 0, [[-c, n // c], [0, c]], 1, 0.0)
                pool.drain()

            chunks_only(chunk_mask[:, :], P, HG_CHUNK)
            chunks_only(chunk_mask_s[:, :], TS, LS)
            keep(batch_mask[:, :], 0, [[-LS, NB]], 1, 0.0)
            pool.drain()
            keep(batch_mask[:, :], LS - 1, [[LS, NB]], -1, 0.0)
            keep(chunk_pick[:, :], 0, [[-HG_CHUNK, CP]], 1, 0.0)
            pool.drain()
            keep(chunk_pick[:, :], HG_CHUNK - 1, [[HG_CHUNK, CP]], -1, 0.0)
            for part in range(3):
                pool.affine_select(out=neg_pick[:, :, :], in_=neg_pick[:, :, :], compare_op=ALU.not_equal, fill=-1.0,
                                   base=-32 * part, pattern=[[-1, FH], [0, P]], channel_multiplier=1)
                pool.drain()
            pool.affine_select(out=neg_pick_s[:, :, :].rearrange("p b (h q) -> p (b h) q", q=LS),
                               in_=neg_pick_s[:, :, :].rearrange("p b (h q) -> p (b h) q", q=LS),
                               compare_op=ALU.not_equal, fill=-1.0, base=0, pattern=[[-1, NB * FH], [0, LS]],
                               channel_multiplier=1)
            keep(not_after[:, :, :], 0, [[0, FH], [1, LS]], -1, 0.0)
            pool.tensor_copy(ident_b[:, :], ident[:, :])
            pool.drain().then_inc(consts_ready, 1)

            pool.dma_start(pages[:, :], page_table.rearrange("(a b) g -> a (b g)", a=1)).then_inc(pages_landed, 16)
            pool.wait_ge(x_ms, 1)
            nc.gpsimd.tensor_tensor(stat[:, :], stat[:, :], half[:, :], ALU.pow).then_inc(x_rstd, 1)
            phase_end(pool, "pool", 1)
            phase_end(pool, "pool", 2)

            pool.memset(scan_ones, 1.0).then_inc(ones_set, 1)
            pool.wait_ge(pages_landed, 16)
            pool.wait_ge(lf_ready, 1)
            for b in range(NB):
                pool.dma_start(d_past[FH * b:FH * b + FH, PAST:PAST + LS], lf_T[:, L + LS * b:L + LS * b + LS])\
                    .then_inc(lf_new_moved, 16)
            with pool.Fori(0, G // 2) as it:
                for gg in range(2):
                    g = 2 * it + gg
                    pool.wait_ge(acc_read, 6 * it + (U_FOX + 3 * gg + 3))
                    pool.tensor_copy(q_new[:, bass.ds(g, 1), :].rearrange("p a b -> p (a b)"), fqT[:, L:T])
                    pool.tensor_copy(k_new[:, bass.ds(g, 1), :].rearrange("p a b -> p (a b)"), fkT[:, L:T])
                    pool.drain().then_inc(new_stashed, 1)
                    pool.wait_ge(tok_copied, 6 * g + 6)
                    pool.dma_start(kp_v[:, :, bass.ds(g * P, P)], f_ktok).then_inc(kv_stored, 16)
                    pool.dma_start(vp_v[:, :, bass.ds(g * P, P)], f_vtok).then_inc(kv_stored, 16)
                    for i in range(NB // G):
                        b = (NB // G) * g + i
                        for j in range(NPG):
                            page = pool.value_load(pages[0:1, bass.ds(b * NPG + j, 1)], min_val=0, max_val=NPHYS - 1)
                            pool.dma_start(past_lf[:, j, bass.ds(b, 1), :].rearrange("p a h -> p (a h)"),
                                           cl_v[bass.ds(page, 1), :, :].rearrange("a p h -> p (a h)"))\
                                .then_inc(past_logf_landed, 16)
            pool.dma_start(k_sample[0].rearrange("b l h d -> (b l) (h d)"), k_new_tok[:, :]).then_inc(stored, 16)
            pool.dma_start(v_sample[0].rearrange("b l h d -> (b l) (h d)"), v_new[:, :]).then_inc(stored, 16)
            pool.wait_ge(kv_stored, 32 * G)
            pool.wait_ge(lf_out_copied, 1)
            pool.dma_start(logf_prompt[0, 0].rearrange("(t p) h -> p t h", p=P),
                           lf_out[:, 0:NT * FH].rearrange("p (t h) -> p t h", h=FH)).then_inc(stored, 16)
            pool.dma_start(logf_sample[0].rearrange("b l h -> (b l) h"), lf_out[0:TS, NT * FH:NT * FH + FH])\
                .then_inc(stored, 16)
            pool.wait_ge(stored, 64)
            phase_end(pool, "pool", 3)

            pool.memset(sQ_room, 0.0).then_inc(sq_zeroed, 1)

            phase_end(pool, "pool", 4)

            pool.memset(q_by_b_room, 0.0)
            pool.memset(reset[:, :], 1.0)
            pool.drain()
            pool.memset(reset[:, 0:L:HG_CHUNK], 0.0)
            pool.memset(reset[:, L:T:LS], 0.0)
            pool.memset(h_ms, 1.0)
            pool.memset(a_mask[0], 0.0)
            pool.memset(a_mask[1], 0.0)
            pool.memset(a_mask_s, 0.0)
            pool.drain().then_inc(hg_zeroed, 1)
            pool.sem_inc(states_free, 1)
            with pool.Fori(0, HH) as h:
                pool.dma_start(s_states, state_hgrn[0, :, bass.ds(h, 1), :, :].rearrange("b a k v -> k b (a v)"))\
                    .then_inc(s0_landed, 16)
                pool.wait_ge(hv_copied, h + 1)
                for t in range(NT):
                    if t >= 2:
                        pool.wait_ge(ds_ready, NT * h + t - 1)
                    nc.gpsimd.tensor_tensor(v_by_chunk[:, t % 2, :, :],
                                            h_vtok[:, t, :].unsqueeze(1).broadcast_to([P, CP, P]),
                                            chunk_pick[:, :].unsqueeze(2).broadcast_to([P, CP, P]), ALU.mult)\
                        .then_inc(v_spread, 1)
                pool.wait_ge(hms_ready, h + 1)
                nc.gpsimd.tensor_tensor(h_ms, h_ms, half[:, :], ALU.pow).then_inc(hrstd, 1)
                pool.wait_ge(s_ready, NCH * h + NCH)
                past_waits(pool, "pool")
                pool.dma_start(s_prompt[0, 0, bass.ds(h, 1), :, :].rearrange("a k v -> k (a v)"), states[NCH % 8])\
                    .then_inc(state_stored, 16)
                pool.wait_ge(s_new_ready, h + 1)
                past_waits(pool, "pool")
                pool.dma_start(s_sample[0, :, bass.ds(h, 1), :, :].rearrange("b a k v -> k b (a v)"), s_states)\
                    .then_inc(state_stored, 16)
                pool.wait_ge(state_stored, 32 * h + 32)
                pool.sem_inc(states_free, 1)
            phase_end(pool, "pool", 5)

            def load_br(d, slot):
                v = br_raw[slot].rearrange("p (k n) -> p k n", n=P)
                pool.dma_start(v[:, 0:HH, :], w_bh_v[:, :, bass.ds(d * P, P)]).then_inc(br_landed[slot], 16)
                pool.dma_start(v[:, HH:HH + G, :], w_bf_v[:, :, bass.ds(d * P, P)]).then_inc(br_landed[slot], 16)

            load_br(0, 0)
            load_br(1, 1)
            for m in range(NM - NM1):
                if m:
                    pool.wait_ge(ada_used, NM1 // 4 + m)
                pool.dma_start(ada_raw.rearrange("p (k n) -> p k n", n=P),
                               ada_v[:, :, P * (NM1 + m):P * (NM1 + m) + P]).then_inc(ada_rest_landed, 16)
                if m % 4 == 3 and m // 4 < KD - 2:
                    pool.wait_ge(br_ready, 6 * (m // 4) + 6)
                    load_br(m // 4 + 2, m // 4 % 2)
            phase_end(pool, "pool", 6)

            pool.memset(ssq[1], 0.0)
            pool.drain()
            pool.sem_inc(sq_free, 2)
            for t in range(NT):
                pool.dma_start(xall[:, t, :], xp_v[:, t, :]).then_inc(x_again_landed, 16)
            pool.dma_start(xs_again, xs_v).then_inc(x_again_landed, 16)

            def rstd(k):
                pool.wait_ge(ms_ready, k)
                nc.gpsimd.tensor_tensor(stat[:, :], stat[:, :], half[:, :], ALU.pow).then_inc(rstd_ready, 1)

            def add_squares(k, squares, ready, count):
                pool.wait_ge(ready, count)
                nc.gpsimd.tensor_add(ssq[k], ssq[k], squares)
                pool.drain().then_inc(sq_free, 1)

            with pool.Fori(0, KD // 2 - 1) as it:
                for j in range(2):
                    add_squares(1, sq[j], acc_read, 2 * it + (U_OUT + j + 1))
            add_squares(1, sq[0], acc_read, U_OUT + KD - 1)
            rstd(1)
            pool.memset(ssq[2], 0.0)
            pool.drain()
            for d in range(KD - 1):
                add_squares(2, sq[d % 2], x1_sq, d + 1)
            rstd(2)
            phase_end(pool, "pool", 7)

            pool.memset(yT, 0.0)
            for i in range(2):
                pool.memset(down[i], 0.0).then_inc(down_free, 1)
            pool.drain()

            def add_down(it, j):
                pool.wait_ge(down_copied, KD * it + j + 1)
                nc.gpsimd.tensor_add(yT[:, j, :], yT[:, j, :], down[j % 2]).then_inc(down_free, 1)

            with pool.Fori(0, NMB - 1) as it:
                for j in range(KD):
                    add_down(it, j)
            pool.wait_ge(unit_done, U_MLP + 2 * UT * (NMB - 1) + UT)
            pool.dma_start(x1_all, x1_dram).then_inc(x1_back, 16)
            pool.drain()
            rstd(3)
            phase_end(pool, "pool", 8)

        @block.scalar
        def _(act):
            copy, ACTIVATE = nc.scalar.copy, nc.scalar.activation

            def hi(base, per, it, j):
                n, slot, landed = number(base, per, it, j)
                split_hi(act, n, slot, landed)

            for t in range(NT):
                act.dma_start(xall[:, t, :], xp_v[:, t, :]).then_inc(x_landed, 16)
            act.dma_start(xs_tile, xs_v).then_inc(xs_landed, 16)
            act.wait_ge(vecs_tr, 1)
            ACTIVATE(vec[:, :], bank(6, 0, NV), ACT.Copy).then_inc(vecs_copied, 1)
            ACTIVATE(c_act[:, :], bank(7, 0, NC * KD), ACT.Silu).then_inc(c_ready, 1)
            act.wait_ge(x_landed, 16 * NT)
            act.wait_ge(xs_landed, 16)
            act.wait_ge(dve_consts_ready, 1)
            for t in range(NT):
                ACTIVATE(junk, xall[:, t, :], ACT.Square, accum_out=stat[:, t:t + 1])
                act.drain()
            ACTIVATE(junk[0:TS, :], xs_tile, ACT.Square, accum_out=stat[0:TS, NT:NT + 1])
            act.drain().then_inc(x_sumsq, 1)
            for i in range(NM1 // 4):
                act.wait_ge(ada_used, i + 1)
                ACTIVATE(mod_rows[i % 2], bank(i, rows=NC), ACT.Copy).then_inc(mod_rows_copied, 1)
            act.wait_ge(mod_done, 1)
            ACTIVATE(lb[:, :], lb_diff[:, :], ACT.Sigmoid)
            ACTIVATE(omlb[:, :], lb_diff[:, :], ACT.Sigmoid, scale=-1.0)
            phase_end(act, "act", 1)

            split_hi(act, 0, 0, 16)
            split_hi(act, 1, 1, 16)
            for i in range(2 * KD):
                d, half_no = i // 2, i % 2
                act.wait_ge(h_tr, i + 1)
                if i >= 2:
                    act.wait_ge(h_split, i - 1)
                ACTIVATE(h_tmp[i % 2], bank(3 + i % 2), ACT.Identity, scale=pre1[:, d, 0:1], bias=mod[:, d, 0:1])
                act.drain()
                ACTIVATE(h_hi[:, d, 512 * half_no:512 * half_no + 512], h_tmp[i % 2], ACT.Copy).then_inc(h_raw, 1)
            phase_end(act, "act", 2)

            act.wait_ge(unit_done, 1)
            ACTIVATE(lf_T, acc(0)[0:FH, :], ACT.Identity, bias=fox_b[:, 0:1]).then_inc(acc_read, 1)
            act.drain()
            ACTIVATE(lf_a, lf_T, ACT.Abs)
            act.drain()
            ACTIVATE(lf_a, lf_a, ACT.Exp, scale=-1.0)
            act.drain()
            ACTIVATE(lf_a, lf_a, ACT.Ln, bias=1.0)
            act.drain().then_inc(lf_ln, 1)
            with act.Fori(0, G // 2) as it:
                for gg in range(2):
                    g = 2 * it + gg
                    for j, (dst, scale) in enumerate(((fkT, 1.0), (fqT, float(DH) ** -0.5), (fvT, 1.0))):
                        hi(U_FOX, 6, it, 3 * gg + j + 1)
                        n, slot, _ = number(U_FOX, 6, it, 3 * gg + j)
                        act.wait_ge(unit_done, n + 1)
                        ACTIVATE(dst, acc(slot), ACT.Copy, scale=scale)
                        for head in range(2):
                            own, other = (slice(64 * x, 64 * x + 64) for x in (head, 1 - head))
                            if j == 0:
                                ACTIVATE(k_parts[head][own, 0:L], acc(slot)[own, 0:L], ACT.Copy)
                            if j == 1:
                                for rows in (own, other):
                                    ACTIVATE(q_hi[head][rows, 0:L], acc(slot)[own, 0:L], ACT.Copy, scale=scale)
                        act.drain().then_inc(acc_read, 1)
                    for a in range(17):
                        if a < 16:
                            n = P * (a % NT + 1)
                            act.wait_ge(max_ready, 16 * g + a + 1)
                            if a >= 2:
                                act.wait_ge(probs_tr, 16 * g + a - 1)
                            ACTIVATE(probs[a % 2][:, 0:n], bank(3 * (a % 2), 0, n), ACT.Exp,
                                     bias=nmax[:, a % 2:a % 2 + 1], accum_out=sums[:, a:a + 1])
                            act.drain().then_inc(probs_ready, 1)
                        e = a - 1
                        if e >= 0 and e % NT >= 4:
                            act.wait_ge(probs_tr, 16 * g + e + 1)
                            if e >= 2:
                                act.wait_ge(pv_done, 16 * g + e - 1)
                            ACTIVATE(probsT[e % 2][:, 4:e % NT + 1, :].rearrange("p a b -> p (a b)"),
                                     bank(5, 0, P * (e % NT - 3)), ACT.Copy).then_inc(pt_high, 1)
                    for i in range(2):
                        act.wait_ge(o_tr, 2 * g + i + 1)
                        ACTIVATE(mix[:, bass.ds(g, 1), 512 * i:512 * i + 512].rearrange("p a b -> p (a b)"),
                                 bank(6 + i), ACT.Copy).then_inc(o_copied, 1)
                    act.wait_ge(new_stashed, g + 1)
            act.wait_ge(lf_out_tr, 1)
            ACTIVATE(lf_out[:, 0:NT * FH], bank(6, 0, NT * FH), ACT.Copy)
            ACTIVATE(lf_out[0:TS, NT * FH:NT * FH + FH], bank(6, NT * FH, NT * FH + FH, rows=TS), ACT.Copy)
            act.drain().then_inc(lf_out_copied, 1)
            phase_end(act, "act", 3)

            def odd_keys(b):
                for i in range(4):
                    act.wait_ge(sk_tr, 8 * b + (2 * i + 2))
                    ACTIVATE(sKT[:, i, 512:1024], bank(5), ACT.Copy).then_inc(sk_copied_act, 1)

            def sample(b, last=False):
                act.wait_ge(smax_ready, b + 1)
                ACTIVATE(sP, psum[0:TS, 0:PAST + TS], ACT.Exp, bias=nmax[0:TS, 0:1], accum_out=sums[0:TS, 0:1])
                act.drain().then_inc(sexp_ready, 1)
                if not last:
                    odd_keys(b + 1)

            odd_keys(0)
            with act.Fori(0, NB - 1) as b:
                sample(b)
            sample(NB - 1, last=True)
            phase_end(act, "act", 4)

            with act.Fori(0, HH) as h:
                hi(U_HG, 4, h, 1)
                act.wait_ge(unit_done, 4 * h + (U_HG + 1))
                a0 = acc(U_HG % 2)
                ACTIVATE(hK, a0, ACT.Sigmoid, scale=-1.0)
                ACTIVATE(hF, a0, ACT.Sigmoid)
                act.drain().then_inc(acc_read, 1)
                hi(U_HG, 4, h, 2)
                act.wait_ge(unit_done, 4 * h + (U_HG + 2))
                ACTIVATE(hQ, acc((U_HG + 1) % 2), ACT.Copy, scale=float(DK) ** -0.5).then_inc(acc_read, 1)
                act.wait_ge(f_ready, h + 1)
                ACTIVATE(hF, hF, ACT.Ln).then_inc(g_ready, 1)
                hi(U_HG, 4, h, 3)
                act.wait_ge(unit_done, 4 * h + (U_HG + 3))
                ACTIVATE(hV, acc(U_HG % 2), ACT.Copy).then_inc(acc_read, 1)
                act.wait_ge(b_ready, h + 1)
                ACTIVATE(hE, hB, ACT.Exp)
                ACTIVATE(hN, hB, ACT.Exp, scale=-1.0)
                act.drain().then_inc(eb_ready, 1)
                hi(U_HG, 4, h, 4)
                act.wait_ge(unit_done, 4 * h + (U_HG + 4))
                ACTIVATE(hS, acc((U_HG + 1) % 2), ACT.Silu).then_inc(acc_read, 1)
                for t in range(NT + 1):
                    r = P if t < NT else TS
                    act.wait_ge(ho_ready, (NT + 1) * h + t + 1)
                    ACTIVATE(h_otok[0:r, t, :], bank(4 + t % 2 if t < NT else 6, 0, P, rows=r), ACT.Copy).then_inc(ho_copied, 1)
                    act.drain()
                    ACTIVATE(hF[0:r, P * (t % 2):P * (t % 2) + P], h_otok[0:r, t, :],
                             ACT.Square, accum_out=h_ms[0:r, t:t + 1])
                act.drain().then_inc(hss_ready, 1)
            phase_end(act, "act", 5)

            with act.Fori(0, KD // 2) as it:
                for dd in range(2):
                    for j, dst in enumerate((gate_h, gate_f)):
                        hi(U_MG, 4, it, 2 * dd + j + 1)
                        n, slot, _ = number(U_MG, 4, it, 2 * dd + j)
                        act.wait_ge(unit_done, n + 1)
                        ACTIVATE(dst, acc(slot), ACT.Sigmoid).then_inc(acc_read, 1)
                    act.wait_ge(br_added, 2 * it + dd + 1)
            for d in range(KD):
                ACTIVATE(h_hi[:, d, :], merged[:, d, :], ACT.Copy).then_inc(h_raw, 1)
            phase_end(act, "act", 6)

            with act.Fori(0, KD // 2) as it:
                for j in range(2):
                    hi(U_OUT, 2, it, j + 1)
                    n, slot, _ = number(U_OUT, 2, it, j)
                    act.wait_ge(unit_done, n + 1)
                    act.wait_ge(sq_free, 2 * it + j + 1)
                    ACTIVATE(sq[j], acc(slot), ACT.Square)
                    ACTIVATE(yT[:, bass.ds(2 * it + j, 1), :].rearrange("p a b -> p (a b)"), acc(slot), ACT.Copy)
                    act.drain().then_inc(acc_read, 1)

            def norm_rows(k):
                act.wait_ge(rb_ready, k)
                ACTIVATE(rb, psum[:, 0:T], ACT.Copy).then_inc(rb_copied, 1)

            norm_rows(1)
            for d in range(KD):
                act.wait_ge(x1_ready, d + 1)
                act.dma_start(x1_dram[:, d, :], yT[:, d, :]).then_inc(x1_stored, 16)
                act.wait_ge(sq_free, KD + (d if d else 1))
                ACTIVATE(sq[d % 2], yT[:, d, :], ACT.Square).then_inc(x1_sq, 1)
            norm_rows(2)
            for d in range(KD):
                act.wait_ge(h2_scaled, d + 1)
                ACTIVATE(h_hi[:, d, 0:L], t1[d % 2][:, 0:L], ACT.Identity, bias=mod[:, 3 * KD + d, 0:1])
                act.drain().then_inc(h2_raw, 1)
            act.wait_ge(x1_stored, 16 * KD)
            phase_end(act, "act", 7)

            def squares(d):
                act.wait_ge(down_free, KD * (NMB - 1) + d + 3)
                if d >= 2:
                    act.wait_ge(sq_free, 2 * KD + d - 1)
                ACTIVATE(relu[d % 2], yT[:, d, :], ACT.Square).then_inc(fin_sq, 1)

            def mlp_block(it, last=False):
                for j in range(UT):
                    hi(U_MLP, 2 * UT, it, j + 1)
                    n, slot, _ = number(U_MLP, 2 * UT, it, j)
                    act.wait_ge(unit_done, n + 1)
                    ACTIVATE(relu[j % 2], acc((U_MLP + j) % 2), ACT.Relu).then_inc(acc_read, 1)
                    act.drain().then_inc(relu_ready, 1)
                    ACTIVATE(u_hi[:, j, :], relu[j % 2], ACT.Square).then_inc(u_hi_ready, 1)
                for j in range(UT):
                    if not (last and j == UT - 1):
                        hi(U_MLP, 2 * UT, it, UT + j + 1)
                    n, slot, _ = number(U_MLP, 2 * UT, it, UT + j)
                    for i in range(2):
                        act.wait_ge(*((down_half, UT * it + j + 1), (unit_done, n + 1))[i])
                        act.wait_ge(down_free, KD * it + (2 * j + i + 1))
                        ACTIVATE(down[i], acc((U_MLP + i) % 2), ACT.Copy).then_inc(acc_read, 1)
                        act.drain().then_inc(down_copied, 1)
                    if last and j >= 1:
                        squares(2 * j - 2)
                        squares(2 * j - 1)
                if last:
                    squares(KD - 2)
                    squares(KD - 1)

            with act.Fori(0, NMB - 1) as it:
                mlp_block(it)
            mlp_block(NMB - 1, last=True)
            norm_rows(3)
            phase_end(act, "act", 8)
            for d in range(KD):
                act.wait_ge(fin_tr, d + 1)
                if d >= 2:
                    act.wait_ge(fin_stored[d % 2], 32 * (d // 2))
                ACTIVATE(out_tok[d % 2][:, 0:NT, :].rearrange("p a b -> p (a b)"), psum[:, 2048 * (d % 2):2048 * (d % 2) + L],
                         ACT.Copy)
                ACTIVATE(out_tok[d % 2][0:TS, NT, :], psum[0:TS, 2048 * (d % 2) + L:2048 * (d % 2) + L + P], ACT.Copy)
                act.drain().then_inc(fin_copied, 1)

        @block.vector
        def _(dve):
            v = nc.vector

            def lo(base, per, it, j):
                n, slot, _ = number(base, per, it, j)
                split_lo(dve, n, slot)

            v.memset(stat[:, :], 1.0)
            dve.drain().then_inc(dve_consts_ready, 1)
            dve.wait_ge(consts_ready, 1)
            dve.wait_ge(vecs_copied, 1)
            v.tensor_sub(lb_diff[:, :], vec[:, V_L0:V_L0 + HH], vec[:, V_L1:V_L1 + HH])
            dve.wait_ge(vecs_tr, 2)
            v.tensor_scalar(new_neg_own, bank(4, 0, LS, rows=TS).unsqueeze(1).broadcast_to([TS, NB, LS]), -NEG, NEG,
                            ALU.mult, ALU.add)
            dve.wait_ge(x_sumsq, 1)
            v.tensor_scalar(stat[:, :], stat[:, :], 1.0 / D, EPS, ALU.mult, ALU.add).then_inc(x_ms, 1)
            dve.wait_ge(x_rstd, 1)
            for t in range(NT):
                v.tensor_scalar(xall[:, t, :], xall[:, t, :], stat[:, t:t + 1], None, ALU.mult)
            v.tensor_scalar(xs_tile, xs_tile, stat[0:TS, NT:NT + 1], None, ALU.mult)
            dve.wait_ge(mod_ready, 1)
            v.tensor_tensor(mod[:, 0:NM1, :], bank(5, 0, NM1 * NC).rearrange("p (m c) -> p m c", c=NC),
                            vec[:, V_AB:V_AB + NM1].unsqueeze(2).broadcast_to([P, NM1, NC]), ALU.add)
            dve.drain()

            def times_norm(dst, row, weight, plus_one):
                w = vec[:, weight:weight + KD].unsqueeze(2).broadcast_to([P, KD, NC])
                v.scalar_tensor_tensor(dst[:, :, :], mod[:, row * KD:row * KD + KD, :], 1.0 if plus_one else 0.0, w,
                                       ALU.add, ALU.mult)

            times_norm(pre1, 1, V_N1, True)
            dve.drain().then_inc(mod_done, 1)
            phase_end(dve, "dve", 1)

            split_lo(dve, 0, 0)
            split_lo(dve, 1, 1)
            hs_tmp = junk[:, 0:KD * TS].rearrange("p (d b l) -> p d b l", b=NB, l=LS)
            dve.wait_ge(hs_tr, 1)
            v.tensor_tensor(hs_tmp, bank(5).rearrange("p (d b l) -> p d b l", b=NB, l=LS),
                            pre1[:, :, 1:NC].unsqueeze(3).broadcast_to([P, KD, NB, LS]), ALU.mult)
            dve.drain()
            v.tensor_tensor(hs_tmp, hs_tmp, mod[:, 0:KD, 1:NC].unsqueeze(3).broadcast_to([P, KD, NB, LS]), ALU.add)
            dve.drain()
            flat = junk[:, 0:KD * TS].rearrange("p (d t) -> p d t", t=TS)
            v.tensor_copy(h_hi[:, :, L:T], flat)
            dve.drain()
            v.tensor_sub(h_lo[:, :, L:T], flat, h_hi[:, :, L:T].bitcast(F32))
            dve.drain()
            for i in range(2 * KD):
                d, c = i // 2, 512 * (i % 2)
                dve.wait_ge(h_raw, i + 1)
                v.tensor_sub(h_lo[:, d, c:c + 512], h_tmp[i % 2], h_hi[:, d, c:c + 512].bitcast(F32))\
                    .then_inc(h_split, 1)
            phase_end(dve, "dve", 2)

            dve.wait_ge(lf_ln, 1)
            dve.wait_ge(ones_set, 1)
            v.tensor_scalar(lf_m, lf_T, 0.0, None, ALU.min)
            dve.drain()
            v.tensor_sub(lf_T, lf_m, lf_a)
            dve.drain().then_inc(lf_ready, 1)
            v.tensor_tensor_scan(lf_d, scan_ones[0:FH, :], lf_T[:, 0:L], 0.0, ALU.mult, ALU.add)
            dve.drain()
            for part in range(3):
                v.tensor_copy(lf_b, lf_d)
                dve.drain()
                v.tensor_sub(lf_d, lf_d, lf_b)
                v.tensor_copy(d_parts[32 * part:32 * part + FH, :], lf_b)
                dve.drain()
            dve.drain().then_inc(d_ready, 1)

            with dve.Fori(0, G // 2) as it:
                for gg in range(2):
                    g = 2 * it + gg
                    for j in range(3):
                        lo(U_FOX, 6, it, 3 * gg + j + 1)
                        if j < 2:
                            dve.wait_ge(acc_read, 6 * it + (U_FOX + 3 * gg + j + 1))
                            for head in range(2):
                                own, other = (slice(64 * x, 64 * x + 64) for x in (head, 1 - head))
                                if j == 0:
                                    v.tensor_sub(k_parts[head][other, 0:L], fkT[own, 0:L],
                                                 k_parts[head][own, 0:L].bitcast(F32))
                                else:
                                    v.tensor_sub(q_lo[own, 0:L], fqT[own, 0:L], q_hi[head][own, 0:L].bitcast(F32))
                    dve.drain().then_inc(qk_split, 1)
                    for i, (src, dst) in enumerate((
                            (bank(6), f_ktok[:, 0:4, :].rearrange("p a b -> p (a b)")),
                            (bank(7), f_ktok[:, 4:8, :].rearrange("p a b -> p (a b)")),
                            (bank(2), f_vtok[:, 0:4, :].rearrange("p a b -> p (a b)")),
                            (bank(5), f_vtok[:, 4:8, :].rearrange("p a b -> p (a b)")),
                            (bank(6, 0, P, rows=TS), v_new[:, bass.ds(g * P, P)]),
                            (bank(7, 0, P, rows=TS), k_new_tok[:, bass.ds(g * P, P)]))):
                        dve.wait_ge(tok_tr, 6 * g + i + 1)
                        v.tensor_copy(dst, src).then_inc(tok_copied, 1)
                    for a in range(18):
                        if a < 16:
                            n = P * (a % NT + 1)
                            dve.wait_ge(scores_ready, 16 * g + a + 1)
                            v.tensor_reduce(nmax[:, a % 2:a % 2 + 1], bank(3 * (a % 2), 0, n), axis=AX, op=ALU.max,
                                            negate=True).then_inc(max_ready, 1)
                        e = a - 1
                        if 0 <= e < 16:
                            dve.wait_ge(probs_tr, 16 * g + e + 1)
                            if e >= 2:
                                dve.wait_ge(pv_done, 16 * g + e - 1)
                            m = min(e % NT + 1, 4)
                            v.tensor_copy(probsT[e % 2][:, 0:m, :].rearrange("p a b -> p (a b)"),
                                          bank(2, 0, P * m)).then_inc(pt_low, 1)
                        o = a - 2
                        if o >= 0:
                            dve.wait_ge(pv_done, 16 * g + o + 1)
                            v.reciprocal(rinv[:, o % 2:o % 2 + 1], sums[:, o:o + 1])
                            dve.drain()
                            c = DH * (o // NT)
                            v.tensor_scalar(f_otok[:, o % NT, c:c + DH], bank(6 + o % 2, 0, DH),
                                            rinv[:, o % 2:o % 2 + 1], None, ALU.mult).then_inc(o_ready, 1)
                    dve.wait_ge(kv_stored, 32 * g + 32)
            dve.wait_ge(lf_tr, 1)
            v.tensor_tensor_scan(d_past[:, 0:PAST], scan_ones, psum[0:TS, 1536:1536 + PAST], 0.0, ALU.mult,
                                 ALU.add)
            dve.drain()
            dve.wait_ge(lf_new_moved, 16 * NB)
            v.tensor_tensor_scan(d_past[:, PAST:PAST + LS], scan_ones[:, 0:LS], d_past[:, PAST:PAST + LS],
                                 d_past[:, PAST - 1:PAST], ALU.mult, ALU.add)
            phase_end(dve, "dve", 3)

            v.tensor_copy(d_two[0:TS, :], d_past)
            dve.drain()
            v.tensor_sub(d_two[TS:2 * TS, :], d_past, d_two[0:TS, :].bitcast(F32))
            dve.wait_ge(sq_zeroed, 1)

            def queries(b):
                for i in range(2):
                    v.tensor_copy(sQ_own[64 * i:64 * i + 64, :, LS * i:LS * i + LS],
                                  q_new[64 * i:64 * i + 64, :, bass.ds(b * LS, LS)])
                    v.tensor_copy(pick[64 * i:64 * i + 64, :],
                                  neg_pick_s[:, bass.ds(b, 1), :].rearrange("p a c -> p (a c)"))
                v.tensor_copy(sNeg, new_neg[:, bass.ds(b, 1), :].rearrange("p a k -> p (a k)"))
                dve.drain().then_inc(sq_ready, 1)

            def even_keys(b):
                for i in range(4):
                    dve.wait_ge(sk_tr, 8 * b + (2 * i + 1))
                    v.tensor_copy(sKT[:, i, 0:512], bank(4)).then_inc(sk_copied_dve, 1)

            def largest(b):
                dve.wait_ge(ss_ready, b + 1)
                v.tensor_reduce(nmax[0:TS, 0:1], psum[0:TS, 0:PAST + TS], axis=AX, op=ALU.max, negate=True)\
                    .then_inc(smax_ready, 1)

            def mixed(b):
                dve.wait_ge(so_tr, b + 1)
                for i in range(2):
                    v.tensor_copy(
                        mix[64 * i:64 * i + 64, 0:G, bass.ds(b * LS + L, LS)],
                        diagonal(bank(6, TS, TS + G * TS)[64 * i:64 * i + 64, :], LS * i))

            def diagonal(ap, at):
                s = ap[:, at:at + 1]
                return bass.AP(tensor=s.tensor, offset=s.offset, ap=[s.ap[0], [TS + 2 * LS, G], [1, LS]])

            def sample(b, first=False, last=False, before_last=False):
                if not last:
                    even_keys(b + 1)
                dve.wait_ge(sp_tr, b + 1)
                v.tensor_copy(sPT[:, 0:NPG, :].rearrange("p a b -> p (a b)"), bank(3))
                v.tensor_copy(sPT[0:TS, NPG, :], bank(6, 0, TS, rows=TS)).then_inc(spt_ready, 1)
                if not first:
                    mixed(b - 1)
                v.reciprocal(rinv[0:TS, 0:1], sums[0:TS, 0:1])
                if not last:
                    largest(b + 1)
                if not (last or before_last):
                    queries(b + 2)
                dve.drain()
                dve.wait_ge(spv_done, b + 1)
                v.tensor_scalar(sO, bank(7, rows=TS), rinv[0:TS, 0:1], None, ALU.mult).then_inc(so_copied, 1)

            queries(0)
            even_keys(0)
            largest(0)
            queries(1)
            sample(0, first=True)
            with dve.Fori(1, NB - 2) as b:
                sample(b)
            sample(NB - 2, before_last=True)
            sample(NB - 1, last=True)
            mixed(NB - 1)
            phase_end(dve, "dve", 4)

            def chunk_ends(ap, c):
                e = ap.rearrange("p (n c) -> p n c", c=c)[:, :, c - 1:c]
                return e.broadcast_to([P, ap.shape[1] // c, c])

            dve.wait_ge(hg_zeroed, 1)
            def head(h, last=False):
                dve.wait_ge(acc_read, 4 * h + (U_HG + 1))
                om, lbh = omlb[:, bass.ds(h, 1)], lb[:, bass.ds(h, 1)]
                v.tensor_tensor(hK, hK, om.broadcast_to([P, T]), ALU.mult)
                v.tensor_tensor(hF, hF, om.broadcast_to([P, T]), ALU.mult)
                dve.drain()
                v.tensor_tensor(hF, hF, lbh.broadcast_to([P, T]), ALU.add).then_inc(f_ready, 1)
                lo(U_HG, 4, h, 2)
                dve.wait_ge(g_ready, h + 1)
                v.tensor_tensor_scan(hB, reset[:, :], hF, 0.0, ALU.mult, ALU.add).then_inc(b_ready, 1)
                lo(U_HG, 4, h, 3)
                dve.wait_ge(eb_ready, h + 1)
                v.tensor_mul(hQ, hQ, hE)
                v.tensor_mul(hN, hK, hN)
                dve.drain().then_inc(hg_ops, 1)
                v.tensor_copy(q_by_b_own, by_batch(hQ[:, L:T]))
                v.tensor_tensor(hK[:, 0:L].rearrange("p (n c) -> p n c", c=HG_CHUNK),
                                hN[:, 0:L].rearrange("p (n c) -> p n c", c=HG_CHUNK),
                                chunk_ends(hE[:, 0:L], HG_CHUNK), ALU.mult)
                v.tensor_tensor(by_batch(hK[:, L:T]), by_batch(hN[:, L:T]), chunk_ends(hE[:, L:T], LS), ALU.mult)
                dve.wait_ge(states_free, h + 1)
                v.memset(states[0], 0.0)
                dve.drain().then_inc(hg_ops, 1)
                lo(U_HG, 4, h, 4)
                dve.wait_ge(hv_tr, h + 1)
                v.tensor_copy(h_vtok[:, 0:NT, :].rearrange("p a b -> p (a b)"), psum[:, 1536:1536 + L])
                v.tensor_copy(h_vtok[0:TS, NT, :], bank(5, 0, P, rows=TS))
                dve.drain().then_inc(hv_copied, 1)
                dve.wait_ge(hkd_tr, h + 1)
                v.tensor_copy(h_kdtok[:, 0:NT, :].rearrange("p a b -> p (a b)"), psum[:, 0:L])
                v.tensor_copy(h_kdtok[0:TS, NT, :], bank(2, 0, P, rows=TS))
                dve.drain().then_inc(hkd_copied, 1)
                v.tensor_tensor(kd_by_b, h_kdtok[0:TS, NT, :].unsqueeze(1).broadcast_to([TS, NB, DK]),
                                batch_mask[:, :].unsqueeze(2).broadcast_to([TS, NB, DK]), ALU.mult)
                dve.drain().then_inc(masked_ready, 1)
                for t in range(NT):
                    dve.wait_ge(a_ready, (NT + 1) * h + t + 1)
                    if t >= 2:
                        dve.wait_ge(ho_ready, (NT + 1) * h + t - 1)
                    past_waits(dve, "dve")
                    v.copy_predicated(a_mask[t % 2], chunk_mask[:, :].bitcast(I32), bank(2 + t % 2, 0, P))\
                        .then_inc(a_masked, 1)
                    dve.wait_ge(ds_ready, NT * h + t + 1)
                    for i in range(CP):
                        c = CP * t + i
                        if c + 1 >= 8 and (c + 1) % CP == 0:
                            dve.wait_ge(ho_ready, (NT + 1) * h + (c - 7) // CP + 1)
                        end = HG_CHUNK * (c + 1) - 1
                        v.scalar_tensor_tensor(states[(c + 1) % 8], states[c % 8], hE[:, end:end + 1],
                                               bank(t % 2, P * i, P * i + P), ALU.mult, ALU.add)\
                            .then_inc(s_ready, 1)
                        dve.wait_ge(s_ready, NCH * h + c + 1)
                dve.wait_ge(a_ready, (NT + 1) * h + NT + 1)
                past_waits(dve, "dve")
                v.copy_predicated(a_mask_s, chunk_mask_s[:, :].bitcast(I32), bank(2, 0, TS, rows=TS))\
                    .then_inc(a_masked, 1)
                dve.wait_ge(sds_ready, h + 1)
                dve.wait_ge(ho_ready, (NT + 1) * h + NT + 1)
                for b in range(NB):
                    end = L + LS * (b + 1) - 1
                    v.scalar_tensor_tensor(s_states[:, b, :], s_states[:, b, :], hE[:, end:end + 1],
                                           psum[:, P * b:P * b + P], ALU.mult, ALU.add)
                dve.drain().then_inc(s_new_ready, 1)
                dve.wait_ge(hss_ready, h + 1)
                v.tensor_scalar(h_ms, h_ms, 1.0 / DV, EPS, ALU.mult, ALU.add).then_inc(hms_ready, 1)
                dve.wait_ge(hrstd, h + 1)
                v.tensor_tensor(h_otok[:, 0:NT, :], h_otok[:, 0:NT, :],
                                h_ms[:, 0:NT].unsqueeze(2).broadcast_to([P, NT, DV]), ALU.mult)
                v.tensor_scalar(h_otok[0:TS, NT, :], h_otok[0:TS, NT, :], h_ms[0:TS, NT:NT + 1], None, ALU.mult)
                dve.drain().then_inc(hn_ready, 1)
                if not last:
                    lo(U_HG, 4, h, 5)
                mixed_head = mix[:, bass.ds(h + G, 1), :].rearrange("p a b -> p (a b)")
                for i, (a, b, src) in enumerate(((L, T, bank(2, 0, TS)), (0, L, psum[:, 3072:3072 + L]))):
                    dve.wait_ge(ho_tr, 2 * h + i + 1)
                    v.scalar_tensor_tensor(mixed_head[:, a:b], src, vec[:, V_ON:V_ON + 1], hS[:, a:b], ALU.mult,
                                           ALU.mult).then_inc(ho_mixed, 1)

            lo(U_HG, 4, 0, 1)
            with dve.Fori(0, HH - 1) as h:
                head(h)
            head(HH - 1, last=True)
            phase_end(dve, "dve", 5)

            with dve.Fori(0, KD // 2) as it:
                for dd in range(2):
                    d = 2 * it + dd
                    def ada_tile(m):
                        dve.wait_ge(ada_used, 8 * it + (NM1 // 4 + 4 * dd + m + 1))
                        at = 8 * it + (NM1 + 4 * dd + m)
                        v.tensor_tensor(mod[:, bass.ds(at, 1), :].rearrange("p a c -> p (a c)"),
                                        bank((6, 7, 7, 7)[m], 0, NC), vec[:, bass.ds(at, 1)].broadcast_to([P, NC]),
                                        ALU.add).then_inc(ada_rest_read, 1)

                    def branch(first):
                        for i in range(first, first + 3):
                            a, b = PIECES[i % 3]
                            dve.wait_ge(br_ready, 6 * d + i + 1)
                            v.tensor_mul(dst[:, a:b] if i < 3 else br_tmp[:, a:b], bank(BR_BANK[i], 0, b - a),
                                         (gate_h if i < 3 else gate_f)[:, a:b]).then_inc(br_read, 1)

                    lo(U_MG, 4, it, 2 * dd + 1)
                    ada_tile(0)
                    lo(U_MG, 4, it, 2 * dd + 2)
                    ada_tile(1)
                    dve.wait_ge(acc_read, 4 * it + (U_MG + 2 * dd + 2))
                    dst = merged[:, bass.ds(d, 1), :].rearrange("p a b -> p (a b)")
                    branch(0)
                    ada_tile(2)
                    branch(3)
                    ada_tile(3)
                    dve.drain()
                    v.tensor_add(dst, dst, br_tmp)
                    dve.drain().then_inc(br_added, 1)
            for d in range(KD):
                dve.wait_ge(h_raw, 2 * KD + d + 1)
                v.tensor_sub(h_lo[:, d, :], merged[:, d, :], h_hi[:, d, :].bitcast(F32)).then_inc(merged_split, 1)
            phase_end(dve, "dve", 6)

            times_norm(post1, 2, V_P1, False)
            times_norm(pre2, 4, V_N2, True)
            times_norm(post2, 5, V_P2, False)
            dve.drain()

            def mean_square(k):
                dve.wait_ge(ss_tr, k)
                for a, b, r in ((0, NT, P), (NT, NT + 1, TS)):
                    s = stat[0:r, a:b]
                    v.tensor_scalar(s, bank(6, a, b, rows=r), 1.0 / D, EPS, ALU.mult, ALU.add)
                    dve.drain()
                    v.scalar_tensor_tensor(s, bank(6, 16 + a, 16 + b, rows=r), 1.0 / D, s, ALU.mult, ALU.add)
                dve.drain().then_inc(ms_ready, 1)

            def scaled(dst, y, m, d):
                v.scalar_tensor_tensor(dst[:, 0:L], y[:, 0:L], m[:, d, 0:1], rb[:, 0:L], ALU.mult, ALU.mult)
                dve.drain()

            y_s = yT[:, :, L:T]
            h2_s = sq[0][:, 0:KD * TS].rearrange("p (d t) -> p d t", t=TS)

            def samples_with(dst, src, m, op):
                v.tensor_tensor(dst.rearrange("p d (b l) -> p d b l", l=LS), src.rearrange("p d (b l) -> p d b l", l=LS),
                                m[:, :, 1:NC].unsqueeze(3).broadcast_to([P, KD, NB, LS]), op)
                dve.drain()

            def samples_by_rms(dst):
                v.tensor_tensor(dst, dst, rb[:, L:T].unsqueeze(1).broadcast_to([P, KD, TS]), ALU.mult)
                dve.drain()

            with dve.Fori(0, KD // 2) as it:
                for j in range(2):
                    lo(U_OUT, 2, it, j + 1)
            mean_square(1)
            samples_with(y_s, y_s, post1, ALU.mult)
            dve.wait_ge(rb_copied, 1)
            samples_by_rms(y_s)
            dve.wait_ge(xT_ready, 1)
            v.tensor_tensor(y_s, y_s, bank(7).rearrange("p (d t) -> p d t", t=TS), ALU.add)
            for d in range(KD):
                scaled(t1[0], yT[:, d, :], post1, d)
                dve.wait_ge(xT_ready, d + 2)
                v.tensor_add(yT[:, d, 0:L], t1[0][:, 0:L], psum[:, 1536 * (d % 2):1536 * (d % 2) + L])
                dve.drain().then_inc(x1_ready, 1)
            mean_square(2)
            samples_with(h2_s, y_s, pre2, ALU.mult)
            dve.wait_ge(rb_copied, 2)
            samples_by_rms(h2_s)
            samples_with(h2_s, h2_s, mod[:, 3 * KD:4 * KD, :], ALU.add)
            v.tensor_copy(h_hi[:, :, L:T], h2_s)
            dve.drain()
            v.tensor_sub(h_lo[:, :, L:T], h2_s, h_hi[:, :, L:T].bitcast(F32))
            for d in range(KD + 1):
                if d < KD:
                    scaled(t1[d % 2], yT[:, d, :], pre2, d)
                    dve.drain().then_inc(h2_scaled, 1)
                if d >= 1:
                    e, t = d - 1, t1[(d - 1) % 2]
                    dve.wait_ge(h2_raw, d)
                    v.scalar_tensor_tensor(h_lo[:, e, 0:L], t[:, 0:L], mod[:, 3 * KD + e, 0:1],
                                           h_hi[:, e, 0:L].bitcast(F32), ALU.add, ALU.subtract)
                    dve.drain().then_inc(h2_split, 1)
            phase_end(dve, "dve", 7)

            def mlp_block(it, last=False):
                for j in range(UT):
                    lo(U_MLP, 2 * UT, it, j + 1)
                    dve.wait_ge(relu_ready, UT * it + j + 1)
                    v.tensor_mul(usq, relu[j % 2], relu[j % 2])
                    dve.drain()
                    dve.wait_ge(u_hi_ready, UT * it + j + 1)
                    v.tensor_sub(u_lo[:, j, :], usq, u_hi[:, j, :].bitcast(F32))
                    dve.drain().then_inc(u_lo_ready, 1)
                for j in range(UT):
                    if not (last and j == UT - 1):
                        lo(U_MLP, 2 * UT, it, UT + j + 1)
                    if last and j == 0:
                        v.memset(ssq[3], 0.0)
                        dve.wait_ge(down_free, 2 + KD * (NMB - 1))
                    if last:
                        for d in (2 * j, 2 * j + 1):
                            dve.wait_ge(down_copied, KD * (NMB - 1) + d + 1)
                            v.tensor_add(yT[:, d, :], yT[:, d, :], down[d % 2])
                            dve.drain().then_inc(down_free, 1)
                        if j >= 1:
                            add_squares(2 * j - 2)
                            add_squares(2 * j - 1)
                if last:
                    add_squares(KD - 2)

            def add_squares(d):
                dve.wait_ge(fin_sq, d + 1)
                v.tensor_add(ssq[3], ssq[3], relu[d % 2])
                dve.drain().then_inc(sq_free, 1)

            with dve.Fori(0, NMB - 1) as it:
                mlp_block(it)
            mlp_block(NMB - 1, last=True)
            mean_square(3)
            samples_with(y_s, y_s, post2, ALU.mult)
            phase_end(dve, "dve", 8)
            dve.wait_ge(rb_copied, 3)
            samples_by_rms(y_s)
            for d in range(KD):
                scaled(yT[:, d, :], yT[:, d, :], post2, d)
                if d == 0:
                    dve.wait_ge(x1_back, 16)
                v.tensor_add(yT[:, d, :], yT[:, d, :], x1_all[:, d, :])
                dve.drain().then_inc(fin_ready, 1)

        @block.tensor
        def _(pe):
            mm, tr = nc.tensor.matmul, nc.tensor.transpose

            pe.wait_ge(consts_ready, 1)
            pe.wait_ge(vecs_landed, 16 * 10)
            tr(bank(6, 0, NV), vec_rows[:, :], ident[0:NV, 0:NV])
            tr(bank(7, 0, NC * KD), c_rows[:, :], ident[0:NC * KD, 0:NC * KD]).then_inc(vecs_tr, 1)
            tr(bank(4, 0, LS, rows=TS), not_after[:, :, :].rearrange("p h q -> p (h q)"), ident[0:LS, 0:LS])\
                .then_inc(vecs_tr, 1)
            pe.wait_ge(c_ready, 1)
            c_cols = c_act[:, :].rearrange("p (c k) -> p k c", k=KD)

            def mod_columns(i):
                pe.wait_ge(mod_rows_copied, i + 1)
                for m in range(4):
                    tr(bank(5, (4 * i + m) * NC, (4 * i + m) * NC + NC), mod_rows[i % 2][:, P * m:P * m + P],
                       ident[0:NC, 0:NC])

            for i in range(NM1 // 4):
                pe.wait_ge(ada_landed[i % 3], 16 * (i // 3) + 16)
                w = ada_ring[i % 3].rearrange("p (k n) -> p k n", n=512)
                for k in range(KD):
                    last = mm(bank(i, rows=NC), c_cols[:, k, :], w[:, k, :], start=(k == 0), stop=(k == KD - 1))
                last.then_inc(ada_used, 1)
                if i >= 1:
                    mod_columns(i - 1)
            mod_columns(NM1 // 4 - 1)
            pe.drain().then_inc(mod_ready, 1)
            phase_end(pe, "pe", 1)

            for d in range(KD):
                last = tr(bank(5, TS * d, TS * d + TS), xs_tile[:, P * d:P * d + P], ident[0:TS, 0:TS])
            last.then_inc(hs_tr, 1)
            for d in range(KD + 1):
                for i in (2 * d, 2 * d + 1):
                    if i >= 2 * KD:
                        break
                    if i >= 2:
                        pe.wait_ge(h_raw, i - 1)
                    for t in range(4):
                        tile = 4 * (i % 2) + t
                        last = tr(bank(3 + i % 2, P * t, P * t + P), xall[:, tile, P * d:P * d + P], ident[:, :])
                    last.then_inc(h_tr, 1)
                if d == 1:
                    pe.wait_ge(w_lo_ready, U_FF + 1)
                    pe.wait_ge(w_hi_ready, U_FF + 1)
                if d >= 1:
                    pe.wait_ge(h_split, 2 * d)
                    last = channel_tile(U_FF % 2, U_FF % 2, d - 1)
            last.then_inc(unit_done, 1)
            phase_end(pe, "pe", 2)

            with pe.Fori(0, G // 2) as it:
                for gg in range(2):
                    g = 2 * it + gg
                    for j in range(3):
                        n, slot, _ = number(U_FOX, 6, it, 3 * gg + j)
                        project(pe, n, slot, acc_free=(j == 0))
                    def four(src, dst, first):
                        for t in range(4):
                            last = tr(bank(dst, P * t, P * t + P), src[:, P * (first + t):P * (first + t) + P],
                                      ident[:, :])
                        last.then_inc(tok_tr, 1)

                    pe.wait_ge(acc_read, 6 * it + (U_FOX + 3 * gg + 2))
                    four(fkT, 6, 0)
                    four(fkT, 7, 4)
                    pe.wait_ge(acc_read, 6 * it + (U_FOX + 3 * gg + 3))
                    four(fvT, 2, 0)
                    four(fvT, 5, 4)
                    for i, src in enumerate((fvT, fkT)):
                        pe.wait_ge(tok_copied, 6 * g + (i + 1))
                        past_waits(pe, "pe")
                        tr(bank(6 + i, 0, P, rows=TS), src[:, L:T], ident[:, :]).then_inc(tok_tr, 1)
                    pe.wait_ge(d_ready, 1)
                    pe.wait_ge(qk_split, g + 1)
                    for a in range(18):
                        if a < 16:
                            j, i = a // NT, a % NT
                            n = P * (i + 1)
                            rows = slice(64 * j, 64 * j + 64)
                            if a >= 2:
                                pe.wait_ge(probs_ready, 16 * g + a - 1)
                            base = 1536 * (a % 2)
                            for c in range(0, n, 512):
                                e = min(c + 512, n)
                                queries = slice(P * i, P * i + P)
                                out = psum[:, base + c:base + e]
                                if e - c >= 256:
                                    mm(out, q_hi[j][:, queries], k_parts[j][:, c:e], start=True, stop=False)
                                    mm(out, q_lo[rows, queries], k_parts[j][rows, c:e], start=False, stop=False)
                                else:
                                    mm(out, fqT[rows, queries], fkT[rows, c:e], start=True, stop=False)
                                if e == n:
                                    mm(psum[:, base + n - P:base + n], ident_b[:, :], causal_neg[:, :], start=False,
                                       stop=False)
                                last = mm(psum[:, base + c:base + e],
                                          neg_pick[0:96, bass.ds(2 * g + j, 1), :].rearrange("p a b -> p (a b)"),
                                          d_parts[:, c:e], start=False, stop=True)
                            last.then_inc(scores_ready, 1)
                        if a == 1:
                            pe.wait_ge(tok_copied, 6 * g + 6)
                        e = a - 1
                        if 0 <= e < 16:
                            pe.wait_ge(probs_ready, 16 * g + e + 1)
                            if e >= 1:
                                pe.wait_ge(pt_low, 16 * g + e)
                            if e >= 5 and (e - 1) // NT >= 0:
                                done = (e // NT) * 4 + max(0, e % NT - 4)
                                if done:
                                    pe.wait_ge(pt_high, 8 * g + done)
                            for kb in range(e % NT + 1):
                                last = tr(bank(2 if kb < 4 else 5, P * (kb % 4), P * (kb % 4) + P),
                                          probs[e % 2][:, P * kb:P * kb + P], ident[:, :])
                            last.then_inc(probs_tr, 1)
                        o = a - 2
                        if o >= 0:
                            pe.wait_ge(pt_low, 16 * g + o + 1)
                            if o % NT >= 4:
                                pe.wait_ge(pt_high, 8 * g + (o // NT) * 4 + o % NT - 3)
                            if o >= 2:
                                pe.wait_ge(o_ready, 16 * g + o - 1)
                            for kb in range(o % NT + 1):
                                last = mm(bank(6 + o % 2, 0, DH), probsT[o % 2][:, kb, :],
                                          f_vtok[:, kb, DH * (o // NT):DH * (o // NT) + DH], start=(kb == 0),
                                          stop=(kb == o % NT))
                            last.then_inc(pv_done, 1)
                    pe.wait_ge(o_ready, 16 * g + 16)
                    for i in range(2):
                        for t in range(4):
                            last = tr(bank(6 + i, P * t, P * t + P), f_otok[:, 4 * i + t, :], ident[:, :])
                        last.then_inc(o_tr, 1)
            pe.wait_ge(o_copied, 2 * G)
            pe.wait_ge(past_logf_landed, 16 * NB * NPG)
            for g in range(NPG):
                tr(psum[0:TS, 1536 + P * g:1536 + P * g + P],
                   past_lf[:, g, :, :].rearrange("p b h -> p (b h)"), ident[:, :])
            pe.drain().then_inc(lf_tr, 1)
            pe.wait_ge(lf_ready, 1)
            for t in range(NT + 1):
                r = P if t < NT else TS
                last = tr(bank(6, FH * t, FH * t + FH, rows=r), lf_T[:, P * t:P * t + r], ident[0:FH, 0:FH])
            last.then_inc(lf_out_tr, 1)
            phase_end(pe, "pe", 3)

            def keys(b):
                pe.wait_ge(sk_landed, 16 * NPG * b + 16 * NPG)
                for i in range(8):
                    if i >= 2:
                        pe.wait_ge(*((sk_copied_dve, 4 * b + i // 2), (sk_copied_act, 4 * b + i // 2))[i % 2])
                    for t in range(4):
                        last = tr(bank(4 + i % 2, P * t, P * t + P),
                                  sK[:, 4 * (i % 2) + t, P * (i // 2):P * (i // 2) + P], ident[:, :])
                    last.then_inc(sk_tr, 1)

            def scores(b):
                pe.wait_ge(sk_copied_dve, 4 * b + 4)
                pe.wait_ge(sk_copied_act, 4 * b + 4)
                pe.wait_ge(sq_ready, b + 1)
                new = psum[0:TS, PAST:PAST + TS]
                for c in range(2):
                    for g in range(G):
                        mm(bank(c, rows=TS), sQ[:, g, :], sKT[:, g, 512 * c:512 * c + 512], start=(g == 0), stop=False)
                    mm(bank(c, rows=TS), pick, d_two[:, 512 * c:512 * c + 512], start=False, stop=True)
                for g in range(G):
                    mm(new, sQ[:, g, :], k_new[:, g, :], start=(g == 0), stop=False)
                mm(new, ident_b[0:TS, 0:TS], sNeg, start=False, stop=False)
                mm(new, pick, d_two[:, PAST:PAST + LS].unsqueeze(1).broadcast_to([P, NB, LS]), start=False,
                   stop=True).then_inc(ss_ready, 1)

            def output_columns(b):
                pe.wait_ge(so_copied, b + 1)
                past_waits(pe, "pe")
                for g in range(G):
                    last = tr(bank(6, TS + TS * g, TS + TS * g + TS), sO[:, P * g:P * g + P], ident[0:TS, 0:TS])
                last.then_inc(so_tr, 1)

            def sample(b, first=False, last_one=False):
                if not last_one:
                    keys(b + 1)
                pe.wait_ge(sexp_ready, b + 1)
                past_waits(pe, "pe")
                for t in range(NPG):
                    tr(bank(3, TS * t, TS * t + TS), sP[:, P * t:P * t + P], ident[0:TS, 0:TS])
                tr(bank(6, 0, TS, rows=TS), sP[:, PAST:PAST + TS], ident[0:TS, 0:TS])
                if not first:
                    output_columns(b - 1)
                pe.drain().then_inc(sp_tr, 1)
                if not last_one:
                    scores(b + 1)
                pe.wait_ge(spt_ready, b + 1)
                pe.wait_ge(sv_landed, 16 * NPG * b + 16 * NPG)
                for t in range(NPG):
                    mm(bank(7, rows=TS), sPT[:, t, :], sV[:, t, :], start=(t == 0), stop=False)
                mm(bank(7, rows=TS), sPT[0:TS, NPG, :], v_new[:, :], start=False, stop=True).then_inc(spv_done, 1)

            keys(0)
            scores(0)
            sample(0, first=True)
            with pe.Fori(1, NB - 1) as b:
                sample(b)
            sample(NB - 1, last_one=True)
            output_columns(NB - 1)
            phase_end(pe, "pe", 4)

            pe.wait_ge(hg_zeroed, 1)
            def head(h, last_one=False):
                for j in range(1, 4):
                    n, slot, _ = number(U_HG, 4, h, j)
                    project(pe, n, slot)
                pe.wait_ge(acc_read, 4 * h + (U_HG + 3))
                for t in range(NT):
                    tr(psum[:, 1536 + P * t:1536 + P * t + P], hV[:, P * t:P * t + P], ident[:, :])
                tr(bank(5, 0, P, rows=TS), hV[:, L:T], ident[:, :]).then_inc(hv_tr, 1)
                pe.wait_ge(acc_read, 4 * h + (U_HG + 4))
                pe.wait_ge(hg_ops, 2 * h + 2)
                for t in range(NT):
                    tr(psum[:, P * t:P * t + P], hK[:, P * t:P * t + P], ident[:, :])
                tr(bank(2, 0, P, rows=TS), hK[:, L:T], ident[:, :]).then_inc(hkd_tr, 1)
                pe.wait_ge(hv_copied, h + 1)
                pe.wait_ge(hkd_copied, h + 1)
                for t in range(NT + 1):
                    if t < NT:
                        cols = slice(P * t, P * t + P)
                        if t >= 2:
                            pe.wait_ge(a_masked, (NT + 1) * h + t - 1)
                        mm(bank(2 + t % 2, 0, P), hN[:, cols], hQ[:, cols], start=True, stop=True).then_inc(a_ready, 1)
                        if t >= 2:
                            pe.wait_ge(s_ready, NCH * h + CP * (t - 1))
                        pe.wait_ge(v_spread, NT * h + t + 1)
                        mm(bank(t % 2), h_kdtok[:, t, :], v_by_chunk[:, t % 2, :, :].rearrange("p c v -> p (c v)"),
                           start=True, stop=True).then_inc(ds_ready, 1)
                    e = t - 1
                    if e >= 0:
                        pe.wait_ge(a_masked, (NT + 1) * h + e + 1)
                        if e >= 1:
                            pe.wait_ge(s_ready, NCH * h + CP * e + CP - 1)
                        else:
                            pe.wait_ge(s_ready, NCH * h + CP - 1)
                        if e >= 2:
                            pe.wait_ge(ho_copied, (NT + 1) * h + e - 1)
                        mm(bank(4 + e % 2, 0, P), a_mask[e % 2], h_vtok[:, e, :], start=True, stop=False)
                        for i in range(CP):
                            last = mm(bank(4 + e % 2, 0, P)[32 * i:32 * i + 32, :],
                                      hQ[:, P * e + 32 * i:P * e + 32 * i + 32], states[(CP * e + i) % 8], start=False,
                                      stop=True)
                        last.then_inc(ho_ready, 1)
                mm(bank(2, 0, TS, rows=TS), hN[:, L:T], hQ[:, L:T], start=True, stop=True).then_inc(a_ready, 1)
                pe.wait_ge(masked_ready, h + 1)
                pe.wait_ge(s_ready, NCH * h + NCH)
                for b in range(NB):
                    last = mm(psum[:, P * b:P * b + P], kd_by_b[:, b, :], h_vtok[0:TS, NT, :], start=True, stop=True)
                last.then_inc(sds_ready, 1)
                pe.wait_ge(a_masked, (NT + 1) * h + NT + 1)
                pe.wait_ge(s0_landed, 16 * h + 16)
                past_waits(pe, "pe")
                mm(bank(6, 0, P, rows=TS), a_mask_s, h_vtok[0:TS, NT, :], start=True, stop=False)
                for b in range(NB):
                    last = mm(bank(6, 0, P, rows=TS), q_by_b[:, b, :], s_states[:, b, :], start=False,
                              stop=(b == NB - 1))
                last.then_inc(ho_ready, 1)
                if not last_one:
                    pe.wait_ge(ho_copied, (NT + 1) * h + NT)
                    n, slot, _ = number(U_HG, 4, h, 4)
                    project(pe, n, slot)
                pe.wait_ge(hn_ready, h + 1)
                past_waits(pe, "pe")
                tr(bank(2, 0, TS), h_otok[0:TS, NT, :], ident[0:TS, 0:TS]).then_inc(ho_tr, 1)
                for t in range(NT):
                    last = tr(psum[:, 3072 + P * t:3072 + P * t + P], h_otok[:, t, :], ident[:, :])
                last.then_inc(ho_tr, 1)
                pe.wait_ge(ho_mixed, 2 * h + 1)

            project(pe, U_HG, U_HG % 2)
            with pe.Fori(0, HH - 1) as h:
                head(h)
            head(HH - 1, last_one=True)
            phase_end(pe, "pe", 5)

            with pe.Fori(0, KD // 2) as it:
                for dd in range(2):
                    d = 2 * it + dd
                    def ada_tile(m, gate_after):
                        pe.wait_ge(ada_rest_landed, 64 * d + (16 * m + 16))
                        pe.wait_ge(*gate_after)
                        w = ada_raw.rearrange("p (k n) -> p k n", n=P)
                        for k in range(KD):
                            last = mm(bank((6, 7, 7, 7)[m], 0, NC), w[:, k, :], c_cols[:, k, :], start=(k == 0),
                                      stop=(k == KD - 1))
                        last.then_inc(ada_used, 1)

                    def branch(first):
                        for i in range(first, first + 3):
                            a, b = PIECES[i % 3]
                            if i in (0, 1):
                                pe.wait_ge(ada_rest_read, 4 * d + i + 1)
                            elif i == 4:
                                pe.wait_ge(ada_rest_read, 4 * d + 3)
                            else:
                                pe.wait_ge(br_read, 6 * d + {2: 1, 3: 3, 5: 4}[i])
                            for k in range(4):
                                kw = k if i < 3 else HH + k
                                km = G + k if i < 3 else k
                                last = mm(bank(BR_BANK[i], 0, b - a), w_br[:, kw, :], mix[:, km, a:b], start=(k == 0),
                                          stop=(k == 3))
                            last.then_inc(br_ready, 1)

                    w_br = br_raw[dd].rearrange("p (k n) -> p k n", n=P)
                    n, slot, _ = number(U_MG, 4, it, 2 * dd)
                    project(pe, n, slot)
                    ada_tile(0, (consts_ready, 1))
                    n, slot, _ = number(U_MG, 4, it, 2 * dd + 1)
                    project(pe, n, slot)
                    ada_tile(1, (consts_ready, 1))
                    pe.wait_ge(br_landed[dd], 32 * it + 32)
                    branch(0)
                    ada_tile(2, (br_read, 6 * d + 2))
                    branch(3)
                    ada_tile(3, (br_read, 6 * d + 5))
                    pe.wait_ge(ada_rest_read, 4 * d + 4)
                    pe.wait_ge(br_read, 6 * d + 6)
            phase_end(pe, "pe", 6, wait=False)

            def norm_rows(k, last_squares):
                for i, (squares, ready, count) in enumerate((
                        (ssq[k], sq_free, 1 + KD * k - (k - 1)),
                        ((relu if k == 3 else sq)[(KD - 1) % 2],) + last_squares)):
                    pe.wait_ge(ready, count)
                    for t in range(NT + 1):
                        r = P if t < NT else TS
                        last = mm(bank(6, 16 * i + t, 16 * i + t + 1, rows=r), squares[:, P * t:P * t + r],
                                  ones[:, 0:1], start=True, stop=True)
                last.then_inc(ss_tr, 1)
                pe.wait_ge(rstd_ready, k)
                for t in range(NT + 1):
                    r = P if t < NT else TS
                    last = mm(psum[:, P * t:P * t + r], stat[0:r, t:t + 1].broadcast_to([r, P]), ident[0:r, 0:r],
                              start=True, stop=True)
                last.then_inc(rb_ready, 1)

            n, slot, _ = number(U_OUT, 0, 0, 0)
            project(pe, n, slot, parts_ready=(merged_split, 0))
            with pe.Fori(0, KD // 2 - 1) as it:
                for j in range(2):
                    n, slot, _ = number(U_OUT, 2, it, j + 1)
                    project(pe, n, slot)
            n, slot, _ = number(U_OUT, 0, 0, KD - 1)
            project(pe, n, slot)
            for e in ("act", "dve", "pool"):
                pe.wait_ge(done_of[e], 6)
            pe.wait_ge(x_again_landed, 16 * (NT + 1))
            for d in range(KD):
                last = tr(bank(7, TS * d, TS * d + TS), xs_again[:, P * d:P * d + P], ident[0:TS, 0:TS])
            last.then_inc(xT_ready, 1)
            norm_rows(1, (acc_read, U_OUT + KD))
            pe.wait_ge(rb_copied, 1)
            for d in range(KD):
                if d >= 2:
                    pe.wait_ge(x1_ready, d - 1)
                base = 1536 * (d % 2)
                for t in range(NT):
                    last = tr(psum[:, base + P * t:base + P * t + P], xall[:, t, P * d:P * d + P], ident[:, :])
                last.then_inc(xT_ready, 1)
            pe.wait_ge(x1_ready, KD)
            norm_rows(2, (x1_sq, KD))
            pe.wait_ge(rb_copied, 2)
            phase_end(pe, "pe", 7, wait=False)

            def mlp_block(it, last=False):
                for j in range(UT):
                    n, slot, _ = number(U_MLP, 2 * UT, it, j)
                    project(pe, n, slot, acc_no=3 * UT * it + (U_MLP + j), acc_slot=(U_MLP + j) % 2,
                            parts_ready=(h2_split, 0) if j == 0 else None)
                for j in range(UT):
                    n, slot, _ = number(U_MLP, 2 * UT, it, UT + j)
                    pe.wait_ge(w_hi_ready, n + 1)
                    pe.wait_ge(w_lo_ready, n + 1)
                    for i in range(2):
                        pe.wait_ge(acc_read, 3 * UT * it + (U_MLP + UT + 2 * j + i - 1))
                        out = acc((U_MLP + i) % 2)
                        for k in range(UT):
                            if j == 0 and i == 0:
                                pe.wait_ge(u_hi_ready, UT * it + k + 1)
                                pe.wait_ge(u_lo_ready, UT * it + k + 1)
                            at = 2 * P * k + P * i
                            wh, wl = (w[:, slot, at:at + P] for w in (w_hi, w_lo))
                            for w, m in ((wh, u_hi), (wh, u_lo), (wl, u_hi)):
                                for a, b in PIECES:
                                    product = mm(out[:, a:b], w, m[:, k, a:b],
                                                 start=(k == 0 and w is wh and m is u_hi),
                                                 stop=(k == UT - 1 and w is wl))
                        product.then_inc((down_half, unit_done)[i], 1)

            with pe.Fori(0, NMB - 1) as it:
                mlp_block(it)
            mlp_block(NMB - 1, last=True)
            norm_rows(3, (fin_sq, KD))
            phase_end(pe, "pe", 8)
            pe.wait_ge(rb_copied, 3)
            for d in range(KD):
                pe.wait_ge(fin_ready, d + 1)
                if d >= 2:
                    pe.wait_ge(fin_copied, d - 1)
                base = 2048 * (d % 2)
                for t in range(NT):
                    tr(psum[:, base + P * t:base + P * t + P], yT[:, d, P * t:P * t + P], ident[:, :])
                tr(psum[0:TS, base + L:base + L + P], yT[:, d, L:T], ident[:, :]).then_inc(fin_tr, 1)


_INS = ['x_prompt', 'x_sample', 'c_prompt', 'c_sample', 'cache_k', 'cache_v', 'cache_logf', 'state_hgrn', 'page_table',
        'ada_w', 'ada_b', 'norm_mix_pre', 'norm_mix_post', 'norm_mlp_pre', 'norm_mlp_post', 'w_in',
        'hgrn_lower_bounds', 'hgrn_onorm', 'fox_b_f', 'w_br_h', 'w_br_f', 'w_out', 'w_mlp_up', 'w_mlp_down']


def kernel(**inputs):
    import numpy as _np
    import concourse.bacc as _bacc
    from concourse import mybir as _mybir
    from concourse.bass_utils import run_bass_kernel_spmd as _run

    xp, xs, ck, st = (inputs[n].shape for n in ('x_prompt', 'x_sample', 'cache_k', 'state_hgrn'))
    heads = (ck[3], ck[4])
    outs = [xp, xs, (1, 1, xp[1]) + heads, (1, 1, xp[1]) + heads, (1, 1, xp[1], ck[3]), (1, 1) + tuple(st[2:]),
            (1, xs[0], xs[1]) + heads, (1, xs[0], xs[1]) + heads, (1, xs[0], xs[1], ck[3]), tuple(st)]
    nc = _bacc.Bacc("TRN2", target_bir_lowering=False, num_devices=1)
    arrays, args = {}, []
    for name in _INS:
        a = _np.ascontiguousarray(inputs[name])
        arrays[f"in_{name}"] = a
        args.append(nc.dram_tensor(f"in_{name}", a.shape, _mybir.dt.from_np(a.dtype), kind="ExternalInput").ap())
    for i, shape in enumerate(outs):
        args.append(nc.dram_tensor(f"out_{i}", tuple(shape), F32, kind="ExternalOutput").ap())
    build_layer(nc, *args)
    r = _run(nc, [arrays], core_ids=[0])
    return tuple(r.results[0][f"out_{i}"] for i in range(len(outs)))
```
